# Optimizing a Trainium2 kernel written in Bass

```python
import math
import jax, jax.numpy as jnp
from jax import lax
import numpy as np

D_MODEL = 1024
BATCH = 1
SEQ = 128
DEPTH = 2
DEC_BATCH = 1
DEC_SEQ = 256
PAST_LEN = 128

GRID_W = 64
N_EVEN = (DEPTH + 1) // 2
N_ODD = DEPTH // 2
EPS = 1e-6
GN_EPS = 64e-5
ROPE_BASE = 10000.0
Q_BLOCK = 128
H_A = 4
DK_A = 64
DV_A = 128
ALPHA_RANK = 16
GATE_NORM = 16.0
CHUNK = 64
H_B = 8
N_B = 64
W_LORA = 64
A_LORA = 64
G_LORA = 128
H_C = 8
Q_RANK = 256
KV_RANK = 128
NOPE_C = 64
ROPE_C = 32
DV_C = 64
H_D = 4
DH_D = 64
DV_D = 128
N_EXPERTS = 16
N_GROUPS = 4
EXPERTS_PER_GROUP = N_EXPERTS // N_GROUPS
TOP_K = 2
D_FF_EXPERT = 512

MIX_WIDTH = H_A * DV_A + H_B * N_B
EVEN_SPLITS = (H_A * DK_A, H_A * DK_A, H_A * DV_A, H_A * DV_A, 2 * ALPHA_RANK,
               H_B * N_B, H_B * N_B, H_B * N_B, 2 * W_LORA, 2 * A_LORA, G_LORA)
ODD_SPLITS = (Q_RANK, KV_RANK, ROPE_C, H_D * 2 * DH_D, H_D * 2 * DH_D, H_D * DV_D)
EVEN_COLS = sum(EVEN_SPLITS)
ODD_COLS = sum(ODD_SPLITS)

kernel_name = 'hybrid_diffusion_prefix_trunk_step'

def rms_norm(x, g):
    xf = x.astype(jnp.float32)
    y = xf * lax.rsqrt(jnp.mean(xf * xf, axis=-1, keepdims=True) + EPS)
    return (y * g.astype(jnp.float32)).astype(x.dtype)

def split_cols(h, sizes):
    idx = [int(i) for i in np.cumsum(sizes)[:-1]]
    return jnp.split(h, idx, axis=-1)

def to_heads(x, n_heads):
    b, l, _ = x.shape
    return x.reshape(b, l, n_heads, -1).transpose(0, 2, 1, 3)

def from_heads(x):
    b, h, l, d = x.shape
    return x.transpose(0, 2, 1, 3).reshape(b, l, h * d)

def flip_seq(x):
    return jnp.flip(x, axis=2)

def head_group_norm(y, g, b):
    mu = jnp.mean(y, axis=-1, keepdims=True)
    var = jnp.mean(jnp.square(y - mu), axis=-1, keepdims=True)
    return from_heads((y - mu) * lax.rsqrt(var + GN_EPS)) * g + b

def axial_rope_tables(n_tokens, dim):
    n_rows = n_tokens // GRID_W
    rows = jnp.repeat(jnp.arange(n_rows), GRID_W).astype(jnp.float32)
    cols = jnp.tile(jnp.arange(GRID_W), n_rows).astype(jnp.float32)
    half = dim // 2
    inv = 1.0 / (ROPE_BASE ** (jnp.arange(0, half, 2, dtype=jnp.float32) / half))
    ang_r = rows[:, None] * inv
    ang_c = cols[:, None] * inv
    ang = jnp.concatenate([ang_r, ang_r, ang_c, ang_c], axis=-1)
    return jnp.cos(ang), jnp.sin(ang)

def apply_axial_rope(x, cos, sin):
    half = x.shape[-1] // 2
    qt = half // 2

    def rot_half(t):
        return jnp.concatenate([-t[..., qt:], t[..., :qt]], axis=-1)

    rot = jnp.concatenate([rot_half(x[..., :half]), rot_half(x[..., half:])], axis=-1)
    return x * cos + rot * sin

def rope_tail(x, cos, sin):
    return jnp.concatenate([x[..., :-ROPE_C], apply_axial_rope(x[..., -ROPE_C:], cos, sin)], axis=-1)

def gla_scan(q, k, v, log_a, s0):
    b, h, l, dk = q.shape
    dv = v.shape[-1]
    n = l // CHUNK
    q, k, v, log_a = [t.astype(jnp.float32).reshape(b, h, n, CHUNK, -1) for t in (q, k, v, log_a)]
    cum = jnp.cumsum(log_a, axis=3)
    cum_last = cum[:, :, :, -1:, :]
    q_t = q * jnp.exp(cum)
    k_t = k * jnp.exp(-cum)
    k_end = k * jnp.exp(cum_last - cum)
    mask = jnp.tril(jnp.ones((CHUNK, CHUNK), dtype=jnp.bool_))
    att = jnp.where(mask, jnp.einsum('bhncd,bhnsd->bhncs', q_t, k_t), 0.0)
    o_intra = jnp.einsum('bhncs,bhnsv->bhncv', att, v)
    u = jnp.einsum('bhnsd,bhnsv->bhndv', k_end, v)
    decay = jnp.exp(cum_last[:, :, :, 0, :])

    def step(s, inp):
        dec, uj = inp
        return dec[..., None] * s + uj, s

    s_fin, s_starts = lax.scan(step, s0.astype(jnp.float32),
                               (jnp.moveaxis(decay, 2, 0), jnp.moveaxis(u, 2, 0)))
    s_starts = jnp.moveaxis(s_starts, 0, 2)
    o_inter = jnp.einsum('bhncd,bhndv->bhncv', q_t, s_starts)
    return (o_intra + o_inter).reshape(b, h, l, dv), s_fin

def rwkv7_scan(r, w, k, v, kk, a, s0):
    def step(s, inp):
        r_t, w_t, k_t, v_t, kk_t, a_t = inp
        sa = jnp.einsum('bhvk,bhk->bhv', s, -kk_t)
        s = s * w_t[:, :, None, :] + sa[..., None] * (kk_t * a_t)[:, :, None, :] + v_t[..., None] * k_t[:, :, None, :]
        return s, jnp.einsum('bhvk,bhk->bhv', s, r_t)

    xs = tuple(jnp.moveaxis(t.astype(jnp.float32), 2, 0) for t in (r, w, k, v, kk, a))
    s_fin, ys = lax.scan(step, s0.astype(jnp.float32), xs)
    return jnp.moveaxis(ys, 0, 2), s_fin

def blocked_attention(q, k, v, scale):
    b, h, g, lq, d = q.shape
    nb = lq // Q_BLOCK
    qb = jnp.moveaxis(q.reshape(b, h, g, nb, Q_BLOCK, d), 3, 0)
    kf = k.astype(jnp.float32)
    vf = v.astype(jnp.float32)

    def one(qblk):
        s = jnp.einsum('bhgqd,bhgkd->bhgqk', qblk.astype(jnp.float32), kf) * scale
        p = jax.nn.softmax(s, axis=-1)
        return jnp.einsum('bhgqk,bhkv->bhgqv', p, vf)

    o = lax.map(one, qb)
    return jnp.moveaxis(o, 0, 3).reshape(b, h, g, lq, -1)

def even_mixer(h, s0_gla, s0_rwkv, w_in, gla_a_up, gla_a_b, gla_o_g, rw_w0, rw_w2, rw_a0, rw_a2, rw_g2,
               rw_kk, rw_ka, rw_rk, rw_gn_g, rw_gn_b, w_out):
    b, l, _ = h.shape
    q, k, v, g, a_lr, r_b, k_b, v_b, w_lr, aa_lr, g_lr = [t.astype(jnp.float32) for t in split_cols(h @ w_in, EVEN_SPLITS)]
    q = to_heads(q, H_A) * DK_A ** -0.5
    k = to_heads(k, H_A)
    v = to_heads(v, H_A)
    log_a = jax.nn.log_sigmoid(jnp.einsum('blpr,prd->pbld', a_lr.reshape(b, l, 2, ALPHA_RANK), gla_a_up)
                               + gla_a_b[:, None, None, :]) / GATE_NORM
    o_f, sg_f = gla_scan(q, k, v, to_heads(log_a[0], H_A), s0_gla[:, 0])
    o_b, sg_b = gla_scan(flip_seq(q), flip_seq(k), flip_seq(v), flip_seq(to_heads(log_a[1], H_A)), s0_gla[:, 1])
    o_gla = from_heads(rms_norm(o_f + flip_seq(o_b), gla_o_g)) * jax.nn.silu(g)
    r_h = to_heads(r_b, H_B)
    v_h = to_heads(v_b, H_B)
    kk = to_heads(k_b * rw_kk, H_B)
    kk = kk * lax.rsqrt(jnp.sum(kk * kk, axis=-1, keepdims=True) + EPS)
    z_w = rw_w0[:, None, None, :] + jnp.einsum('blpr,prd->pbld', jnp.tanh(w_lr.reshape(b, l, 2, W_LORA)), rw_w2)
    decay = jnp.exp(-jnp.exp(-jax.nn.softplus(-z_w) - 0.5))
    icl = jax.nn.sigmoid(rw_a0[:, None, None, :] + jnp.einsum('blpr,prd->pbld', aa_lr.reshape(b, l, 2, A_LORA), rw_a2))
    k_mod = k_b[None] * (1.0 + (icl - 1.0) * rw_ka)
    y_f, sr_f = rwkv7_scan(r_h, to_heads(decay[0], H_B), to_heads(k_mod[0], H_B), v_h, kk,
                           to_heads(icl[0], H_B), s0_rwkv[:, 0])
    y_b, sr_b = rwkv7_scan(flip_seq(r_h), flip_seq(to_heads(decay[1], H_B)), flip_seq(to_heads(k_mod[1], H_B)),
                           flip_seq(v_h), flip_seq(kk), flip_seq(to_heads(icl[1], H_B)), s0_rwkv[:, 1])
    bonus = jnp.sum(r_h * to_heads(k_b, H_B) * rw_rk[None, :, None, :], axis=-1, keepdims=True) * v_h
    o_rwkv = (head_group_norm(y_f + flip_seq(y_b), rw_gn_g, rw_gn_b) + from_heads(bonus)) * (jax.nn.sigmoid(g_lr) @ rw_g2)
    out = jnp.concatenate([o_gla, o_rwkv], axis=-1) @ w_out
    return out, jnp.stack([sg_f, sg_b], axis=1), jnp.stack([sr_f, sr_b], axis=1)

def odd_project(h, w_in, q_norm_g, w_q_up, kv_norm_g, mla_qn_g, diff_qn_g, diff_kn_g):
    b, l, _ = h.shape
    cq, ckv, krope, qd, kd, vd = split_cols(h @ w_in, ODD_SPLITS)
    q_c = rms_norm(to_heads(rms_norm(cq, q_norm_g) @ w_q_up, H_C), mla_qn_g)
    ckv = rms_norm(ckv, kv_norm_g)
    q_d = rms_norm(qd.reshape(b, l, H_D, 2, DH_D).transpose(0, 2, 3, 1, 4), diff_qn_g)
    k_d = rms_norm(kd.reshape(b, l, H_D, 2, DH_D).transpose(0, 2, 3, 1, 4), diff_kn_g)
    v_d = to_heads(vd, H_D)
    return q_c, ckv, krope, q_d, k_d, v_d

def mla_keys(ckv, krope, w_kv_up, mla_kn_g):
    b, l, _ = ckv.shape
    kv = to_heads(ckv @ w_kv_up, H_C)
    k_r = jnp.broadcast_to(krope[:, None], (b, H_C, l, ROPE_C)).astype(kv.dtype)
    k = rms_norm(jnp.concatenate([kv[..., :NOPE_C], k_r], axis=-1), mla_kn_g)
    return k, kv[..., NOPE_C:]

def lambda_init(layer_idx):
    return 0.8 - 0.6 * math.exp(-0.3 * layer_idx)

def odd_attend(q_c, k_c, v_c, q_d, k_d, v_d, lam_p, lam_init, subln_g, w_out):
    o_c = blocked_attention(q_c[:, :, None], k_c[:, :, None], v_c, (NOPE_C + ROPE_C) ** -0.5)[:, :, 0]
    o_d = blocked_attention(q_d, k_d, v_d, DH_D ** -0.5)
    lp = lam_p.astype(jnp.float32)
    lam = jnp.exp(jnp.sum(lp[0] * lp[1])) - jnp.exp(jnp.sum(lp[2] * lp[3])) + lam_init
    o_d = rms_norm(o_d[:, :, 0] - lam * o_d[:, :, 1], subln_g) * (1.0 - lam_init)
    return jnp.concatenate([from_heads(o_c), from_heads(o_d)], axis=-1) @ w_out

def moe(h, w_router, b_router, w_gate, w_up, w_down):
    b, l, d = h.shape
    t = h.reshape(b * l, d)
    scores = jax.nn.sigmoid((t @ w_router).astype(jnp.float32))
    sel = scores + b_router.astype(jnp.float32)
    group_score = jnp.sum(lax.top_k(sel.reshape(-1, N_GROUPS, EXPERTS_PER_GROUP), TOP_K)[0], axis=-1)
    best_group = jnp.argmax(group_score, axis=-1)
    in_group = jnp.repeat(best_group[:, None] == jnp.arange(N_GROUPS)[None, :], EXPERTS_PER_GROUP, axis=-1)
    _, top_idx = lax.top_k(jnp.where(in_group, sel, -jnp.inf), TOP_K)
    top_w = jnp.take_along_axis(scores, top_idx, axis=-1)
    top_w = top_w / jnp.sum(top_w, axis=-1, keepdims=True)
    gates = jnp.einsum('nk,nke->ne', top_w, jax.nn.one_hot(top_idx, N_EXPERTS, dtype=jnp.float32))
    hidden = jax.nn.silu(jnp.einsum('nd,edf->nef', t, w_gate)) * jnp.einsum('nd,edf->nef', t, w_up)
    out = jnp.einsum('nef,efd->nd', hidden * gates[..., None].astype(hidden.dtype), w_down)
    return out.reshape(b, l, d)

def setup_inputs(seed: int = 0) -> dict:
    key = jax.random.key(seed)
    ks = iter(jax.random.split(key, 80))

    def nrm(shape, s):
        return s * jax.random.normal(next(ks), shape, jnp.float32)

    def gain(shape):
        return 1.0 + 0.05 * jax.random.normal(next(ks), shape, jnp.float32)

    D = D_MODEL
    return {
        'x_prompt': nrm((BATCH, SEQ, D), 1.0),
        'x_sample': nrm((DEC_BATCH, DEC_SEQ, D), 1.0),
        'state_gla': nrm((DEC_BATCH, N_EVEN, 2, H_A, DK_A, DV_A), 0.3),
        'state_rwkv': nrm((DEC_BATCH, N_EVEN, 2, H_B, N_B, N_B), 0.3),
        'cache_mla_ckv': nrm((DEC_BATCH, N_ODD, PAST_LEN, KV_RANK), 1.0),
        'cache_mla_krope': nrm((DEC_BATCH, N_ODD, PAST_LEN, ROPE_C), 1.0),
        'cache_diff_k': nrm((DEC_BATCH, N_ODD, H_D, 2, PAST_LEN, DH_D), 1.0),
        'cache_diff_v': nrm((DEC_BATCH, N_ODD, H_D, PAST_LEN, DV_D), 1.0),
        'c': nrm((DEC_BATCH, D), 1.0),
        'c_ctx': nrm((D,), 1.0),
        'norm_g': gain((DEPTH, 2, D)),
        'w_mod': nrm((DEPTH, D, 6 * D), 0.5 * D ** -0.5),
        'b_mod': nrm((DEPTH, 6 * D), 0.02),
        'ev_w_in': nrm((N_EVEN, D, EVEN_COLS), D ** -0.5),
        'gla_a_up': nrm((N_EVEN, 2, ALPHA_RANK, H_A * DK_A), ALPHA_RANK ** -0.5),
        'gla_a_b': 1.0 + nrm((N_EVEN, 2, H_A * DK_A), 0.1),
        'gla_o_g': gain((N_EVEN, DV_A)),
        'rw_w0': nrm((N_EVEN, 2, H_B * N_B), 0.5),
        'rw_w2': nrm((N_EVEN, 2, W_LORA, H_B * N_B), 0.1),
        'rw_a0': nrm((N_EVEN, 2, H_B * N_B), 0.1),
        'rw_a2': nrm((N_EVEN, 2, A_LORA, H_B * N_B), 0.1),
        'rw_g2': nrm((N_EVEN, G_LORA, H_B * N_B), G_LORA ** -0.5),
        'rw_kk': 0.85 + nrm((N_EVEN, H_B * N_B), 0.05),
        'rw_ka': gain((N_EVEN, H_B * N_B)),
        'rw_rk': nrm((N_EVEN, H_B, N_B), 0.1),
        'rw_gn_g': gain((N_EVEN, H_B * N_B)),
        'rw_gn_b': nrm((N_EVEN, H_B * N_B), 0.02),
        'ev_w_out': nrm((N_EVEN, MIX_WIDTH, D), MIX_WIDTH ** -0.5),
        'od_w_in': nrm((N_ODD, D, ODD_COLS), D ** -0.5),
        'mla_qa_g': gain((N_ODD, Q_RANK)),
        'mla_q_up': nrm((N_ODD, Q_RANK, H_C * (NOPE_C + ROPE_C)), Q_RANK ** -0.5),
        'mla_kva_g': gain((N_ODD, KV_RANK)),
        'mla_kv_up': nrm((N_ODD, KV_RANK, H_C * (NOPE_C + DV_C)), KV_RANK ** -0.5),
        'mla_qn_g': gain((N_ODD, NOPE_C + ROPE_C)),
        'mla_kn_g': gain((N_ODD, NOPE_C + ROPE_C)),
        'diff_qn_g': gain((N_ODD, DH_D)),
        'diff_kn_g': gain((N_ODD, DH_D)),
        'diff_lam': nrm((N_ODD, 4, DH_D), 0.1),
        'diff_subln_g': gain((N_ODD, DV_D)),
        'od_w_out': nrm((N_ODD, MIX_WIDTH, D), MIX_WIDTH ** -0.5),
        'moe_w_router': nrm((D, N_EXPERTS), D ** -0.5),
        'moe_b_router': nrm((N_EXPERTS,), 0.01),
        'moe_w_gate': nrm((DEPTH, N_EXPERTS, D, D_FF_EXPERT), D ** -0.5),
        'moe_w_up': nrm((DEPTH, N_EXPERTS, D, D_FF_EXPERT), D ** -0.5),
        'moe_w_down': nrm((DEPTH, N_EXPERTS, D_FF_EXPERT, D), D_FF_EXPERT ** -0.5),
    }

def reference(x_prompt, x_sample, state_gla, state_rwkv, cache_mla_ckv, cache_mla_krope, cache_diff_k, cache_diff_v,
              c, c_ctx, norm_g, w_mod, b_mod,
              ev_w_in, gla_a_up, gla_a_b, gla_o_g, rw_w0, rw_w2, rw_a0, rw_a2, rw_g2, rw_kk, rw_ka, rw_rk,
              rw_gn_g, rw_gn_b, ev_w_out,
              od_w_in, mla_qa_g, mla_q_up, mla_kva_g, mla_kv_up, mla_qn_g, mla_kn_g, diff_qn_g, diff_kn_g,
              diff_lam, diff_subln_g, od_w_out,
              moe_w_router, moe_b_router, moe_w_gate, moe_w_up, moe_w_down):

    def trunk(x, cond, latent, st_gla, st_rwkv, c_ckv, c_krope, c_dk, c_dv):
        b, l, _ = x.shape
        out_gla, out_rwkv, out_ckv, out_krope, out_dk, out_dv = [], [], [], [], [], []
        if latent:
            cos_c, sin_c = axial_rope_tables(l, ROPE_C)
            cos_d, sin_d = axial_rope_tables(l, DH_D)
        for li in range(DEPTH):
            j = li // 2
            mod = (jax.nn.silu(cond) @ w_mod[li] + b_mod[li])[:, None, :]
            sh1, sc1, g1, sh2, sc2, g2 = jnp.split(mod, 6, axis=-1)
            h = rms_norm(x, norm_g[li, 0]) * (1.0 + sc1) + sh1
            if li % 2 == 0:
                if latent:
                    s0g, s0r = st_gla[:, j], st_rwkv[:, j]
                else:
                    s0g = jnp.zeros((b, 2, H_A, DK_A, DV_A), x.dtype)
                    s0r = jnp.zeros((b, 2, H_B, N_B, N_B), x.dtype)
                mix, sg, sr = even_mixer(h, s0g, s0r, ev_w_in[j], gla_a_up[j], gla_a_b[j], gla_o_g[j], rw_w0[j],
                                         rw_w2[j], rw_a0[j], rw_a2[j], rw_g2[j], rw_kk[j], rw_ka[j], rw_rk[j],
                                         rw_gn_g[j], rw_gn_b[j], ev_w_out[j])
                out_gla.append(sg)
                out_rwkv.append(sr)
            else:
                q_c, ckv, krope, q_d, k_d, v_d = odd_project(h, od_w_in[j], mla_qa_g[j], mla_q_up[j], mla_kva_g[j],
                                                             mla_qn_g[j], diff_qn_g[j], diff_kn_g[j])
                k_c, v_c = mla_keys(ckv, krope, mla_kv_up[j], mla_kn_g[j])
                if latent:
                    q_c = rope_tail(q_c, cos_c, sin_c)
                    k_c = rope_tail(k_c, cos_c, sin_c)
                    q_d = apply_axial_rope(q_d, cos_d, sin_d)
                    k_d = apply_axial_rope(k_d, cos_d, sin_d)
                    k_x, v_x = mla_keys(c_ckv[:, j], c_krope[:, j], mla_kv_up[j], mla_kn_g[j])
                    k_c = jnp.concatenate([k_x.astype(k_c.dtype), k_c], axis=2)
                    v_c = jnp.concatenate([v_x.astype(v_c.dtype), v_c], axis=2)
                    k_d = jnp.concatenate([c_dk[:, j].astype(k_d.dtype), k_d], axis=3)
                    v_d = jnp.concatenate([c_dv[:, j].astype(v_d.dtype), v_d], axis=2)
                else:
                    out_ckv.append(ckv)
                    out_krope.append(krope)
                    out_dk.append(k_d)
                    out_dv.append(v_d)
                mix = odd_attend(q_c, k_c, v_c, q_d, k_d, v_d, diff_lam[j], lambda_init(li), diff_subln_g[j], od_w_out[j])
            x = x + g1 * mix.astype(x.dtype)
            h = rms_norm(x, norm_g[li, 1]) * (1.0 + sc2) + sh2
            x = x + g2 * moe(h, moe_w_router, moe_b_router, moe_w_gate[li], moe_w_up[li], moe_w_down[li]).astype(x.dtype)
        return x, out_gla, out_rwkv, out_ckv, out_krope, out_dk, out_dv

    y_prompt, gla_p, rwkv_p, ckv_p, krope_p, dk_p, dv_p = trunk(x_prompt, c_ctx[None, :], False,
                                                                None, None, None, None, None, None)
    y_sample = trunk(x_sample, c, True, state_gla, state_rwkv, cache_mla_ckv, cache_mla_krope,
                     cache_diff_k, cache_diff_v)[0]
    dt = x_prompt.dtype
    new_state_gla = jnp.stack(gla_p, axis=1).astype(dt)
    new_state_rwkv = jnp.stack(rwkv_p, axis=1).astype(dt)
    new_cache_mla_ckv = jnp.stack(ckv_p, axis=1).astype(dt)
    new_cache_mla_krope = jnp.stack(krope_p, axis=1).astype(dt)
    new_cache_diff_k = jnp.stack(dk_p, axis=1).astype(dt)
    new_cache_diff_v = jnp.stack(dv_p, axis=1).astype(dt)
    return (y_prompt, y_sample, new_state_gla, new_state_rwkv, new_cache_mla_ckv, new_cache_mla_krope,
            new_cache_diff_k, new_cache_diff_v)


_drawn_inputs = setup_inputs


def setup_inputs(seed=0):
    import zlib

    import numpy as np

    out = dict(_drawn_inputs(seed))
    spreads = {}
    factors = {'state_gla': 8.0,
     'state_rwkv': 8.0,
     'cache_mla_ckv': 3.044,
     'cache_mla_krope': 5.997,
     'gla_o_g': 3.178,
     'rw_kk': 5.908,
     'rw_gn_b': 3.846,
     'mla_qa_g': 8.0,
     'mla_qn_g': 8.0,
     'mla_kn_g': 5.538,
     'diff_qn_g': 3.589,
     'diff_subln_g': 3.186}
    for name, (base, spread) in spreads.items():
        noise = np.random.default_rng([zlib.crc32(name.encode()), seed]).standard_normal(out[name].shape)
        drawn = base * np.exp(spread * noise) if base else spread * noise
        out[name] = __import__('jax').numpy.asarray(drawn.astype(out[name].dtype))
    for name, factor in factors.items():
        out[name] = (out[name] * factor).astype(out[name].dtype)
    return out
```

```python
import math
from contextlib import ExitStack

import concourse.bass as bass
from concourse import mybir

F32 = mybir.dt.float32
ALU = mybir.AluOpType
ACT = mybir.ActivationFunctionType
AX = mybir.AxisListType

P = 128
D = 1024
KD = D // P
TILES = 3
NTOK = TILES * P
CH = 64
EPS = 1e-6
GN_EPS = 64e-5
NE = 16
FF = 512
KF = FF // P
SLOTS = 3
CHUNK = KD * 512
EQ, EK_, EV, EG, EAL, ER, EKB, EVB, EWL, EAA, EGL, EVEN = 0, 256, 512, 1024, 1536, 1568, 2080, 2592, 3104, 3232, 3360, 3488
OCQ, OCKV, OKR, OQD, OKD, OVD, ODD = 0, 256, 384, 416, 928, 1440, 1952
RW = math.exp(-0.5)
LAM_INIT = 0.8 - 0.6 * math.exp(-0.3 * 1)
MIX_EIN, MIX_EOUT, MIX_OIN, MIX_OOUT = 0, 7, 9, 13

_C = {}
_at = 0
for _n, _w in [("ident", 128), ("lt", 128), ("le", 128), ("gt", 128), ("ge", 128), ("half", 2),
               ("lvl0", 768), ("lvl1", 768), ("sel", 256), ("bdg", 256), ("bdr", 128), ("tie", 16),
               ("cosc", 64), ("sinc", 64), ("cosd", 128), ("sind", 128), ("one", 1)]:
    _C[_n] = (_at, _w)
    _at += _w
NCONST = _at
COL_C, COL_NG, COL_BM, NCOL = 0, 16, 48, 144
_R = {}
_at = 0
for _n, _w in [("gla_a_b", 512), ("rw_w0", 1024), ("rw_a0", 1024), ("rw_kk", 512), ("rw_ka", 512), ("rw_rk", 512)]:
    _R[_n] = (_at, _w)
    _at += _w
NROW_E = _at
_at = 0
for _n, _w in [("rw_gn_g", 512), ("rw_gn_b", 512), ("gla_o_g", 128)]:
    _R[_n] = (_at, _w)
    _at += _w
NROW_G = _at
_at = 0
for _n, _w in [("mla_qa_g", 256), ("mla_kva_g", 128), ("mla_qn_g", 96), ("mla_kn_g", 96), ("diff_qn_g", 64),
               ("diff_kn_g", 64), ("diff_lam", 256), ("diff_subln_g", 128)]:
    _R[_n] = (_at, _w)
    _at += _w
NROW_O = _at


def bc(ap, axis, n):
    a = ap.unsqueeze(axis)
    shape = list(a.shape)
    shape[axis] = n
    return a.broadcast_to(shape)


def build(nc, io, known):
    seen = {}
    count = {"pe": 0, "act": 0, "dve": 0, "pool": 0}
    with ExitStack() as ctx:
        def sb(name, cols, rows=P):
            return ctx.enter_context(nc.sbuf_tensor(name, [rows, cols], F32))

        sems = {}

        def sem(name):
            if name not in sems:
                sems[name] = ctx.enter_context(nc.semaphore(name))
            return sems[name]

        for e in count:
            sem(e)

        def tick(engine, *name):
            count[engine] += 1
            if name:
                seen[name] = (engine, count[engine])
            return sem(engine), 1

        def when(*name):
            engine, value = known.get(name, ("pe", 1)) if known is not None else ("pe", 1)
            if known and name not in known:
                raise KeyError(name)
            return sem(engine), value

        def end(engine, stage):
            seen[("end", engine, stage)] = (engine, count[engine])

        def meet(eng, me, stage, others=("pe", "act", "dve")):
            for e in others:
                if e != me:
                    s, value = when("end", e, stage)
                    if value > 0:
                        eng.wait_ge(s, value)

        PB = ctx.enter_context(nc.psum_tensor("PB", [P, 8, 512], F32))
        cst = sb("cst", NCONST)
        cols = sb("cols", NCOL)
        x = sb("x", TILES * D)
        hT = sb("hT", KD * NTOK)
        ring = sb("ring", SLOTS * CHUNK)
        gate = sb("gate", 2 * 2 * D)
        modT = sb("modT", 96)
        mulA = sb("mulA", 2 * KD * 2)
        scT = sb("scT", 16)
        small = sb("small", 256)
        brout = sb("brout", 16)
        wrout = sb("wrout", KD * NE)
        gates = sb("gates", TILES * NE)
        arena_words = 26448
        arena = sb("arena", arena_words)

        def C(name, lo=0, n=None):
            s, w = _C[name]
            return cst[:, s + lo:s + (w if n is None else lo + n)]

        xv = x[:, :].rearrange("p (t d) -> p t d", t=TILES)
        hTv = hT[:, :].rearrange("p (k n) -> p k n", k=KD)
        slot = [ring[:, s * CHUNK:(s + 1) * CHUNK].rearrange("p (k n) -> p k n", k=KD) for s in range(SLOTS)]
        slot_dn = [ring[:, s * CHUNK:(s + 1) * CHUNK].rearrange("p (k n) -> p k n", k=KF) for s in range(SLOTS)]
        gatev = gate[:, :].rearrange("p (c s d) -> p c s d", c=2, s=2)
        modTv = modT[:, :].rearrange("p (j c) -> p j c", c=2)
        mulAv = mulA[:, :].rearrange("p (s k c) -> p s k c", s=2, c=2)
        ident = C("ident")

        def carve(at):
            pos = [at]

            def take(words):
                a = pos[0]
                pos[0] += words
                assert pos[0] <= arena_words, pos[0]
                return arena[:, a:a + words]
            return take

        take = carve(0)
        E = take(2 * EVEN).rearrange("p (t n) -> p t n", t=2)
        rowsE = take(NROW_E)
        oG = take(2 * 512).rearrange("p (t n) -> p t n", t=2)
        yR = take(2 * 512).rearrange("p (t n) -> p t n", t=2)
        kkn = take(2 * 512).rearrange("p (t n) -> p t n", t=2)
        loT = take(2 * 512).rearrange("p (t j n) -> p t j n", t=2, j=4)
        bon = take(16).rearrange("p (t h) -> p t h", t=2)
        SG = take(2 * 512).rearrange("p (d j n) -> p d j n", d=2, j=2)
        SR = take(2 * 512).rearrange("p (d j n) -> p d j n", d=2, j=4)
        tokm = take(4 * 512).rearrange("p (a n) -> p a n", a=4)
        G4 = take(4 * 512).rearrange("p (h n) -> p h n", h=4)
        TA = take(512).rearrange("p (a n) -> p a n", a=4)
        TB = take(512).rearrange("p (a n) -> p a n", a=4)
        X4 = take(512).rearrange("p (h n) -> p h n", h=4)
        XT4 = take(512).rearrange("p (h n) -> p h n", h=4)
        T14 = take(512).rearrange("p (h n) -> p h n", h=4)
        LJ4 = take(512).rearrange("p (h n) -> p h n", h=4)
        RH = take(256)
        UU = take(256)
        aup = take(512)
        w2 = take(512)
        a2 = take(512)
        rowsG = tokm.rearrange("p a n -> p (a n)")[:, 0:NROW_G]
        g2w = tokm[:, 3, :]
        tmpE = X4.rearrange("p h n -> p (h n)"), XT4.rearrange("p h n -> p (h n)"), T14.rearrange("p h n -> p (h n)")
        stg = G4

        xn = tokm.rearrange("p a n -> p (a n)")[:, 0:1024]
        rowb = xn[0:2, :]

        take = carve(0)
        O = take(3 * ODD).rearrange("p (t n) -> p t n", t=3)
        rowsO = take(NROW_O)
        cdk = take(512).rearrange("p (m n) -> p m n", m=8)
        cdv = take(512).rearrange("p (h n) -> p h n", h=4)
        cckv = take(128)
        ckr = take(32)
        kvup = take(1024)
        u0 = take(1536)
        cqT = take(2 * NTOK).rearrange("p (k n) -> p k n", k=2)
        ckT = take(4 * P).rearrange("p (k n) -> p k n", k=4)
        kT = take(8 * 512).rearrange("p (h n) -> p h n", h=8)
        vC = take(4 * 512).rearrange("p (k h n) -> p k h n", k=4, h=8)
        dqT = take(4 * NTOK).rearrange("p (h n) -> p h n", h=4)
        dkT = take(4 * 512).rearrange("p (h n) -> p h n", h=4)
        hd = take(768)
        hd2 = take(768)
        qup = u0.rearrange("p (k n) -> p k n", k=2)
        prob = take(2 * 384).rearrange("p (b n) -> p b n", b=2)
        probT = take(2 * 384).rearrange("p (b k n) -> p b k n", b=2, k=3)
        mix = u0[:, 0:1024]

        take = carve(0)
        hid = take(2 * KF * NTOK).rearrange("p (b j n) -> p b j n", b=2, j=KF)
        sil = take(4 * NTOK).rearrange("p (b n) -> p b n", b=4)
        acc = take(TILES * D).rearrange("p (t d) -> p t d", t=TILES)
        gcur = take(TILES)

        def R(rows, name, lo=0, n=None):
            s, w = _R[name]
            return rows[:, s + lo:s + (w if n is None else lo + n)]

        stream = [("mod", (0, n), ("modp", 0, n)) for n in range(12)]
        stream += [("mix", MIX_EIN + n, ("ein", 0, n)) for n in range(7)]
        stream += [("mix", MIX_EIN + n, ("ein", 1, n)) for n in range(7)]
        stream += [("mix", MIX_EOUT + n, ("outp", 0, n)) for n in range(2)]
        first = len(stream)
        stream += [("mod", (1, n), ("modp", 1, n)) for n in range(12)]
        stream += [("mix", MIX_OIN + n, ("oin", n)) for n in range(4)]
        stream += [("mix", MIX_OOUT + n, ("outp", 1, n)) for n in range(2)]
        where, landed, before = {}, {}, []
        cnt, pos = [0] * SLOTS, 0
        for i, (kind, src, name) in enumerate(stream):
            if i == first:
                pos = 0
                cnt = [c + NE for c in cnt]
            s = pos % SLOTS
            pos += 1
            cnt[s] += 1
            where[name], landed[name] = s, 16 * cnt[s]
        base = [0, 0]
        per = [sum(1 for n in stream[:first] if where[n[2]] == s) for s in range(SLOTS)]
        per1 = [sum(1 for n in stream[first:] if where[n[2]] == s) for s in range(SLOTS)]
        moe_base = [[16 * c for c in per], [16 * (a + NE + b) for a, b in zip(per, per1)]]
        w_land = [sem(f"w_landed{s}") for s in range(SLOTS)]
        gu_done, silu_done, hid_done, dn_done, acc_done = (sem(n) for n in (
            "gate_up_done", "silu_done", "hidden_done", "down_done", "acc_done"))
        NJ = KF
        ND = TILES * 2
        CREDIT = 4

        block = ctx.enter_context(nc.Block())

        @block.sync
        def _(sp):
            owner = [None] * SLOTS

            def load(kind, src, name):
                s = where[name]
                if owner[s] is not None:
                    sp.wait_ge(*when(*owner[s]))
                owner[s] = name
                dram = io["w_mod"][src[0], src[1]] if kind == "mod" else io["w_mix"][src]
                sp.dma_start(ring[:, s * CHUNK:(s + 1) * CHUNK], dram).then_inc(w_land[s], 16)

            def experts(layer):
                for s in range(SLOTS):
                    if owner[s] is not None:
                        sp.wait_ge(*when(*owner[s]))
                    owner[s] = None
                with sp.Fori(0, NE) as i:
                    sp.wait_ge(gu_done, i * NJ + (layer * NE * NJ + 1))
                    for m in range(2):
                        sp.dma_start(ring[:, m * CHUNK:(m + 1) * CHUNK],
                                     io["w_moe"][layer][m][bass.ds(i, 1)].rearrange("e p n -> (e p) n"))\
                            .then_inc(w_land[m], 16)
                    sp.wait_ge(dn_done, i * ND + (layer * NE * ND + 1))
                    sp.dma_start(ring[:, 2 * CHUNK:3 * CHUNK],
                                 io["w_moe"][layer][2][bass.ds(i, 1)].rearrange("e p n -> (e p) n"))\
                        .then_inc(w_land[2], 16)

            for item in stream[:first]:
                load(*item)
            experts(0)
            sp.wait_ge(gu_done, NE * NJ + 1)
            sp.wait_ge(dn_done, NE * ND + 1)
            for item in stream[first:]:
                load(*item)
            experts(1)

        @block.gpsimd
        def _(pool):
            def dma(dst, src, name):
                pool.dma_start(dst, src).then_inc(sem(name), 16)

            dma(cst[:, :], io["consts"], "ld_const")
            dma(cols[:, :], io["cols"], "ld_const")
            for t in range(TILES):
                dma(xv[:, t, :], io["x"][t], "ld_x")
            dma(brout[:, :], io["b_router"].partition_broadcast(P), "ld_router")
            dma(wrout[:, :], io["w_router"], "ld_router")
            for c in range(2):
                for s in range(2):
                    dma(gatev[:, c, s, :], io["b_gate"][0, s].partition_broadcast(P), "ld_bgate")
            dma(rowsE, io["rows_even"].partition_broadcast(P), "ld_even")
            nc.gpsimd.memset(aup[0:32, :], 0.0).then_inc(*tick("pool", "aup0"))
            pool.wait_ge(*when("aup0"))
            for d in range(2):
                dma(aup[16 * d:16 * d + 16, 256 * d:256 * d + 256], io["gla_a_up"][d], "ld_even")
            dma(w2, io["rw_w2"], "ld_even")
            dma(a2, io["rw_a2"], "ld_even")

            def late_rows(g):
                meet(pool, "pool", f"units{g}")
                dma(rowsG, io["rows_gain"].partition_broadcast(P), "ld_late")
                dma(g2w, io["rw_g2"], "ld_late")

            nc.gpsimd.memset(SG, 0.0).then_inc(*tick("pool", "SG0"))
            nc.gpsimd.memset(SR, 0.0).then_inc(*tick("pool", "SR0"))
            late_rows(0)
            for d in range(2):
                for h in range(4):
                    r = 64 * (h % 2)
                    dma(io["new_state_gla"][d, h], SG[r:r + 64, d, h // 2, 128 * (h % 2):128 * (h % 2) + 128], "st_gla")
            pool.wait_ge(*when("state_out_T"))
            for d in range(2):
                for h in range(8):
                    r = 64 * (h % 2)
                    dma(io["new_state_rwkv"][d, h], stg[r:r + 64, d, (h // 2) * 128 + r:(h // 2) * 128 + r + 64], "st_rwkv")
            pool.wait_ge(sem("st_gla"), 8 * 16)
            pool.wait_ge(sem("st_rwkv"), 16 * 16)
            nc.gpsimd.memset(SG, 0.0).then_inc(*tick("pool", "SG1"))
            nc.gpsimd.memset(stg[:, 0:2, :], 0.0).then_inc(*tick("pool", "stg0"))
            pool.wait_ge(*when("stg0"))
            for d in range(2):
                for h in range(4):
                    r = 64 * (h % 2)
                    dma(SG[r:r + 64, d, h // 2, 128 * (h % 2):128 * (h % 2) + 128], io["state_gla"][d, h], "ld_sg")
                for h in range(8):
                    r = 64 * (h % 2)
                    dma(stg[r:r + 64, d, (h // 2) * 128 + r:(h // 2) * 128 + r + 64], io["state_rwkv"][d, h], "ld_sr")
            late_rows(1)
            meet(pool, "pool", "moe0")
            for c in range(2):
                for s in range(2):
                    dma(gatev[:, c, s, :], io["b_gate"][1, s].partition_broadcast(P), "ld_bgate")
            dma(rowsO, io["rows_odd"].partition_broadcast(P), "ld_odd")
            dma(qup, io["mla_q_up"].rearrange("(k p) n -> p k n", p=P), "ld_odd")
            dma(kvup, io["mla_kv_up"], "ld_odd")
            dma(cckv, io["cache_mla_ckv"], "ld_odd")
            dma(ckr, io["cache_mla_krope"], "ld_odd")
            for m in range(8):
                dma(cdk[:, m, :], io["cache_diff_k"][m // 2, m % 2], "ld_odd")
            for h in range(4):
                dma(cdv[:, h, :], io["cache_diff_v"][h], "ld_odd")
            pool.wait_ge(*when("caches"))
            dma(io["new_ckv"], O[:, 0, OCKV:OCKV + 128], "st_cache")
            dma(io["new_krope"], O[:, 0, OKR:OKR + 32], "st_cache")
            for m in range(8):
                dma(io["new_dk"][m // 2, m % 2], O[:, 0, OKD + 64 * m:OKD + 64 * m + 64], "st_cache")
            for h in range(4):
                dma(io["new_dv"][h], O[:, 0, OVD + 128 * h:OVD + 128 * h + 128], "st_cache")
            pool.wait_ge(sem("st_cache"), 14 * 16)
            nc.gpsimd.memset(small[:, 255:256], 0.0).then_inc(*tick("pool", "caches_stored"))
            for t in range(TILES):
                pool.wait_ge(*when("x_moe", 1, t))
                dma(io["y"][t], xv[:, t, :], "st_y")
            pool.wait_ge(sem("st_y"), TILES * 16)

        @block.tensor
        def _(pe):
            reader = [None] * 8

            def claim(b, *name):
                if reader[b] is not None:
                    pe.wait_ge(*when(*reader[b]))
                reader[b] = name

            def mm(out, lhsT, rhs, start=True, stop=True, **k):
                return nc.tensor.matmul(out, lhsT, rhs, start=start, stop=stop, **k)

            def tp(out, in_, n=P):
                return nc.tensor.transpose(out, in_, ident[0:n, 0:n])

            def chunk_landed(*name):
                pe.wait_ge(w_land[where[name]], landed[name])
                return slot[where[name]]

            def mods(l):
                def post(n):
                    pe.wait_ge(*when("modrow", l, n))
                    row = rowb[0:2, 512 * (n % 2):512 * (n % 2) + 512]
                    if n // 2 in (2, 5):
                        for c in range(2):
                            claim(2 + c, "gadd", l, n, c)
                            mm(PB[:, 2 + c, :], C("sel", 128 * c, 128)[0:2, :], row).then_inc(*tick("pe", "gb", l, n, c))
                    else:
                        claim(4 + n % 2, "modT", l, n)
                        for j in range(4):
                            ins = tp(PB[:, 4 + n % 2, 2 * j:2 * j + 2], row[:, 128 * j:128 * j + 128], 2)
                        ins.then_inc(*tick("pe", "mt", l, n))
                for n in range(12):
                    w = chunk_landed("modp", l, n)
                    claim(n % 2, "modrow", l, n)
                    for k in range(KD):
                        ins = mm(PB[0:2, n % 2, :], scT[:, 2 * k:2 * k + 2], w[:, k, :], k == 0, k == KD - 1)
                    ins.then_inc(*tick("pe", "modp", l, n))
                    if n:
                        post(n - 1)
                post(11)
                end("pe", f"mods{l}")

            def norm(l, s):
                for t in range(TILES):
                    pe.wait_ge(*when("xn", l, s, t))
                    for b in range(2):
                        claim(6 + b, "hT", l, s, t, b)
                        for k in range(4):
                            ins = tp(PB[:, 6 + b, 128 * k:128 * k + 128], xn[:, (4 * b + k) * 128:(4 * b + k + 1) * 128])
                        ins.then_inc(*tick("pe", "xnT", l, s, t, b))

            def project(name, tiles, chunks, width):
                bank = 0
                for n in range(chunks):
                    w = chunk_landed(*name, n)
                    ncol = min(512, width - 512 * n)
                    for i, t in enumerate(tiles):
                        claim(bank % 4, *name, "evac", n, i)
                        for k in range(KD):
                            ins = mm(PB[:, bank % 4, 0:ncol], hTv[:, k, t * P:(t + 1) * P], w[:, k, 0:ncol],
                                     k == 0, k == KD - 1)
                        bank += 1
                        ins.then_inc(*tick("pe", *name, "p", n, i))
                    seen[(*name, n)] = ("pe", count["pe"])

            def lora_T(g, i):
                pe.wait_ge(*when("lora", g, i))
                claim(0, "loT", g, i)
                for j, (c0, n) in enumerate([(EWL, 128), (EAA, 128), (EGL, 128), (EAL, 32)]):
                    ins = tp(PB[0:n, 0, 128 * j:128 * j + 128], E[:, i, c0:c0 + n])
                ins.then_inc(*tick("pe", "lora_T", g, i))

            def gla(g, i, d):
                u = (g, i, d)
                inc, rest = (C("le"), C("gt")) if d == 0 else (C("ge"), C("lt"))
                pe.wait_ge(*when("loT", g, i))
                claim(0, "ga_z", *u)
                mm(PB[:, 0, 0:256], loT[0:32, i, 3, :], aup[0:32, 256 * d:256 * d + 256]).then_inc(*tick("pe", "za", *u))
                pe.wait_ge(*when("la", *u))
                claim(1, "g_exp", *u)
                claim(2, "g_dec", *u)
                la = tmpE[0][:, 0:256]
                mm(PB[:, 1, 0:256], inc, la)
                mm(PB[:, 1, 256:512], rest, la)
                for j in range(2):
                    ins = mm(PB[:, 2, 2 * j:2 * j + 2], la[:, 128 * j:128 * j + 128], C("half"))
                ins.then_inc(*tick("pe", "gcum", *u))
                pe.wait_ge(*when("gk", *u))
                claim(3, "gqkT", *u)
                for j in range(4):
                    ins = tp(PB[:, 3, 128 * j:128 * j + 128], tokm[:, j // 2, 128 * (j % 2):128 * (j % 2) + 128])
                ins.then_inc(*tick("pe", "gT", *u))
                pe.wait_ge(*when("gqkT", *u))
                claim(4, "gatt", *u)
                claim(5, "gatt", *u)
                for h in range(4):
                    r, j = 64 * (h % 2), h // 2
                    ins = mm(PB[:, 4 + h % 2, 128 * j:128 * j + 128], TA[r:r + 64, 2 + j, :], TA[r:r + 64, j, :])
                ins.then_inc(*tick("pe", "gA", *u))
                pe.wait_ge(*when("gatt", *u))
                claim(6, "gout", *u)
                for h in range(4):
                    mm(PB[:, 6, 128 * h:128 * h + 128], G4[:, h, 0:128], E[:, i, EV + 128 * h:EV + 128 * h + 128],
                       h == 0, False, skip_group_check=True)
                for n, c in enumerate((0, 1) if d == 0 else (1, 0)):
                    if n:
                        pe.wait_ge(*when("gS", *u, 0))
                    r = CH * c
                    for j in range(2):
                        mm(PB[r:r + CH, 6, 256 * j:256 * j + 256], TA[:, j, r:r + CH], SG[:, d, j, :],
                           False, n == 1, skip_group_check=True)
                    claim(7, "gS", *u, n)
                    for j in range(2):
                        ins = mm(PB[:, 7, 256 * j:256 * j + 256], tokm[r:r + CH, 2, 128 * j:128 * j + 128],
                                 E[r:r + CH, i, EV + 256 * j:EV + 256 * j + 256], skip_group_check=True)
                    ins.then_inc(*tick("pe", "gu", *u, n))

            def rwkv(g, i, d):
                u = (g, i, d)
                inc, exc = (C("le"), C("lt")) if d == 0 else (C("ge"), C("gt"))
                r = 64 * d
                claim(d, "r_zw", *u)
                mm(PB[:, d, :], loT[r:r + 64, i, 0, :], w2[r:r + 64, :]).then_inc(*tick("pe", "zw", *u))
                claim(2 + d, "r_za", *u)
                mm(PB[:, 2 + d, :], loT[r:r + 64, i, 1, :], a2[r:r + 64, :]).then_inc(*tick("pe", "zr", *u))
                pe.wait_ge(*when("lw", *u))
                lw = tmpE[0]
                claim(4, "e_inc", *u)
                mm(PB[:, 4, :], inc, lw)
                claim(5, "e_exc", *u)
                mm(PB[:, 5, :], exc, lw)
                claim(6, "e_wc", *u)
                for j in range(4):
                    ins = mm(PB[:, 6, 2 * j:2 * j + 2], lw[:, 128 * j:128 * j + 128], C("half"))
                ins.then_inc(*tick("pe", "rcum", *u))
                pe.wait_ge(*when("tokm", *u))
                for hf in range(2):
                    rwkv_half(g, i, d, hf)

            def rwkv_half(g, i, d, hf):
                u = (g, i, d, hf)
                claim(0, "TA", *u)
                claim(1, "TB", *u)
                for j in range(2):
                    f = (2 * hf + j) * 128
                    tp(PB[:, 0, 256 * j:256 * j + 128], tokm[:, 0, f:f + 128])
                    ins = tp(PB[:, 0, 256 * j + 128:256 * j + 256], tokm[:, 1, f:f + 128])
                ins.then_inc(*tick("pe", "tA", *u))
                for j in range(2):
                    f = (2 * hf + j) * 128
                    tp(PB[:, 1, 256 * j:256 * j + 128], tokm[:, 2, f:f + 128])
                    ins = tp(PB[:, 1, 256 * j + 128:256 * j + 256], tokm[:, 3, f:f + 128])
                ins.then_inc(*tick("pe", "tB", *u))
                pe.wait_ge(*when("TA", *u))
                pe.wait_ge(*when("TB", *u))
                for h in range(4):
                    j, r = h // 2, 64 * (h % 2)
                    claim(2 + h, "G4", *u)
                    for a in range(2):
                        ins = mm(PB[:, 2 + h, 256 * a:256 * a + 256], TB[r:r + 64, 2 * j + a, :],
                                 TA[r:r + 64, 2 * j:2 * j + 2, :])
                ins.then_inc(*tick("pe", "gram", *u))
                claim(6, "X0", *u)
                claim(7, "X0", *u)
                for h in range(4):
                    j, r = h // 2, 64 * (h % 2)
                    ins = mm(PB[:, 6 + h % 2, 128 * j:128 * j + 128], TA[r:r + 64, 2 * j, :], TB[r:r + 64, 2 * j, :])
                ins.then_inc(*tick("pe", "gramL", *u))
                for v in range(1, 6):
                    if v == 1:
                        pe.wait_ge(*when("XT0", *u))
                    else:
                        pe.wait_ge(*when("X", *u, v - 1))
                        pe.wait_ge(*when("XT", *u, v - 1))
                    pe.wait_ge(*when("LJ", *u, v))
                    claim(6, "T1", *u, v)
                    for h in range(4):
                        ins = mm(PB[:, 6, 128 * h:128 * h + 128], LJ4[:, h, :], X4[:, h, :])
                    ins.then_inc(*tick("pe", "t1", *u, v))
                    pe.wait_ge(*when("T1", *u, v))
                    if v < 5:
                        claim(7, "X", *u, v)
                        for h in range(4):
                            ins = mm(PB[:, 7, 128 * h:128 * h + 128], XT4[:, h, :], T14[:, h, :])
                        ins.then_inc(*tick("pe", "dx", *u, v))
                    claim(0, "XT", *u, v)
                    for h in range(4):
                        ins = mm(PB[:, 0, 128 * h:128 * h + 128], T14[:, h, :], XT4[:, h, :])
                    ins.then_inc(*tick("pe", "dxt", *u, v))
                pe.wait_ge(*when("XT", *u, 5))
                for n, c in enumerate((0, 1) if d == 0 else (1, 0)):
                    r = CH * c
                    if n:
                        pe.wait_ge(*when("S", *u, 0))
                    claim(1, "RH", *u, n)
                    for h in range(4):
                        V = E[:, i, EVB + (4 * hf + h) * 64:EVB + (4 * hf + h + 1) * 64]
                        mm(PB[r:r + CH, 1, 64 * h:64 * h + 64], G4[:, h, 256 + r:256 + r + CH], V, h == 0, False,
                           skip_group_check=True)
                    for j in range(2):
                        ins = mm(PB[r:r + CH, 1, 128 * j:128 * j + 128], TA[:, 2 * j, r:r + CH], SR[:, d, 2 * hf + j, :],
                                 False, j == 1, skip_group_check=True)
                    ins.then_inc(*tick("pe", "rh", *u, n))
                    claim(4, "Y", *u, n)
                    for h in range(4):
                        V = E[:, i, EVB + (4 * hf + h) * 64:EVB + (4 * hf + h + 1) * 64]
                        mm(PB[r:r + CH, 4, 64 * h:64 * h + 64], G4[:, h, 384 + r:384 + r + CH], V, h == 0, False,
                           skip_group_check=True)
                    for j in range(2):
                        mm(PB[r:r + CH, 4, 128 * j:128 * j + 128], TA[:, 2 * j + 1, r:r + CH], SR[:, d, 2 * hf + j, :],
                           False, False, skip_group_check=True)
                    pe.wait_ge(*when("RH", *u, n))
                    claim(2, "U", *u, n)
                    for h in range(4):
                        ins = mm(PB[r:r + CH, 2, 64 * h:64 * h + 64], XT4[:, h, r:r + CH], RH[:, 64 * h:64 * h + 64],
                                 skip_group_check=True)
                    ins.then_inc(*tick("pe", "uu", *u, n))
                    pe.wait_ge(*when("U", *u, n))
                    claim(6 + c, "S", *u, n)
                    for j in range(2):
                        f = (2 * hf + j) * 128
                        mm(PB[:, 6 + c, 128 * j:128 * j + 128], tokm[r:r + CH, 2, f:f + 128],
                           UU[r:r + CH, 128 * j:128 * j + 128], True, False, skip_group_check=True)
                        ins = mm(PB[:, 6 + c, 128 * j:128 * j + 128], tokm[r:r + CH, 3, f:f + 128],
                                 E[r:r + CH, i, EVB + f:EVB + f + 128], False, True, skip_group_check=True)
                    ins.then_inc(*tick("pe", "su", *u, n))
                    for h in range(4):
                        ins = mm(PB[r:r + CH, 4, 64 * h:64 * h + 64], G4[:, h, 128 + r:128 + r + CH],
                                 UU[:, 64 * h:64 * h + 64], False, h == 3, skip_group_check=True)
                    ins.then_inc(*tick("pe", "yy", *u, n))

            def states_T(name, src, wait):
                pe.wait_ge(*when(*wait)) if isinstance(wait, tuple) else pe.wait_ge(sem(wait), 16 * 16)
                for d in range(2):
                    claim(d, name, d)
                    for j in range(4):
                        ins = tp(PB[:, d, 128 * j:128 * j + 128], src(d, j))
                    ins.then_inc(*tick("pe", name + "_p", d))

            def even_out(g, i, t):
                pe.wait_ge(sem("ld_late"), 32 * (g + 1))
                claim(5, "omix", g, i)
                mm(PB[:, 5, :], loT[:, i, 2, :], g2w).then_inc(*tick("pe", "gm", g, i))
                mixed_T(("omix", g, i), lambda k: (oG if k < 4 else yR)[:, i, 128 * (k % 4):128 * (k % 4) + 128], t, 0)

            def mixed_T(name, src, t, l):
                pe.wait_ge(*when(*name))
                for b in range(2):
                    claim(6 + b, "mT", l, t, b)
                    for k in range(4):
                        ins = tp(PB[:, 6 + b, 128 * k:128 * k + 128], src(4 * b + k))
                    ins.then_inc(*tick("pe", "mixT", l, t, b))

            def router(l):
                pe.wait_ge(sem("ld_router"), 32)
                for t in range(TILES):
                    for b in range(2):
                        pe.wait_ge(*when("hT", l, 1, t, b))
                claim(0, "scores", l)
                for t in range(TILES):
                    for k in range(KD):
                        ins = mm(PB[:, 0, 16 * t:16 * t + 16], hTv[:, k, t * P:(t + 1) * P],
                                 wrout[:, 16 * k:16 * k + 16], k == 0, k == KD - 1)
                ins.then_inc(*tick("pe", "rt", l))

            def experts(l):
                for b in range(8):
                    if reader[b] is not None:
                        pe.wait_ge(*when(*reader[b]))
                    reader[b] = None
                pe.wait_ge(*when("gates", l))
                B = l * NE
                with pe.Fori(0, NE) as i:
                    pe.wait_ge(w_land[0], i * 16 + (moe_base[l][0] + 16))
                    pe.wait_ge(w_land[1], i * 16 + (moe_base[l][1] + 16))
                    for j in range(KF):
                        pe.wait_ge(hid_done, i * NJ + (B * NJ + j + CREDIT - 1))
                        for m in range(2):
                            for k in range(KD):
                                ins = mm(PB[:, 2 * m + j % 2, 0:NTOK], slot[m][:, k, 128 * j:128 * j + 128],
                                         hTv[:, k, :], k == 0, k == KD - 1)
                        ins.then_inc(gu_done, 1)
                    pe.wait_ge(w_land[2], i * 16 + (moe_base[l][2] + 16))
                    pe.wait_ge(hid_done, i * NJ + (B * NJ + NJ + CREDIT))
                    for n in range(ND):
                        t, c = n // 2, n % 2
                        pe.wait_ge(acc_done, i * ND + (B * ND + n + 1))
                        for j in range(KF):
                            ins = mm(PB[:, 4 + n % 2, :], hid[:, 0, j, t * P:(t + 1) * P],
                                     slot_dn[2][:, j, 512 * c:512 * c + 512], j == 0, j == KF - 1)
                        ins.then_inc(dn_done, 1)
                pe.wait_ge(acc_done, (B + NE) * ND + 2)
                pe.wait_ge(hid_done, (B + NE) * NJ + CREDIT)

            def odd_keys_queries():
                for t in range(TILES):
                    pe.wait_ge(*when("ocn", t))
                    claim(0, "cqT", t)
                    for k in range(2):
                        tp(PB[:, 0, 128 * k:128 * k + 128], O[:, t, OCQ + 128 * k:OCQ + 128 * k + 128])
                    ins = tp(PB[:, 0, 256:384], O[:, t, OCKV:OCKV + 128])
                    ins.then_inc(*tick("pe", "cT", t))
                pe.wait_ge(sem("ld_odd"), 17 * 16)
                claim(1, "cqT", 3)
                tp(PB[:, 1, 0:128], cckv).then_inc(*tick("pe", "cT", 3))
                for t in range(TILES):
                    pe.wait_ge(*when("cqT", t))
                    for b in range(2):
                        claim(2 + b, "q_raw", t)
                        for k in range(2):
                            ins = mm(PB[:, 2 + b, 0:384], cqT[:, k, t * P:(t + 1) * P], qup[:, k, 384 * b:384 * b + 384],
                                     k == 0, k == 1)
                    ins.then_inc(*tick("pe", "q_up", t))
                    heads_T(("q_n", t), hd, "qT", t)
                for kt in range(4):
                    pe.wait_ge(*when("cqT", [0, 3, 1, 2][kt]))
                    for b in range(2):
                        claim(2 + b, "k_raw", kt)
                        ins = mm(PB[:, 2 + b, :], ckT[:, kt, :], kvup[:, 512 * b:512 * b + 512])
                    ins.then_inc(*tick("pe", "kv_up", kt))
                    heads_T(("k_n", kt), hd, "kT", kt)
                for t in range(TILES):
                    pe.wait_ge(*when("dqk", t))
                    pairs_T("dqT", t, lambda h: O[:, t, OQD + 128 * h:OQD + 128 * h + 128])
                    pairs_T("dkT", [0, 2, 3][t], lambda h: O[:, t, OKD + 128 * h:OKD + 128 * h + 128])
                pairs_T("dkT", 1, lambda h: cdk[:, 2 * h:2 * h + 2, :].rearrange("p m n -> p (m n)"))

            def heads_T(name, src, out, t):
                pe.wait_ge(*when(*name))
                for b in range(2):
                    claim(4 + b, out, t, b)
                    for h in range(4):
                        ins = tp(PB[0:96, 4 + b, 128 * h:128 * h + 128], src[:, 96 * (4 * b + h):96 * (4 * b + h) + 96])
                    ins.then_inc(*tick("pe", out + "_p", t, b))

            def pairs_T(out, t, src):
                b = 6 if out == "dqT" else 7
                claim(b, out, t)
                for h in range(4):
                    ins = tp(PB[:, b, 128 * h:128 * h + 128], src(h))
                ins.then_inc(*tick("pe", out + "_p", t))

            def attend():
                units = [(t, m) for t in range(TILES) for m in range(16)]

                def operands(u):
                    t, m = units[u]
                    ks = [0] if t == 0 else [1, 2, 3]
                    if m < 8:
                        q, kk = hTv[0:96, m, t * P:(t + 1) * P], kT[0:96, m, 128 * ks[0]:128 * ks[0] + 128 * len(ks)]
                        vs = [vC[:, k, m, :] for k in ks]
                    else:
                        h, r = (m - 8) // 2, 64 * (m % 2)
                        q = dqT[r:r + 64, h, t * P:(t + 1) * P]
                        kk = dkT[r:r + 64, h, 128 * ks[0]:128 * ks[0] + 128 * len(ks)]
                        vt = [O[:, 0, OVD:ODD], cdv.rearrange("p h n -> p (h n)"), O[:, 1, OVD:ODD], O[:, 2, OVD:ODD]]
                        vs = [vt[k][:, 128 * h:128 * h + 128] for k in ks]
                    return q, kk, vs, len(ks)

                def scores(u):
                    q, kk, vs, n = operands(u)
                    claim(u % 2, "prob", u)
                    mm(PB[:, u % 2, 0:128 * n], q, kk).then_inc(*tick("pe", "sc", u))

                def turn(u):
                    n = operands(u)[3]
                    pe.wait_ge(*when("prob", u))
                    claim(2 + u % 2, "probT", u)
                    for k in range(n):
                        ins = tp(PB[:, 2 + u % 2, 128 * k:128 * k + 128], prob[:, u % 2, 128 * k:128 * k + 128])
                    ins.then_inc(*tick("pe", "pT", u))

                def values(u):
                    vs = operands(u)[2]
                    pe.wait_ge(*when("probT", u))
                    claim(4 + u % 2, "ov", u)
                    w = 64 if units[u][1] < 8 else 128
                    for k, v in enumerate(vs):
                        ins = mm(PB[:, 4 + u % 2, 0:w], probT[:, u % 2, k, :], v, k == 0, k == len(vs) - 1)
                    ins.then_inc(*tick("pe", "pv", u))

                for s in ("act", "dve"):
                    pe.wait_ge(*when("end", s, "odd_prep"))
                scores(0)
                for u in range(48):
                    if u + 1 < 48:
                        scores(u + 1)
                    turn(u)
                    if u % 16:
                        values(u - 1)
                    if u % 16 == 15:
                        values(u)
                        t = u // 16
                        mixed_T(("omix1", t), lambda k: mix[:, 128 * k:128 * k + 128], t, 1)

            pe.wait_ge(sem("ld_const"), 32)
            pe.wait_ge(*when("scT"))
            mods(0)
            norm(0, 0)
            for g, tiles in enumerate(((0,), (1, 2))):
                for t in tiles:
                    for b in range(2):
                        pe.wait_ge(*when("hT", 0, 0, t, b))
                project(("ein", g), tiles, 7, EVEN)
                if g == 0:
                    pe.wait_ge(sem("ld_even"), 16 * 5)
                    pe.wait_ge(*when("SG0"))
                    pe.wait_ge(*when("SR0"))
                else:
                    pe.wait_ge(sem("ld_sg"), 8 * 16)
                    pe.wait_ge(*when("SG1"))
                    states_T("state_in", lambda d, j: stg[:, d, 128 * j:128 * j + 128], "ld_sr")
                    pe.wait_ge(*when("state_in", 1))
                for i in range(len(tiles)):
                    lora_T(g, i)
                for i, d in (((0, 0), (0, 1)), ((0, 0), (1, 0), (1, 1), (0, 1)))[g]:
                    gla(g, i, d)
                    rwkv(g, i, d)
                end("pe", f"units{g}")
                if g == 0:
                    states_T("state_out", lambda d, j: SR[:, d, j, :], ("S", 0, 0, 1, 1, 1))
                for i, t in enumerate(tiles):
                    even_out(g, i, t)
                end("pe", f"out_g{g}")
            for l in range(2):
                if l == 1:
                    mods(1)
                    norm(1, 0)
                    for t in range(TILES):
                        for b in range(2):
                            pe.wait_ge(*when("hT", 1, 0, t, b))
                    project(("oin",), (0, 1, 2), 4, ODD)
                    odd_keys_queries()
                    end("pe", "odd_prep")
                    attend()
                for t in range(TILES):
                    for b in range(2):
                        pe.wait_ge(*when("mT", l, t, b))
                project(("outp", l), (0, 1, 2), 2, D)
                end("pe", f"mixer{l}")
                norm(l, 1)
                router(l)
                experts(l)
                end("pe", f"moe{l}")

        @block.scalar
        def _(act):
            def step(ins, *name):
                ins.then_inc(*tick("act", *name))
                act.wait_ge(sem("act"), count["act"])

            def fn(out, in_, f, *name, **k):
                step(nc.scalar.activation(out, in_, f, **k), *name)

            def mods(l):
                for n in range(12):
                    act.wait_ge(*when("modp", l, n))
                    if n >= 2:
                        act.wait_ge(*(when("gb", l, n - 2, 1) if (n - 2) // 2 in (2, 5) else when("mt", l, n - 2)))
                    fn(rowb[0:2, 512 * (n % 2):512 * (n % 2) + 512], PB[0:2, n % 2, :], ACT.Copy, "modrow", l, n)
                end("act", f"mods{l}")

            def root(*name):
                act.wait_ge(*when("var", *name))
                n = known_n[name[0]]
                fn(small[:, 0:n], small[:, 0:n], ACT.Sqrt, "root", *name)

            def copies(name, tiles, chunks, width, dst):
                bank = 0
                for n in range(chunks):
                    ncol = min(512, width - 512 * n)
                    for i in range(len(tiles)):
                        if bank % 2 == 0:
                            act.wait_ge(*when(*name, "p", n, i))
                            fn(dst[:, i, 512 * n:512 * n + ncol], PB[:, bank % 4, 0:ncol], ACT.Copy, *name, "evac", n, i)
                        bank += 1

            def norm(l, s):
                for t in range(TILES):
                    if t:
                        act.wait_ge(*when("xnT", l, s, t - 1, 1))
                    act.wait_ge(*when("norm_in", l, s, t))
                    fn(xn, xv[:, t, :], ACT.Square, "sq", l, s, t, accum_out=small[:, 0:1])
                    root("norm", l, s, t)

            def gla(g, i, d):
                u = (g, i, d)
                la, t1 = tmpE[0][:, 0:256], tmpE[1][:, 0:256]
                act.wait_ge(*when("ga_z", *u))
                fn(t1, la, ACT.Abs)
                fn(t1, t1, ACT.Exp, scale=-1.0)
                fn(t1, t1, ACT.Ln, "ln", *u, bias=1.0)
                act.wait_ge(*when("gcum", *u))
                s = 1.0 / 16
                fn(tmpE[1][:, 0:256], PB[:, 1, 0:256], ACT.Exp, scale=s)
                fn(tmpE[1][:, 256:512], PB[:, 1, 0:256], ACT.Exp, scale=-s)
                fn(tmpE[2][:, 0:256], PB[:, 1, 256:512], ACT.Exp, "g_exp", *u, scale=s)
                fn(small[:, 16:20], PB[:, 2, 0:4], ACT.Exp, "g_dec", *u, scale=s)
                act.wait_ge(*when("gT", *u))
                fn(TA.rearrange("p a n -> p (a n)"), PB[:, 3, :], ACT.Copy, "gqkT", *u)

            def rwkv(g, i, d):
                u = (g, i, d)
                act.wait_ge(*when("r_zw", *u))
                fn(tmpE[0], tmpE[0], ACT.Sigmoid, "lw", *u)
                act.wait_ge(*when("r_za", *u))
                fn(tmpE[1], tmpE[1], ACT.Sigmoid, "aa", *u)
                act.wait_ge(*when("rcum", *u))
                fn(tokm[:, 0, :], PB[:, 5, :], ACT.Exp, "e_exc", *u, scale=-RW)
                fn(tokm[:, 1, :], PB[:, 4, :], ACT.Exp, scale=-RW)
                fn(tmpE[2], PB[:, 4, :], ACT.Exp, "e_inc", *u, scale=RW)
                fn(small[:, 32:40], PB[:, 6, 0:8], ACT.Exp, "e_wc", *u, scale=-RW)
                for hf in range(2):
                    w = (g, i, d, hf)
                    act.wait_ge(*when("tA", *w))
                    if hf:
                        act.wait_ge(*when("yy", g, i, d, 0, 1))
                    fn(TA.rearrange("p a n -> p (a n)"), PB[:, 0, :], ACT.Copy, "TA", *w)
                    for v in range(1, 6):
                        act.wait_ge(*when("t1", *w, v))
                        fn(T14.rearrange("p h n -> p (h n)"), PB[:, 6, :], ACT.Copy, "T1", *w, v)
                    for n in range(2):
                        act.wait_ge(*when("uu", *w, n))
                        r = CH * ((n, 1 - n)[d])
                        fn(UU[r:r + CH, :], PB[r:r + CH, 2, 0:256], ACT.Copy, "U", *w, n)

            known_n = {"norm": 1, "kk": 8, "og": 4, "oy": 8, "cq": 1, "ckv": 1, "qh": 8, "kh": 8, "dq": 8, "dk": 8, "dd": 4}

            def even_out(g, i):
                act.wait_ge(*when("end", "dve", f"units{g}"))
                fn(E[:, i, EG:EG + 512], E[:, i, EG:EG + 512], ACT.Silu, "siluG", g, i)
                root("og", g, i)
                root("oy", g, i)

            def experts(l):
                B = l * NE
                with act.Fori(0, NE) as i:
                    for j in range(KF):
                        act.wait_ge(gu_done, i * NJ + (B * NJ + j + 2))
                        act.wait_ge(hid_done, i * NJ + (B * NJ + j + CREDIT - 3))
                        nc.scalar.activation(sil[:, j, :], PB[:, j % 2, 0:NTOK], ACT.Silu).then_inc(silu_done, 1)

            act.wait_ge(sem("ld_const"), 32)
            fn(scT[:, :], cols[:, COL_C:COL_C + 16], ACT.Silu, "scT")
            mods(0)
            norm(0, 0)
            for g, tiles in enumerate(((0,), (1, 2))):
                if g:
                    meet(act, "act", "out_g0")
                copies(("ein", g), tiles, 7, EVEN, E)
                for i in range(len(tiles)):
                    act.wait_ge(*when("e_ready", g, i))
                    fn(E[:, i, EWL:EWL + 128], E[:, i, EWL:EWL + 128], ACT.Tanh)
                    fn(E[:, i, EGL:EGL + 128], E[:, i, EGL:EGL + 128], ACT.Sigmoid, "lora", g, i)
                    root("kk", g, i)
                for i, d in (((0, 0), (0, 1)), ((0, 0), (1, 0), (1, 1), (0, 1)))[g]:
                    gla(g, i, d)
                    rwkv(g, i, d)
                end("act", f"units{g}")
                for i in range(len(tiles)):
                    even_out(g, i)
                end("act", f"out_g{g}")
            for l in range(2):
                if l == 1:
                    mods(1)
                    norm(1, 0)
                    copies(("oin",), (0, 1, 2), 4, ODD, O)
                    act.wait_ge(*when("lamsum"))
                    fn(small[:, 60:62], small[:, 60:62], ACT.Exp, "lamexp")
                    for t in range(TILES):
                        root("cq", t)
                        root("ckv", t)
                    for t in range(TILES):
                        root("qh", t)
                    for kt in range(4):
                        root("kh", kt)
                    for t in range(TILES):
                        root("dq", t)
                        root("dk", t)
                    end("act", "odd_prep")
                    for u in range(48):
                        m = u % 16
                        n = 128 if u < 16 else 384
                        act.wait_ge(*when("nmax", u))
                        if u >= 2:
                            act.wait_ge(*when("pT", u - 2))
                            act.wait_ge(*when("ov", u - 2))
                        scale = (96 if m < 8 else 64) ** -0.5
                        fn(prob[:, u % 2, 0:n], PB[:, u % 2, 0:n], ACT.Exp, "prob", u,
                           bias=small[:, 64 + u % 2:65 + u % 2], scale=scale, accum_out=small[:, 66 + u % 2:67 + u % 2])
                        if m == 15:
                            root("dd", u // 16)
                end("act", f"mixer{l}")
                norm(l, 1)
                act.wait_ge(*when("rt", l))
                fn(small[:, 128:176], PB[:, 0, 0:48], ACT.Sigmoid, "scores", l)
                act.wait_ge(*when("gates", l))
                experts(l)
                end("act", f"moe{l}")

        @block.vector
        def _(dve):
            V = nc.vector

            def step(ins, *name):
                ins.then_inc(*tick("dve", *name))
                dve.wait_ge(sem("dve"), count["dve"])

            def tt(out, a, b, op, *name):
                step(V.tensor_tensor(out, a, b, op), *name)

            def ts(out, a, s1, s2, op0, op1, *name):
                step(V.tensor_scalar(out, a, s1, s2, op0, op1) if op1 is not None else
                     V.tensor_scalar(out, a, s1, None, op0), *name)

            def stt(out, a, s, b, op0, op1, *name):
                step(V.scalar_tensor_tensor(out=out, in0=a, scalar=s, in1=b, op0=op0, op1=op1), *name)

            def cp(out, a, *name):
                step(V.tensor_copy(out, a), *name)

            def red(out, a, *name, op=ALU.add):
                step(V.tensor_reduce(out, a, AX.X, op), *name)

            def rstd(n, scale, eps, *name):
                ts(small[:, 0:n], small[:, 0:n], scale, eps, ALU.mult, ALU.add, "var", *name)
                dve.wait_ge(*when("root", *name))
                step(V.reciprocal(small[:, 0:n], small[:, 0:n]))
                return small[:, 0:n]

            def mods(l):
                dve.wait_ge(sem("ld_bgate"), 16 * 4 * (l + 1))
                for n in range(12):
                    kind, half = n // 2, n % 2
                    if kind in (2, 5):
                        for c in range(2):
                            dve.wait_ge(*when("gb", l, n, c))
                            gv = gatev[:, c, kind // 3, 512 * half:512 * half + 512]
                            tt(gv, gv, PB[:, 2 + c, :], ALU.add, "gadd", l, n, c)
                    else:
                        dve.wait_ge(*when("mt", l, n))
                        tt(modTv[:, 4 * n:4 * n + 4, :], PB[:, 4 + n % 2, 0:8].rearrange("p (j c) -> p j c", c=2),
                           bc(cols[:, COL_BM + 48 * l + 4 * n:COL_BM + 48 * l + 4 * n + 4], 2, 2), ALU.add, "modT", l, n)
                for s in range(2):
                    sc = modTv[:, 24 * s + 8:24 * s + 16, :]
                    ng = bc(cols[:, COL_NG + 8 * (2 * l + s):COL_NG + 8 * (2 * l + s) + 8], 2, 2)
                    stt(mulAv[:, s, :, :], sc, 1.0, ng, ALU.add, ALU.mult)
                end("dve", f"mods{l}")

            def norm(l, s):
                for t in range(TILES):
                    ts(small[:, 1:2], cols[:, 0:1], 0.0, None, ALU.mult, None, "norm_in", l, s, t)
                    dve.wait_ge(*when("sq", l, s, t))
                    r = rstd(1, 1.0 / D, EPS, "norm", l, s, t)
                    ts(xn, xv[:, t, :], r, None, ALU.mult, None, "xn", l, s, t)
                    cond = 0 if t == 0 else 1
                    for b in range(2):
                        dve.wait_ge(*when("xnT", l, s, t, b))
                        for k in range(4):
                            kk = 4 * b + k
                            ts(hTv[:, kk, t * P:(t + 1) * P], PB[:, 6 + b, 128 * k:128 * k + 128],
                               mulAv[:, s, kk, cond:cond + 1], modTv[:, 24 * s + kk, cond:cond + 1],
                               ALU.mult, ALU.add, *(("hT", l, s, t, b) if k == 3 else ()))

            def copies(name, tiles, chunks, width, dst):
                bank = 0
                for n in range(chunks):
                    ncol = min(512, width - 512 * n)
                    for i in range(len(tiles)):
                        if bank % 2:
                            dve.wait_ge(*when(*name, "p", n, i))
                            cp(dst[:, i, 512 * n:512 * n + ncol], PB[:, bank % 4, 0:ncol], *name, "evac", n, i)
                        bank += 1

            def h8(ap, h=8):
                return ap.rearrange("p (h n) -> p h n", h=h)

            def prepare(g, i):
                tmp = tmpE[0]
                dve.wait_ge(*when("lora_T", g, i))
                for j, n in ((0, 128), (1, 128), (2, 128), (3, 32)):
                    cp(loT[0:n, i, j, :], PB[0:n, 0, 128 * j:128 * j + 128], *(("loT", g, i) if j == 3 else ()))
                kk = kkn[:, i, :]
                kb, rr = E[:, i, EKB:EKB + 512], E[:, i, ER:ER + 512]
                tt(kk, kb, R(rowsE, "rw_kk"), ALU.mult)
                tt(tmp, kk, kk, ALU.mult)
                red(small[:, 0:8], h8(tmp))
                r = rstd(8, 1.0, EPS, "kk", g, i)
                tt(h8(kk), h8(kk), bc(r, 2, 64), ALU.mult)
                tt(tmp, rr, kb, ALU.mult)
                tt(tmp, tmp, R(rowsE, "rw_rk"), ALU.mult)
                red(bon[:, i, :], h8(tmp))

            def gla(g, i, d, first):
                u = (g, i, d)
                la, t1 = tmpE[0][:, 0:256], tmpE[1][:, 0:256]
                q, k = E[:, i, EQ:EQ + 256], E[:, i, EK_:EK_ + 256]
                dve.wait_ge(*when("za", *u))
                tt(la, PB[:, 0, 0:256], R(rowsE, "gla_a_b", 256 * d, 256), ALU.add, "ga_z", *u)
                dve.wait_ge(*when("ln", *u))
                stt(la, la, 0.0, t1, ALU.min, ALU.subtract, "la", *u)
                dve.wait_ge(*when("g_exp", *u))
                stt(tokm[:, 0, 0:256], q, 64 ** -0.5, tmpE[1][:, 0:256], ALU.mult, ALU.mult)
                tt(tokm[:, 1, 0:256], k, tmpE[1][:, 256:512], ALU.mult)
                tt(tokm[:, 2, 0:256], k, tmpE[2][:, 0:256], ALU.mult, "gk", *u)
                dve.wait_ge(*when("g_dec", *u))
                dve.wait_ge(*when("gA", *u))
                m = C("le") if d == 0 else C("ge")
                for b in range(2):
                    tt(G4[:, b:4:2, 0:128], PB[:, 4 + b, 0:256].rearrange("p (j n) -> p j n", j=2), bc(m, 1, 2),
                       ALU.mult, *(("gatt", *u) if b else ()))
                for n, c in enumerate((0, 1) if d == 0 else (1, 0)):
                    dve.wait_ge(*when("gu", *u, n))
                    tt(tmpE[1].rearrange("p (j n) -> p j n", j=2), PB[:, 7, :].rearrange("p (j n) -> p j n", j=2),
                       bc(C("bdg"), 1, 2), ALU.mult)
                    for j in range(2):
                        stt(SG[:, d, j, :], SG[:, d, j, :], small[:, 16 + 2 * j + c:17 + 2 * j + c],
                            tmpE[1][:, 256 * j:256 * j + 256], ALU.mult, ALU.add, *(("gS", *u, n) if j else ()))
                if first:
                    cp(oG[:, i, :], PB[:, 6, :], "gout", *u)
                else:
                    tt(oG[:, i, :], oG[:, i, :], PB[:, 6, :], ALU.add, "gout", *u)

            def rwkv(g, i, d, first):
                u = (g, i, d)
                kb, rr = E[:, i, EKB:EKB + 512], E[:, i, ER:ER + 512]
                dve.wait_ge(*when("zw", *u))
                tt(tmpE[0], PB[:, d, :], R(rowsE, "rw_w0", 512 * d, 512), ALU.add, "r_zw", *u)
                dve.wait_ge(*when("zr", *u))
                tt(tmpE[1], PB[:, 2 + d, :], R(rowsE, "rw_a0", 512 * d, 512), ALU.add, "r_za", *u)
                dve.wait_ge(*when("e_wc", *u))
                tt(tokm[:, 0, :], tokm[:, 0, :], kkn[:, i, :], ALU.mult)
                tt(tokm[:, 1, :], tokm[:, 1, :], rr, ALU.mult)
                tt(tokm[:, 2, :], tmpE[1], kkn[:, i, :], ALU.mult)
                tt(tokm[:, 2, :], tokm[:, 2, :], tmpE[2], ALU.mult)
                stt(tokm[:, 3, :], tmpE[1], -1.0, R(rowsE, "rw_ka"), ALU.add, ALU.mult)
                stt(tokm[:, 3, :], tokm[:, 3, :], 1.0, kb, ALU.add, ALU.mult)
                tt(tokm[:, 3, :], tokm[:, 3, :], tmpE[2], ALU.mult, "tokm", *u)
                strict = cst[:, _C["lt" if d == 0 else "gt"][0]:_C["lt" if d == 0 else "gt"][0] + 256]
                lvl, lvl_t = (C("lvl0"), C("lvl1")) if d == 0 else (C("lvl1"), C("lvl0"))
                I4 = bc(ident, 1, 4)
                for hf in range(2):
                    w = (g, i, d, hf)
                    dve.wait_ge(*when("tB", *w))
                    cp(TB.rearrange("p a n -> p (a n)"), PB[:, 1, :], "TB", *w)
                    dve.wait_ge(*when("gramL", *w))
                    tt(G4.rearrange("p h (a n) -> p (h a) n", a=2), PB[:, 2:6, :].rearrange("p h (a n) -> p (h a) n", a=2),
                       bc(strict, 1, 8), ALU.mult, "G4", *w)
                    for b in range(2):
                        tt(T14[:, b:4:2, :], PB[:, 6 + b, 0:256].rearrange("p (j n) -> p j n", j=2),
                           bc(lvl_t[:, 0:128], 1, 2), ALU.mult, *(("X0", *w) if b else ()))
                    tt(X4, I4, T14, ALU.subtract)
                    tt(T14, G4[:, :, 0:128], bc(lvl[:, 0:128], 1, 4), ALU.mult)
                    tt(XT4, I4, T14, ALU.subtract, "XT0", *w)
                    for v in range(1, 6):
                        if v == 1:
                            tt(LJ4, G4[:, :, 0:128], bc(lvl[:, 128:256], 1, 4), ALU.mult, "LJ", *w, 1)
                        if v < 5:
                            dve.wait_ge(*when("t1", *w, v))
                            tt(LJ4, G4[:, :, 0:128], bc(lvl[:, 128 * v + 128:128 * v + 256], 1, 4),
                               ALU.mult, "LJ", *w, v + 1)
                            dve.wait_ge(*when("dx", *w, v))
                            tt(X4, X4, PB[:, 7, :].rearrange("p (h n) -> p h n", h=4), ALU.subtract, "X", *w, v)
                        dve.wait_ge(*when("dxt", *w, v))
                        tt(XT4, XT4, PB[:, 0, :].rearrange("p (h n) -> p h n", h=4), ALU.subtract, "XT", *w, v)
                    for n in range(2):
                        c = (n, 1 - n)[d]
                        r = CH * c
                        dve.wait_ge(*when("rh", *w, n))
                        ts(RH[r:r + CH, :], PB[r:r + CH, 1, 0:256], -1.0, None, ALU.mult, None, "RH", *w, n)
                        dve.wait_ge(*when("su", *w, n))
                        s2 = SR[:, d, 2 * hf:2 * hf + 2, :]
                        dve.wait_ge(*when("yy", *w, n))
                        tt(s2, s2, PB[:, 6 + c, 0:256].rearrange("p (j n) -> p j n", j=2), ALU.add)
                        tt(s2, s2, bc(small[:, 32 + 4 * hf + c:32 + 4 * hf + c + 3:2], 2, 128), ALU.mult)
                        tt(s2, s2, bc(C("bdr"), 1, 2), ALU.mult, "S", *w, n)
                        yo = yR[r:r + CH, i, 256 * hf:256 * hf + 256]
                        if first:
                            cp(yo, PB[r:r + CH, 4, 0:256], "Y", *w, n)
                        else:
                            tt(yo, yo, PB[r:r + CH, 4, 0:256], ALU.add, "Y", *w, n)

            def even_out(g, i):
                dve.wait_ge(sem("ld_late"), 32 * (g + 1))
                o, y, tmp = oG[:, i, :], yR[:, i, :], tmpE[0]
                tt(tmp, o, o, ALU.mult)
                red(small[:, 0:4], h8(tmp, 4))
                r = rstd(4, 1.0 / 128, EPS, "og", g, i)
                tt(h8(o, 4), h8(o, 4), bc(r, 2, 128), ALU.mult)
                tt(h8(o, 4), h8(o, 4), bc(R(rowsG, "gla_o_g"), 1, 4), ALU.mult)
                dve.wait_ge(*when("siluG", g, i))
                tt(o, o, E[:, i, EG:EG + 512], ALU.mult)
                red(small[:, 8:16], h8(y))
                ts(small[:, 8:16], small[:, 8:16], 1.0 / 64, None, ALU.mult, None)
                tt(h8(y), h8(y), bc(small[:, 8:16], 2, 64), ALU.subtract)
                tt(tmp, y, y, ALU.mult)
                red(small[:, 0:8], h8(tmp))
                r = rstd(8, 1.0 / 64, GN_EPS, "oy", g, i)
                tt(h8(y), h8(y), bc(r, 2, 64), ALU.mult)
                tt(y, y, R(rowsG, "rw_gn_g"), ALU.mult)
                tt(y, y, R(rowsG, "rw_gn_b"), ALU.add)
                tt(h8(tmp), h8(E[:, i, EVB:EVB + 512]), bc(bon[:, i, :], 2, 64), ALU.mult)
                tt(y, y, tmp, ALU.add)
                dve.wait_ge(*when("gm", g, i))
                tt(y, y, PB[:, 5, :], ALU.mult, "omix", g, i)

            def mixed(l, t):
                for b in range(2):
                    dve.wait_ge(*when("mixT", l, t, b))
                    cp(hTv[:, 4 * b:4 * b + 4, t * P:(t + 1) * P], PB[:, 6 + b, :].rearrange("p (k n) -> p k n", k=4),
                       "mT", l, t, b)

            def residual(l):
                bank = 0
                for n in range(2):
                    for t in range(TILES):
                        dve.wait_ge(*when("outp", l, "p", n, t))
                        gv = gatev[:, 0 if t == 0 else 1, 0, 512 * n:512 * n + 512]
                        tmp = xn[:, 0:512]
                        tt(tmp, PB[:, bank % 4, :], gv, ALU.mult, "outp", l, "evac", n, t)
                        xs = xv[:, t, 512 * n:512 * n + 512]
                        tt(xs, xs, tmp, ALU.add)
                        bank += 1

            def route(l):
                dve.wait_ge(sem("ld_router"), 32)
                dve.wait_ge(*when("scores", l))
                s, sel, rank, keep = (arena[:, 64 * n:64 * n + 16] for n in range(4))
                gsc, grank = arena[:, 256:260], arena[:, 264:268]
                c1, c2 = arena[:, 320:384], arena[:, 384:448]
                tie = C("tie")
                tie44 = tie.rearrange("p (e j) -> p e j", e=4)
                for t in range(TILES):
                    s = small[:, 128 + 16 * t:144 + 16 * t]
                    tt(sel, s, brout[:, :], ALU.add)
                    for gi in range(4):
                        a = sel[:, 4 * gi:4 * gi + 4]
                        o1 = c1[:, 16 * gi:16 * gi + 16].rearrange("p (e j) -> p e j", e=4)
                        o2 = c2[:, 16 * gi:16 * gi + 16].rearrange("p (e j) -> p e j", e=4)
                        tt(o1, bc(a, 1, 4), bc(a, 2, 4), ALU.is_gt)
                        tt(o2, bc(a, 1, 4), bc(a, 2, 4), ALU.is_equal)
                        tt(o2, o2, tie44, ALU.mult)
                        tt(o1, o1, o2, ALU.add)
                    red(rank, c1.rearrange("p (e j) -> p e j", j=4))
                    ts(keep, rank, 1.5, None, ALU.is_lt, None)
                    tt(c1[:, 0:16], sel, keep, ALU.mult)
                    red(gsc, c1[:, 0:16].rearrange("p (g e) -> p g e", g=4))
                    o1 = c1[:, 0:16].rearrange("p (e j) -> p e j", e=4)
                    o2 = c2[:, 0:16].rearrange("p (e j) -> p e j", e=4)
                    tt(o1, bc(gsc, 1, 4), bc(gsc, 2, 4), ALU.is_gt)
                    tt(o2, bc(gsc, 1, 4), bc(gsc, 2, 4), ALU.is_equal)
                    tt(o2, o2, tie44, ALU.mult)
                    tt(o1, o1, o2, ALU.add)
                    red(grank, o1)
                    ts(grank, grank, 0.5, None, ALU.is_lt, None)
                    tt(h8(keep, 4), h8(keep, 4), bc(grank, 2, 4), ALU.mult)
                    tt(keep, keep, s, ALU.mult)
                    red(small[:, 0:1], keep)
                    step(V.reciprocal(small[:, 0:1], small[:, 0:1]))
                    ts(gates[:, 16 * t:16 * t + 16], keep, small[:, 0:1], None, ALU.mult, None)
                step(V.memset(acc, 0.0))
                cp(small[:, 2:3], small[:, 0:1], "gates", l)

            def experts(l):
                B = l * NE
                with dve.Fori(0, NE) as i:
                    V.tensor_copy(gcur, gates[:, bass.ds(i, TILES, step=NE)]).then_inc(sem("gcur"), 1)
                    for j in range(KF):
                        dve.wait_ge(silu_done, i * NJ + (B * NJ + j + 1))
                        if j == 0:
                            dve.wait_ge(dn_done, i * ND + (B * ND + 1))
                        V.tensor_tensor(hid[:, 0, j, :], sil[:, j, :], PB[:, 2 + j % 2, 0:NTOK], ALU.mult)\
                            .then_inc(hid_done, 1)
                    dve.wait_ge(sem("gcur"), i + (B + 1))
                    for n in range(ND):
                        t, c = n // 2, n % 2
                        dve.wait_ge(dn_done, i * ND + (B * ND + n + 2))
                        a = acc[:, t, 512 * c:512 * c + 512]
                        V.scalar_tensor_tensor(out=a, in0=PB[:, 4 + n % 2, :], scalar=gcur[:, t:t + 1], in1=a,
                                               op0=ALU.mult, op1=ALU.add).then_inc(acc_done, 1)
                    dve.wait_ge(acc_done, i * ND + (B * ND + ND + 2))
                dve.wait_ge(acc_done, (B + NE) * ND + 2)
                for t in range(TILES):
                    tt(acc[:, t, :], acc[:, t, :], gatev[:, 0 if t == 0 else 1, 1, :], ALU.mult)
                    tt(xv[:, t, :], xv[:, t, :], acc[:, t, :], ALU.add, "x_moe", l, t)

            def rope(v, t, kind, nh, tmp):
                w = 32 if kind == "c" else 64
                q = w // 4
                cos = bc(C("cos" + kind, w * (t - 1), w), 1, nh)
                sin = C("sin" + kind, w * (t - 1), w).rearrange("p (a b q) -> p a b q", a=2, b=2)
                for a in range(2):
                    for b in range(2):
                        o = a * 2 * q + b * q
                        src = a * 2 * q + (1 - b) * q
                        tt(tmp[:, :, o:o + q], v[:, :, src:src + q], bc(sin[:, a, b, :], 1, nh), ALU.mult)
                tt(v, v, cos, ALU.mult)
                tt(v, v, tmp, ALU.add)

            def head_norm(v, tmp, nh, width, gain, *name):
                tt(tmp, v, v, ALU.mult)
                red(small[:, 0:nh], tmp)
                r = rstd(nh, 1.0 / width, EPS, *name)
                tt(v, v, bc(r, 2, width), ALU.mult)
                tt(v, v, bc(gain, 1, nh), ALU.mult)

            def odd_prepare():
                dve.wait_ge(sem("ld_odd"), 17 * 16)
                lam = R(rowsO, "diff_lam").rearrange("p (a b n) -> p a b n", a=2, b=2)
                lt_ = hd[:, 0:128].rearrange("p (a n) -> p a n", a=2)
                tt(lt_, lam[:, :, 0, :], lam[:, :, 1, :], ALU.mult)
                red(small[:, 60:62], lt_, "lamsum")
                dve.wait_ge(*when("lamexp"))
                tt(small[:, 62:63], small[:, 61:62], small[:, 60:61], ALU.subtract)
                ts(small[:, 62:63], small[:, 62:63], -LAM_INIT, None, ALU.add, None)
                for t in range(TILES):
                    for c0, w, gn, nm in ((OCQ, 256, "mla_qa_g", "cq"), (OCKV, 128, "mla_kva_g", "ckv")):
                        v = O[:, t, c0:c0 + w]
                        tt(hd[:, 0:w], v, v, ALU.mult)
                        red(small[:, 0:1], hd[:, 0:w])
                        r = rstd(1, 1.0 / w, EPS, nm, t)
                        stt(v, v, r, R(rowsO, gn), ALU.mult, ALU.mult, *(("ocn", t) if nm == "ckv" else ()))
                for t in range(4):
                    dve.wait_ge(*when("cT", t))
                    if t < 3:
                        cp(cqT[:, :, t * P:(t + 1) * P], PB[:, 0, 0:256].rearrange("p (k n) -> p k n", k=2))
                        cp(ckT[:, [0, 2, 3][t], :], PB[:, 0, 256:384], "cqT", t)
                    else:
                        cp(ckT[:, 1, :], PB[:, 1, 0:128], "cqT", 3)
                hv, hv2 = h8(hd), h8(hd2)
                for t in range(TILES):
                    dve.wait_ge(*when("q_up", t))
                    if t:
                        dve.wait_ge(*when("qT_p", t - 1, 1))
                    for b in range(2):
                        cp(hd[:, 384 * b:384 * b + 384], PB[:, 2 + b, 0:384], *(("q_raw", t) if b else ()))
                    head_norm(hv, hv2, 8, 96, R(rowsO, "mla_qn_g"), "qh", t)
                    if t:
                        rope(hv[:, :, 64:96], t, "c", 8, hv2[:, :, 0:32])
                    step(V.tensor_copy(hd2[:, 0:8], hd[:, 0:8]), "q_n", t)
                    for b in range(2):
                        dve.wait_ge(*when("qT_p", t, b))
                        cp(hTv[0:96, 4 * b:4 * b + 4, t * P:(t + 1) * P],
                           PB[0:96, 4 + b, :].rearrange("p (k n) -> p k n", k=4), "qT", t, b)
                for kt in range(4):
                    dve.wait_ge(*when("kv_up", kt))
                    t = [0, None, 1, 2][kt]
                    kr = ckr if kt == 1 else O[:, t, OKR:OKR + 32]
                    for b in range(2):
                        src = PB[:, 2 + b, :].rearrange("p (h n) -> p h n", h=4)
                        cp(hv[:, 4 * b:4 * b + 4, 0:64], src[:, :, 0:64])
                        cp(vC[:, kt, 4 * b:4 * b + 4, :], src[:, :, 64:128], *(("k_raw", kt) if b else ()))
                    cp(hv[:, :, 64:96], bc(kr, 1, 8))
                    head_norm(hv, hv2, 8, 96, R(rowsO, "mla_kn_g"), "kh", kt)
                    if kt >= 2:
                        rope(hv[:, :, 64:96], t, "c", 8, hv2[:, :, 0:32])
                    step(V.tensor_copy(hd2[:, 0:8], hd[:, 0:8]), "k_n", kt)
                    for b in range(2):
                        dve.wait_ge(*when("kT_p", kt, b))
                        cp(kT[0:96, 4 * b:4 * b + 4, 128 * kt:128 * kt + 128],
                           PB[0:96, 4 + b, :].rearrange("p (k n) -> p k n", k=4), "kT", kt, b)
                tmp = h8(hd[:, 0:512])
                for t in range(TILES):
                    qd, kd = h8(O[:, t, OQD:OQD + 512]), h8(O[:, t, OKD:OKD + 512])
                    head_norm(qd, tmp, 8, 64, R(rowsO, "diff_qn_g"), "dq", t)
                    head_norm(kd, tmp, 8, 64, R(rowsO, "diff_kn_g"), "dk", t)
                    if t:
                        rope(qd, t, "d", 8, tmp)
                        rope(kd, t, "d", 8, tmp)
                    else:
                        cp(hd2[:, 0:8], hd[:, 0:8], "caches")
                    cp(hd2[:, 8:16], hd[:, 0:8], "dqk", t)
                for t in (0, 1, 2, 3):
                    if t < 3:
                        dve.wait_ge(*when("dqT_p", t))
                        cp(dqT[:, :, t * P:(t + 1) * P], PB[:, 6, :].rearrange("p (k n) -> p k n", k=4), "dqT", t)
                    kt = [0, 2, 3, 1][t]
                    dve.wait_ge(*when("dkT_p", kt))
                    cp(dkT[:, :, 128 * kt:128 * kt + 128], PB[:, 7, :].rearrange("p (k n) -> p k n", k=4), "dkT", kt)
                end("dve", "odd_prep")

            def attend():
                def top(u):
                    n = 128 if u < 16 else 384
                    dve.wait_ge(*when("sc", u))
                    if u >= 2:
                        dve.wait_ge(*when("prob", u - 2))
                    m = small[:, 64 + u % 2:65 + u % 2]
                    red(m, PB[:, u % 2, 0:n], op=ALU.max)
                    ts(m, m, -((96 if u % 16 < 8 else 64) ** -0.5), None, ALU.mult, None, "nmax", u)

                def turned(u):
                    n = 128 if u < 16 else 384
                    dve.wait_ge(*when("pT", u))
                    cp(probT[:, u % 2, :, :].rearrange("p k n -> p (k n)")[:, 0:n], PB[:, 2 + u % 2, 0:n], "probT", u)

                def out(u):
                    t, m = u // 16, u % 16
                    dve.wait_ge(*when("pv", u))
                    rec = small[:, 68:69]
                    step(V.reciprocal(rec, small[:, 66 + u % 2:67 + u % 2]))
                    if m < 8:
                        ts(mix[:, 64 * m:64 * m + 64], PB[:, 4 + u % 2, 0:64], rec, None, ALU.mult, None, "ov", u)
                        return
                    o = mix[:, 512 + 128 * ((m - 8) // 2):640 + 128 * ((m - 8) // 2)]
                    if m % 2 == 0:
                        ts(o, PB[:, 4 + u % 2, 0:128], rec, None, ALU.mult, None, "ov", u)
                    else:
                        tt(rec, rec, small[:, 62:63], ALU.mult)
                        stt(o, PB[:, 4 + u % 2, 0:128], rec, o, ALU.mult, ALU.add, "ov", u)

                top(0)
                for u in range(48):
                    if u + 1 < 48:
                        top(u + 1)
                    turned(u)
                    if u % 16:
                        out(u - 1)
                    if u % 16 == 15:
                        out(u)
                        t = u // 16
                        od = h8(mix[:, 512:1024], 4)
                        head_norm(od, h8(hd[:, 0:512], 4), 4, 128, R(rowsO, "diff_subln_g"), "dd", t)
                        ts(od, od, 1.0 - LAM_INIT, None, ALU.mult, None, "omix1", t)
                        mixed(1, t)

            dve.wait_ge(sem("ld_const"), 32)
            dve.wait_ge(sem("ld_x"), 16 * TILES)
            V.memset(small[:, 70:71], 0.0).then_inc(hid_done, CREDIT)
            V.memset(small[:, 71:72], 0.0).then_inc(acc_done, 2)
            V.memset(small[:, 73:74], 0.0).then_inc(gu_done, 1)
            V.memset(small[:, 74:75], 0.0).then_inc(dn_done, 1)
            mods(0)
            norm(0, 0)
            for g, tiles in enumerate(((0,), (1, 2))):
                if g == 1:
                    pass
                copies(("ein", g), tiles, 7, EVEN, E)
                if g == 0:
                    dve.wait_ge(sem("ld_even"), 16 * 5)
                    dve.wait_ge(*when("SG0"))
                    dve.wait_ge(*when("SR0"))
                    step(V.memset(RH, 0.0))
                    step(V.memset(UU, 0.0))
                else:
                    dve.wait_ge(sem("ld_sg"), 8 * 16)
                    for d in range(2):
                        dve.wait_ge(*when("state_in_p", d))
                        cp(SR[:, d, :, :], PB[:, d, :].rearrange("p (j n) -> p j n", j=4), "state_in", d)
                for i in range(len(tiles)):
                    cp(small[:, 72:73], small[:, 70:71], "e_ready", g, i)
                    bank = 0
                    for n in range(7):
                        for ii in range(len(tiles)):
                            if bank % 2 == 0 and n == 6:
                                dve.wait_ge(*when("ein", g, "evac", n, ii))
                            bank += 1
                    dve.wait_ge(*when("lora", g, i))
                    prepare(g, i)
                units = (((0, 0), (0, 1)), ((0, 0), (1, 0), (1, 1), (0, 1)))[g]
                done = set()
                for i, d in units:
                    gla(g, i, d, i not in done)
                    rwkv(g, i, d, i not in done)
                    done.add(i)
                end("dve", f"units{g}")
                if g == 0:
                    for d in range(2):
                        dve.wait_ge(*when("state_out_p", d))
                        cp(stg[:, d, :], PB[:, d, :], "state_out", d)
                    cp(small[:, 72:73], small[:, 70:71], "state_out_T")
                for i, t in enumerate(tiles):
                    even_out(g, i)
                    mixed(0, t)
                end("dve", f"out_g{g}")
            for l in range(2):
                if l == 1:
                    mods(1)
                    norm(1, 0)
                    copies(("oin",), (0, 1, 2), 4, ODD, O)
                    dve.wait_ge(*when("oin", "evac", 3, 2)) if False else None
                    dve.wait_ge(*when("oin", "evac", 3, 1))
                    odd_prepare()
                    attend()
                residual(l)
                end("dve", f"mixer{l}")
                norm(l, 1)
                if l == 1:
                    dve.wait_ge(*when("caches_stored"))
                route(l)
                experts(l)
                end("dve", f"moe{l}")
    return seen


def constants():
    import numpy as np
    a, b = np.arange(P)[:, None], np.arange(P)[None, :]
    same = (a // CH) == (b // CH)
    c = np.zeros((P, NCONST), np.float32)

    def put(name, v):
        s, w = _C[name]
        c[:, s:s + w] = v

    put("ident", a == b)
    put("lt", same & (a < b))
    put("le", same & (a <= b))
    put("gt", same & (a > b))
    put("ge", same & (a >= b))
    put("half", np.arange(P)[:, None] // CH == np.arange(2)[None, :])
    lv = np.concatenate([(a >> (v + 1) == b >> (v + 1)) & ((a >> v) % 2 == 0) & ((b >> v) % 2 == 1) for v in range(6)], 1)
    lv_t = np.concatenate([(a >> (v + 1) == b >> (v + 1)) & ((a >> v) % 2 == 1) & ((b >> v) % 2 == 0) for v in range(6)], 1)
    put("lvl0", lv)
    put("lvl1", lv_t)
    sel = np.zeros((P, 256))
    sel[0, 0:128] = 1
    sel[1, 128:256] = 1
    put("sel", sel)
    put("bdg", (a // 64) == (np.arange(256)[None, :] // 128))
    put("bdr", (a // 64) == (b // 64))
    put("tie", np.tile((np.arange(4)[None, :] < np.arange(4)[:, None]).reshape(1, 16), (P, 1)))
    put("one", 1.0)
    for kind, dim in (("c", 32), ("d", 64)):
        half = dim // 2
        inv = (1.0 / (np.float32(10000.0) ** (np.arange(0, half, 2, dtype=np.float32) / np.float32(half)))).astype(np.float32)
        tok = np.arange(256)
        ang_r = (tok // 64).astype(np.float32)[:, None] * inv
        ang_c = (tok % 64).astype(np.float32)[:, None] * inv
        ang = np.concatenate([ang_r, ang_r, ang_c, ang_c], -1).astype(np.float32)
        q = dim // 4
        sign = np.concatenate([-np.ones(q), np.ones(q), -np.ones(q), np.ones(q)])
        put("cos" + kind, np.cos(ang).reshape(2, P, dim).transpose(1, 0, 2).reshape(P, 2 * dim))
        put("sin" + kind, (np.sin(ang) * sign).reshape(2, P, dim).transpose(1, 0, 2).reshape(P, 2 * dim))
    return c


def layout(i):
    import numpy as np

    def blocks(w):
        n = -(-w.shape[1] // 512) * 512
        w = np.concatenate([w, np.zeros((w.shape[0], n - w.shape[1]), w.dtype)], 1) if n != w.shape[1] else w
        return w.reshape(KD, P, n // 512, 512).transpose(2, 1, 0, 3).reshape(n // 512, P, CHUNK)

    def column(v):
        return v.reshape(-1, P).T

    a = {}
    a["consts"] = constants()
    a["x"] = np.concatenate([i["x_prompt"].reshape(1, P, D), i["x_sample"].reshape(2, P, D)], 0)
    cc = np.stack([column(i["c_ctx"]), column(i["c"][0])], 2).reshape(P, 16)
    a["cols"] = np.concatenate([cc, column(i["norm_g"].reshape(-1)), column(i["b_mod"].reshape(-1))], 1)
    a["b_gate"] = np.stack([i["b_mod"][:, 2 * D:3 * D], i["b_mod"][:, 5 * D:6 * D]], 1)
    a["w_mod"] = np.stack([blocks(i["w_mod"][l]) for l in range(2)])
    a["w_mix"] = np.concatenate([blocks(i[n][0]) for n in ("ev_w_in", "ev_w_out", "od_w_in", "od_w_out")])
    for l in range(2):
        for m, n in enumerate(("moe_w_gate", "moe_w_up")):
            a[f"w_moe{l}{m}"] = i[n][l].reshape(NE, KD, P, FF).transpose(0, 2, 1, 3).reshape(NE, P, CHUNK)
        a[f"w_moe{l}2"] = i["moe_w_down"][l].reshape(NE, KF, P, D).transpose(0, 2, 1, 3).reshape(NE, P, CHUNK)
    a["rows_even"] = np.concatenate([i[n].reshape(-1) for n in (
        "gla_a_b", "rw_w0", "rw_a0", "rw_kk", "rw_ka", "rw_rk")])
    a["rows_gain"] = np.concatenate([i[n].reshape(-1) for n in ("rw_gn_g", "rw_gn_b", "gla_o_g")])
    a["rows_odd"] = np.concatenate([i[n].reshape(-1) for n in (
        "mla_qa_g", "mla_kva_g", "mla_qn_g", "mla_kn_g", "diff_qn_g", "diff_kn_g", "diff_lam", "diff_subln_g")])
    a["b_router"] = i["moe_b_router"]
    a["w_router"] = i["moe_w_router"].reshape(KD, P, NE).transpose(1, 0, 2).reshape(P, KD * NE)
    a["gla_a_up"] = i["gla_a_up"][0]
    a["rw_w2"] = i["rw_w2"].reshape(P, 512)
    a["rw_a2"] = i["rw_a2"].reshape(P, 512)
    a["rw_g2"] = i["rw_g2"][0]
    a["state_gla"] = i["state_gla"][0, 0]
    a["state_rwkv"] = i["state_rwkv"][0, 0]
    a["mla_q_up"] = i["mla_q_up"][0]
    a["mla_kv_up"] = i["mla_kv_up"][0]
    for n in ("cache_mla_ckv", "cache_mla_krope", "cache_diff_k", "cache_diff_v"):
        a[n] = i[n][0, 0]
    return {n: np.ascontiguousarray(v) for n, v in a.items()}


_OUTS = {"y": (TILES, P, D), "new_state_gla": (2, 4, 64, 128), "new_state_rwkv": (2, 8, 64, 64), "new_ckv": (P, 128),
         "new_krope": (P, 32), "new_dk": (4, 2, P, 64), "new_dv": (4, P, 128)}


def program(nc, shapes, known):
    io = {n: nc.dram_tensor(f"in_{n}", s, F32, kind="ExternalInput").ap() for n, s in shapes.items()}
    for n, s in _OUTS.items():
        io[n] = nc.dram_tensor(f"out_{n}", s, F32, kind="ExternalOutput").ap()
    io["w_moe"] = [[io[f"w_moe{l}{m}"] for m in range(3)] for l in range(2)]
    return build(nc, io, known)


def kernel(**inputs):
    import numpy as _np
    import concourse.bacc as _bacc
    from concourse.bass_utils import run_bass_kernel_spmd as _run

    arrays = layout({n: _np.asarray(v) for n, v in inputs.items()})
    shapes = {n: v.shape for n, v in arrays.items()}
    stages = program(_bacc.Bacc("TRN2", target_bir_lowering=False, num_devices=1), shapes, None)
    nc = _bacc.Bacc("TRN2", target_bir_lowering=False, num_devices=1)
    program(nc, shapes, stages)
    r = _run(nc, [{f"in_{n}": v for n, v in arrays.items()}], core_ids=[0]).results[0]
    y = r["out_y"]
    return (y[0:1], y[1:3].reshape(1, 2 * P, D), r["out_new_state_gla"][None, None], r["out_new_state_rwkv"][None, None],
            r["out_new_ckv"][None, None], r["out_new_krope"][None, None], r["out_new_dk"][None, None],
            r["out_new_dv"][None, None])
```

```python
import math
from contextlib import ExitStack

import concourse.bass as bass
from concourse import mybir

F32 = mybir.dt.float32
I32 = mybir.dt.int32
ALU = mybir.AluOpType
ACT = mybir.ActivationFunctionType
AX = mybir.AxisListType

P = 128
D = 1024
KD = D // P
TILES = 3
NTOK = TILES * P
CH = 64
EPS = 1e-6
GN_EPS = 64e-5
NE = 16
FF = 512
KF = FF // P
SLOTS = 3
CHUNK = KD * 512
EQ, EK_, EV, EG, EAL, ER, EKB, EVB, EWL, EAA, EGL, EVEN = 0, 256, 512, 1024, 1536, 1568, 2080, 2592, 3104, 3232, 3360, 3488
OCQ, OCKV, OKR, OQD, OKD, OVD, ODD = 0, 256, 384, 416, 928, 1440, 1952
RW = math.exp(-0.5)
LAM_INIT = 0.8 - 0.6 * math.exp(-0.3 * 1)
MIX_EIN, MIX_EOUT, MIX_OIN, MIX_OOUT = 0, 7, 9, 13

_C = {}
_at = 0
for _n, _w in [("ident", 128), ("lt", 128), ("le", 128), ("gt", 128), ("ge", 128), ("half", 2),
               ("lvl0", 768), ("lvl1", 768), ("sel", 256), ("bdg", 256), ("bdr", 128), ("tie", 16),
               ("cosc", 64), ("sinc", 64), ("cosd", 128), ("sind", 128), ("one", 1)]:
    _C[_n] = (_at, _w)
    _at += _w
NCONST = _at
_M = {}
_at = 0
for _n, _w in [("earlier", 128), ("ones", 128), ("tri16", 256), ("row0", 16), ("extra", 80)]:
    _M[_n] = (_at, _w)
    _at += _w
NMOE = _at
CAP = P
NX = (2 * NTOK - NE) // P
ROWS = (NE + NX) * P
COL_C, COL_NG, COL_BM, NCOL = 0, 16, 48, 144
_R = {}
_at = 0
for _n, _w in [("gla_a_b", 512), ("rw_w0", 1024), ("rw_a0", 1024), ("rw_kk", 512), ("rw_ka", 512), ("rw_rk", 512)]:
    _R[_n] = (_at, _w)
    _at += _w
NROW_E = _at
_at = 0
for _n, _w in [("rw_gn_g", 512), ("rw_gn_b", 512), ("gla_o_g", 128)]:
    _R[_n] = (_at, _w)
    _at += _w
NROW_G = _at
_at = 0
for _n, _w in [("mla_qa_g", 256), ("mla_kva_g", 128), ("mla_qn_g", 96), ("mla_kn_g", 96), ("diff_qn_g", 64),
               ("diff_kn_g", 64), ("diff_lam", 256), ("diff_subln_g", 128)]:
    _R[_n] = (_at, _w)
    _at += _w
NROW_O = _at


def bc(ap, axis, n):
    a = ap.unsqueeze(axis)
    shape = list(a.shape)
    shape[axis] = n
    return a.broadcast_to(shape)


def build(nc, io, known):
    seen = {}
    count = {"pe": 0, "act": 0, "dve": 0, "pool": 0}
    with ExitStack() as ctx:
        def sb(name, cols, rows=P):
            return ctx.enter_context(nc.sbuf_tensor(name, [rows, cols], F32))

        sems = {}

        def sem(name):
            if name not in sems:
                sems[name] = ctx.enter_context(nc.semaphore(name))
            return sems[name]

        for e in count:
            sem(e)

        def tick(engine, *name):
            count[engine] += 1
            if name:
                seen[name] = (engine, count[engine])
            return sem(engine), 1

        def when(*name):
            engine, value = known.get(name, ("pe", 1)) if known is not None else ("pe", 1)
            if known and name not in known:
                raise KeyError(name)
            return sem(engine), value

        def end(engine, stage):
            seen[("end", engine, stage)] = (engine, count[engine])

        def meet(eng, me, stage, others=("pe", "act", "dve")):
            for e in others:
                if e != me:
                    s, value = when("end", e, stage)
                    if value > 0:
                        eng.wait_ge(s, value)

        PB = ctx.enter_context(nc.psum_tensor("PB", [P, 8, 512], F32))
        cst = sb("cst", NCONST)
        cols = sb("cols", NCOL)
        x = sb("x", TILES * D)
        hT = sb("hT", KD * NTOK)
        ring = sb("ring", SLOTS * CHUNK)
        gate = sb("gate", 2 * 2 * D)
        modT = sb("modT", 96)
        mulA = sb("mulA", 2 * KD * 2)
        scT = sb("scT", 16)
        small = sb("small", 256)
        brout = sb("brout", 16)
        wrout = sb("wrout", KD * NE)
        gatek = sb("gatek", 2 * TILES)
        rows_i = ctx.enter_context(nc.sbuf_tensor("rows_i", [P, 2 * TILES], I32))
        xtab = ctx.enter_context(nc.sbuf_tensor("xtab", [P, 8], I32))
        Xd = nc.dram_tensor("dispatched", (ROWS, D), F32, kind="Internal").ap()
        Yd = nc.dram_tensor("expert_out", (ROWS, D), F32, kind="Internal").ap()
        arena_words = 26448
        arena = sb("arena", arena_words)

        def C(name, lo=0, n=None):
            s, w = _C[name]
            return cst[:, s + lo:s + (w if n is None else lo + n)]

        xv = x[:, :].rearrange("p (t d) -> p t d", t=TILES)
        hTv = hT[:, :].rearrange("p (k n) -> p k n", k=KD)
        slot = [ring[:, s * CHUNK:(s + 1) * CHUNK].rearrange("p (k n) -> p k n", k=KD) for s in range(SLOTS)]
        slot_dn = [ring[:, s * CHUNK:(s + 1) * CHUNK].rearrange("p (k n) -> p k n", k=KF) for s in range(SLOTS)]
        gatev = gate[:, :].rearrange("p (c s d) -> p c s d", c=2, s=2)
        modTv = modT[:, :].rearrange("p (j c) -> p j c", c=2)
        mulAv = mulA[:, :].rearrange("p (s k c) -> p s k c", s=2, c=2)
        ident = C("ident")

        def carve(at):
            pos = [at]

            def take(words):
                a = pos[0]
                pos[0] += words
                assert pos[0] <= arena_words, pos[0]
                return arena[:, a:a + words]
            return take

        take = carve(0)
        E = take(2 * EVEN).rearrange("p (t n) -> p t n", t=2)
        rowsE = take(NROW_E)
        oG = take(2 * 512).rearrange("p (t n) -> p t n", t=2)
        yR = take(2 * 512).rearrange("p (t n) -> p t n", t=2)
        kkn = take(2 * 512).rearrange("p (t n) -> p t n", t=2)
        loT = take(2 * 512).rearrange("p (t j n) -> p t j n", t=2, j=4)
        bon = take(16).rearrange("p (t h) -> p t h", t=2)
        SG = take(2 * 512).rearrange("p (d j n) -> p d j n", d=2, j=2)
        SR = take(2 * 512).rearrange("p (d j n) -> p d j n", d=2, j=4)
        tokm = take(4 * 512).rearrange("p (a n) -> p a n", a=4)
        G4 = take(4 * 512).rearrange("p (h n) -> p h n", h=4)
        TA = take(512).rearrange("p (a n) -> p a n", a=4)
        TB = take(512).rearrange("p (a n) -> p a n", a=4)
        X4 = take(512).rearrange("p (h n) -> p h n", h=4)
        XT4 = take(512).rearrange("p (h n) -> p h n", h=4)
        T14 = take(512).rearrange("p (h n) -> p h n", h=4)
        LJ4 = take(512).rearrange("p (h n) -> p h n", h=4)
        RH = take(256)
        UU = take(256)
        aup = take(512)
        w2 = take(512)
        a2 = take(512)
        rowsG = tokm.rearrange("p a n -> p (a n)")[:, 0:NROW_G]
        g2w = tokm[:, 3, :]
        zeros = oG.rearrange("p t n -> p (t n)")
        tmpE = X4.rearrange("p h n -> p (h n)"), XT4.rearrange("p h n -> p (h n)"), T14.rearrange("p h n -> p (h n)")
        stg = G4

        xn = tokm.rearrange("p a n -> p (a n)")[:, 0:1024]
        rowb = xn[0:2, :]

        take = carve(0)
        O = take(3 * ODD).rearrange("p (t n) -> p t n", t=3)
        rowsO = take(NROW_O)
        cdk = take(512).rearrange("p (m n) -> p m n", m=8)
        cdv = take(512).rearrange("p (h n) -> p h n", h=4)
        cckv = take(128)
        ckr = take(32)
        kvup = take(1024)
        u0 = take(1536)
        cqT = take(2 * NTOK).rearrange("p (k n) -> p k n", k=2)
        ckT = take(4 * P).rearrange("p (k n) -> p k n", k=4)
        kT = take(8 * 512).rearrange("p (h n) -> p h n", h=8)
        vC = take(4 * 512).rearrange("p (k h n) -> p k h n", k=4, h=8)
        dqT = take(4 * NTOK).rearrange("p (h n) -> p h n", h=4)
        dkT = take(4 * 512).rearrange("p (h n) -> p h n", h=4)
        hd = take(768)
        hd2 = take(768)
        qup = u0.rearrange("p (k n) -> p k n", k=2)
        prob = take(2 * 384).rearrange("p (b n) -> p b n", b=2)
        probT = take(2 * 384).rearrange("p (b k n) -> p b k n", b=2, k=3)
        mix = u0[:, 0:1024]

        take = carve(0)
        slots_x = take(3 * CHUNK)
        xb = take(2 * D).rearrange("p (b d) -> p b d", b=2)
        xT = take(2 * D).rearrange("p (b n) -> p b n", b=2)
        sil = take(2 * FF).rearrange("p (b n) -> p b n", b=2)
        hid = take(2 * FF).rearrange("p (b n) -> p b n", b=2)
        hidT = take(2 * FF).rearrange("p (b n) -> p b n", b=2)
        yb = take(2 * D).rearrange("p (b d) -> p b d", b=2)
        cmoe = take(NMOE)
        route_w = take(1920)
        mask = small[:, 176:224]
        yg = slots_x[:, 0:6 * D].rearrange("p (c d) -> p c d", c=6)
        assert 2 * D + 2 * FF == TILES * D
        htok = arena[:, 3 * CHUNK + 2 * D:3 * CHUNK + 2 * D + TILES * D].rearrange("p (t d) -> p t d", t=TILES)
        wslot = [[ring[:, m * CHUNK:(m + 1) * CHUNK] for m in range(3)],
                 [slots_x[:, m * CHUNK:(m + 1) * CHUNK] for m in range(3)]]

        def M(name):
            a, w = _M[name]
            return cmoe[:, a:a + w]

        def R(rows, name, lo=0, n=None):
            s, w = _R[name]
            return rows[:, s + lo:s + (w if n is None else lo + n)]

        stream = [("mod", (0, n), ("modp", 0, n)) for n in range(12)]
        stream += [("mix", MIX_EIN + n, ("ein", 0, n)) for n in range(7)]
        stream += [("mix", MIX_EIN + n, ("ein", 1, n)) for n in range(7)]
        stream += [("mix", MIX_EOUT + n, ("outp", 0, n)) for n in range(2)]
        first = len(stream)
        stream += [("mod", (1, n), ("modp", 1, n)) for n in range(12)]
        stream += [("mix", MIX_OIN + n, ("oin", n)) for n in range(4)]
        stream += [("mix", MIX_OOUT + n, ("outp", 1, n)) for n in range(2)]
        where, landed = {}, {}
        cnt = [0] * SLOTS
        for i, (kind, src, name) in enumerate(stream):
            s = (i if i < first else i - first) % SLOTS
            cnt[s] += 1
            where[name], landed[name] = s, 16 * cnt[s]
        w_land = [sem(f"w_landed{s}") for s in range(SLOTS)]
        EARLY = 2

        def steps(tag):
            return {n: sem(f"{tag}_{n}") for n in (
                "xT_p", "xT_a", "xT_v", "gu", "silu", "hid", "hT_p", "hT_v", "dn", "y_a", "y_v")}

        def loop(S, base, stride, land, land_base, rows, stores):
            return dict(S=S, base=base, k=stride, land=land, land_base=land_base, rows=rows, stores=stores)

        def steps_of(L, step, i, c):
            v = L["base"] + c + 1 + EARLY
            return L["S"][step], (v if i is None else i * L["k"] + v)

        def loads_of(L, sems, base, i, c):
            v = base + 16 * (c // L["k"] + 1)
            return sems, (v if i is None else i * 16 + v)

        half = NE // 2
        per = [sum(1 for n in stream[:first] if where[n[2]] == m) for m in range(SLOTS)]
        per1 = [sum(1 for n in stream[first:] if where[n[2]] == m) for m in range(SLOTS)]
        for n in stream[first:]:
            landed[n[2]] += 16 * half
        w_land1 = [sem(f"w_landed{m + 3}") for m in range(3)]
        blk = steps("blk")
        x_land = [sem(f"x_landed{b}") for b in range(2)]
        y_st = [sem(f"y_stored{b}") for b in range(2)]
        base_loop, extra_loop = [], []
        for l in range(2):
            ring_base = [16 * (per[m] + l * (half + per1[m])) for m in range(SLOTS)]
            base_loop.append(loop(blk, l * NE, 2, [w_land, w_land1], [ring_base, [16 * half * l] * 3],
                                  (x_land, 16 * half * l), (y_st, 16 * half * l + 16)))
            ext = [sem(f"ext{l}_w_landed{m}") for m in range(3)]
            extra_loop.append(loop(steps(f"ext{l}"), 0, 1, [ext], [[0] * 3],
                                   ([sem(f"ext{l}_x_landed")], 0), ([sem(f"ext{l}_y_stored")], 16)))

        block = ctx.enter_context(nc.Block())

        @block.sync
        def _(sp):
            owner = [None] * SLOTS

            def load(kind, src, name):
                s = where[name]
                if owner[s] is not None:
                    sp.wait_ge(*when(*owner[s]))
                owner[s] = name
                dram = io["w_mod"][src[0], src[1]] if kind == "mod" else io["w_mix"][src]
                sp.dma_start(ring[:, s * CHUNK:(s + 1) * CHUNK], dram).then_inc(w_land[s], 16)

            def weights(L, l, i, c, b, e):
                for m in range(3):
                    sp.wait_ge(*steps_of(L, "gu" if m < 2 else "dn", i, c - L["k"]))
                    sp.dma_start(wslot[b][m], io["w_moe"][l][m][bass.ds(e, 1)].rearrange("e p n -> (e p) n"))\
                        .then_inc(L["land"][b][m], 16)

            def experts(l):
                L = base_loop[l]
                for m in range(SLOTS):
                    if owner[m] is not None:
                        sp.wait_ge(*when(*owner[m]))
                    owner[m] = None
                weights(L, l, None, 0, 0, 0)
                meet(sp, "sp", f"mixer{l}")
                if l:
                    sp.wait_ge(sem("st_cache"), 14 * 16)
                weights(L, l, None, 1, 1, 1)
                with sp.Fori(1, half) as i:
                    for b in range(2):
                        weights(L, l, i, b, b, i * 2 + b)
                sp.wait_ge(*when("rows", l))
                n_extra = nc.sync.value_load(xtab[0:1, 7:8], min_val=0, max_val=NX)
                with sp.If(n_extra > 0):
                    X = extra_loop[l]
                    sp.wait_ge(*steps_of(L, "gu", None, NE - 1))
                    sp.wait_ge(*steps_of(L, "dn", None, NE - 1))
                    with sp.Fori(0, NX) as i:
                        e = nc.sync.value_load(xtab[0:1, bass.ds(i, 1)], min_val=0, max_val=NE - 1)
                        weights(X, l, i, 0, 0, e)
                        sp.wait_ge(*steps_of(X, "xT_p", i, -1))
                        sp.dma_start(xb[:, 0, :], Xd[bass.ds(i * P + NE * P, P), :]).then_inc(X["rows"][0][0], 16)
                sp.wait_ge(*when("y_all", l))

            for item in stream[:first]:
                load(*item)
            experts(0)
            for item in stream[first:]:
                load(*item)
            experts(1)

        @block.gpsimd
        def _(pool):
            def dma(dst, src, name):
                pool.dma_start(dst, src).then_inc(sem(name), 16)

            dma(cst[:, :], io["consts"], "ld_const")
            dma(cols[:, :], io["cols"], "ld_const")
            for t in range(TILES):
                dma(xv[:, t, :], io["x"][t], "ld_x")
            dma(brout[:, :], io["b_router"].partition_broadcast(P), "ld_router")
            dma(wrout[:, :], io["w_router"], "ld_router")
            for c in range(2):
                for s in range(2):
                    dma(gatev[:, c, s, :], io["b_gate"][0, s].partition_broadcast(P), "ld_bgate")
            dma(rowsE, io["rows_even"].partition_broadcast(P), "ld_even")
            nc.gpsimd.memset(aup[0:32, :], 0.0).then_inc(*tick("pool", "aup0"))
            pool.wait_ge(*when("aup0"))
            for d in range(2):
                dma(aup[16 * d:16 * d + 16, 256 * d:256 * d + 256], io["gla_a_up"][d], "ld_even")
            dma(w2, io["rw_w2"], "ld_even")
            dma(a2, io["rw_a2"], "ld_even")

            def late_rows(g):
                meet(pool, "pool", f"units{g}")
                dma(rowsG, io["rows_gain"].partition_broadcast(P), "ld_late")
                dma(g2w, io["rw_g2"], "ld_late")

            nc.gpsimd.memset(SG, 0.0).then_inc(*tick("pool", "SG0"))
            nc.gpsimd.memset(SR, 0.0).then_inc(*tick("pool", "SR0"))
            late_rows(0)
            for d in range(2):
                for h in range(4):
                    r = 64 * (h % 2)
                    dma(io["new_state_gla"][d, h], SG[r:r + 64, d, h // 2, 128 * (h % 2):128 * (h % 2) + 128], "st_gla")
            pool.wait_ge(*when("state_out_T"))
            for d in range(2):
                for h in range(8):
                    r = 64 * (h % 2)
                    dma(io["new_state_rwkv"][d, h], stg[r:r + 64, d, (h // 2) * 128 + r:(h // 2) * 128 + r + 64], "st_rwkv")
            pool.wait_ge(sem("st_gla"), 8 * 16)
            pool.wait_ge(sem("st_rwkv"), 16 * 16)
            nc.gpsimd.memset(SG, 0.0).then_inc(*tick("pool", "SG1"))
            nc.gpsimd.memset(stg[:, 0:2, :], 0.0).then_inc(*tick("pool", "stg0"))
            pool.wait_ge(*when("stg0"))
            for d in range(2):
                for h in range(4):
                    r = 64 * (h % 2)
                    dma(SG[r:r + 64, d, h // 2, 128 * (h % 2):128 * (h % 2) + 128], io["state_gla"][d, h], "ld_sg")
                for h in range(8):
                    r = 64 * (h % 2)
                    dma(stg[r:r + 64, d, (h // 2) * 128 + r:(h // 2) * 128 + r + 64], io["state_rwkv"][d, h], "ld_sr")
            late_rows(1)

            def experts(l):
                meet(pool, "pool", f"mixer{l}")
                dma(cmoe, io["consts_moe"], "ld_cmoe")
                pool.wait_ge(sem("xd_zero"), 32)
                pool.wait_ge(*when("rows", l))
                for t in range(TILES):
                    pool.wait_ge(*when("htok", l, t))
                    for ch in range(2):
                        pool.indirect_dma_start(
                            Xd, bass.IndirectOffsetOnAxis(ap=rows_i[:, 3 * ch + t:3 * ch + t + 1], axis=0),
                            htok[:, t, :], None).then_inc(sem("dispatched"), 16)
                pool.wait_ge(sem("dispatched"), 96 * (l + 1))
                L = base_loop[l]
                with pool.Fori(0, half) as i:
                    for b in range(2):
                        pool.wait_ge(*steps_of(L, "xT_p", i, b - 2))
                        pool.dma_start(xb[:, b, :], Xd[bass.ds(i * 2 * P + b * P, P), :]).then_inc(x_land[b], 16)
                pool.wait_ge(*when("y_all", l))
                for t in range(TILES):
                    for ch in range(2):
                        pool.indirect_dma_start(
                            yg[:, 3 * ch + t, :], None, Yd,
                            bass.IndirectOffsetOnAxis(ap=rows_i[:, 3 * ch + t:3 * ch + t + 1], axis=0))\
                            .then_inc(sem(f"combined{t}"), 16)

            experts(0)
            meet(pool, "pool", "moe0")
            for c in range(2):
                for s in range(2):
                    dma(gatev[:, c, s, :], io["b_gate"][1, s].partition_broadcast(P), "ld_bgate")
            dma(rowsO, io["rows_odd"].partition_broadcast(P), "ld_odd")
            dma(qup, io["mla_q_up"].rearrange("(k p) n -> p k n", p=P), "ld_odd")
            dma(kvup, io["mla_kv_up"], "ld_odd")
            dma(cckv, io["cache_mla_ckv"], "ld_odd")
            dma(ckr, io["cache_mla_krope"], "ld_odd")
            for m in range(8):
                dma(cdk[:, m, :], io["cache_diff_k"][m // 2, m % 2], "ld_odd")
            for h in range(4):
                dma(cdv[:, h, :], io["cache_diff_v"][h], "ld_odd")
            pool.wait_ge(*when("caches"))
            dma(io["new_ckv"], O[:, 0, OCKV:OCKV + 128], "st_cache")
            dma(io["new_krope"], O[:, 0, OKR:OKR + 32], "st_cache")
            for m in range(8):
                dma(io["new_dk"][m // 2, m % 2], O[:, 0, OKD + 64 * m:OKD + 64 * m + 64], "st_cache")
            for h in range(4):
                dma(io["new_dv"][h], O[:, 0, OVD + 128 * h:OVD + 128 * h + 128], "st_cache")
            pool.wait_ge(sem("st_cache"), 14 * 16)
            nc.gpsimd.memset(small[:, 255:256], 0.0).then_inc(*tick("pool", "caches_stored"))
            experts(1)
            for t in range(TILES):
                pool.wait_ge(*when("x_moe", 1, t))
                dma(io["y"][t], xv[:, t, :], "st_y")
            pool.wait_ge(sem("st_y"), TILES * 16)

        @block.tensor
        def _(pe):
            reader = [None] * 8

            def claim(b, *name):
                if reader[b] is not None:
                    pe.wait_ge(*when(*reader[b]))
                reader[b] = name

            def mm(out, lhsT, rhs, start=True, stop=True, **k):
                return nc.tensor.matmul(out, lhsT, rhs, start=start, stop=stop, **k)

            def tp(out, in_, n=P):
                return nc.tensor.transpose(out, in_, ident[0:n, 0:n])

            def chunk_landed(*name):
                pe.wait_ge(w_land[where[name]], landed[name])
                return slot[where[name]]

            def mods(l):
                def post(n):
                    pe.wait_ge(*when("modrow", l, n))
                    row = rowb[0:2, 512 * (n % 2):512 * (n % 2) + 512]
                    if n // 2 in (2, 5):
                        for c in range(2):
                            claim(2 + c, "gadd", l, n, c)
                            mm(PB[:, 2 + c, :], C("sel", 128 * c, 128)[0:2, :], row).then_inc(*tick("pe", "gb", l, n, c))
                    else:
                        claim(4 + n % 2, "modT", l, n)
                        for j in range(4):
                            ins = tp(PB[:, 4 + n % 2, 2 * j:2 * j + 2], row[:, 128 * j:128 * j + 128], 2)
                        ins.then_inc(*tick("pe", "mt", l, n))
                for n in range(12):
                    w = chunk_landed("modp", l, n)
                    claim(n % 2, "modrow", l, n)
                    for k in range(KD):
                        ins = mm(PB[0:2, n % 2, :], scT[:, 2 * k:2 * k + 2], w[:, k, :], k == 0, k == KD - 1)
                    ins.then_inc(*tick("pe", "modp", l, n))
                    if n:
                        post(n - 1)
                post(11)
                end("pe", f"mods{l}")

            def norm(l, s):
                for t in range(TILES):
                    pe.wait_ge(*when("xn", l, s, t))
                    for b in range(2):
                        claim(6 + b, "hT", l, s, t, b)
                        for k in range(4):
                            ins = tp(PB[:, 6 + b, 128 * k:128 * k + 128], xn[:, (4 * b + k) * 128:(4 * b + k + 1) * 128])
                        ins.then_inc(*tick("pe", "xnT", l, s, t, b))

            def project(name, tiles, chunks, width):
                bank = 0
                for n in range(chunks):
                    w = chunk_landed(*name, n)
                    ncol = min(512, width - 512 * n)
                    for i, t in enumerate(tiles):
                        claim(bank % 4, *name, "evac", n, i)
                        for k in range(KD):
                            ins = mm(PB[:, bank % 4, 0:ncol], hTv[:, k, t * P:(t + 1) * P], w[:, k, 0:ncol],
                                     k == 0, k == KD - 1)
                        bank += 1
                        ins.then_inc(*tick("pe", *name, "p", n, i))
                    seen[(*name, n)] = ("pe", count["pe"])

            def lora_T(g, i):
                pe.wait_ge(*when("lora", g, i))
                claim(0, "loT", g, i)
                for j, (c0, n) in enumerate([(EWL, 128), (EAA, 128), (EGL, 128), (EAL, 32)]):
                    ins = tp(PB[0:n, 0, 128 * j:128 * j + 128], E[:, i, c0:c0 + n])
                ins.then_inc(*tick("pe", "lora_T", g, i))

            def gla(g, i, d):
                u = (g, i, d)
                inc, rest = (C("le"), C("gt")) if d == 0 else (C("ge"), C("lt"))
                pe.wait_ge(*when("loT", g, i))
                claim(0, "ga_z", *u)
                mm(PB[:, 0, 0:256], loT[0:32, i, 3, :], aup[0:32, 256 * d:256 * d + 256]).then_inc(*tick("pe", "za", *u))
                pe.wait_ge(*when("la", *u))
                claim(1, "g_exp", *u)
                claim(2, "g_dec", *u)
                la = tmpE[0][:, 0:256]
                mm(PB[:, 1, 0:256], inc, la)
                mm(PB[:, 1, 256:512], rest, la)
                for j in range(2):
                    ins = mm(PB[:, 2, 2 * j:2 * j + 2], la[:, 128 * j:128 * j + 128], C("half"))
                ins.then_inc(*tick("pe", "gcum", *u))
                pe.wait_ge(*when("gk", *u))
                claim(3, "gqkT", *u)
                for j in range(4):
                    ins = tp(PB[:, 3, 128 * j:128 * j + 128], tokm[:, j // 2, 128 * (j % 2):128 * (j % 2) + 128])
                ins.then_inc(*tick("pe", "gT", *u))
                pe.wait_ge(*when("gqkT", *u))
                claim(4, "gatt", *u)
                claim(5, "gatt", *u)
                for h in range(4):
                    r, j = 64 * (h % 2), h // 2
                    ins = mm(PB[:, 4 + h % 2, 128 * j:128 * j + 128], TA[r:r + 64, 2 + j, :], TA[r:r + 64, j, :])
                ins.then_inc(*tick("pe", "gA", *u))
                pe.wait_ge(*when("gatt", *u))
                claim(6, "gout", *u)
                for h in range(4):
                    mm(PB[:, 6, 128 * h:128 * h + 128], G4[:, h, 0:128], E[:, i, EV + 128 * h:EV + 128 * h + 128],
                       h == 0, False, skip_group_check=True)
                for n, c in enumerate((0, 1) if d == 0 else (1, 0)):
                    if n:
                        pe.wait_ge(*when("gS", *u, 0))
                    r = CH * c
                    for j in range(2):
                        mm(PB[r:r + CH, 6, 256 * j:256 * j + 256], TA[:, j, r:r + CH], SG[:, d, j, :],
                           False, n == 1, skip_group_check=True)
                    claim(7, "gS", *u, n)
                    for j in range(2):
                        ins = mm(PB[:, 7, 256 * j:256 * j + 256], tokm[r:r + CH, 2, 128 * j:128 * j + 128],
                                 E[r:r + CH, i, EV + 256 * j:EV + 256 * j + 256], skip_group_check=True)
                    ins.then_inc(*tick("pe", "gu", *u, n))

            def rwkv(g, i, d):
                u = (g, i, d)
                inc, exc = (C("le"), C("lt")) if d == 0 else (C("ge"), C("gt"))
                r = 64 * d
                claim(d, "r_zw", *u)
                mm(PB[:, d, :], loT[r:r + 64, i, 0, :], w2[r:r + 64, :]).then_inc(*tick("pe", "zw", *u))
                claim(2 + d, "r_za", *u)
                mm(PB[:, 2 + d, :], loT[r:r + 64, i, 1, :], a2[r:r + 64, :]).then_inc(*tick("pe", "zr", *u))
                pe.wait_ge(*when("lw", *u))
                lw = tmpE[0]
                claim(4, "e_inc", *u)
                mm(PB[:, 4, :], inc, lw)
                claim(5, "e_exc", *u)
                mm(PB[:, 5, :], exc, lw)
                claim(6, "e_wc", *u)
                for j in range(4):
                    ins = mm(PB[:, 6, 2 * j:2 * j + 2], lw[:, 128 * j:128 * j + 128], C("half"))
                ins.then_inc(*tick("pe", "rcum", *u))
                pe.wait_ge(*when("tokm", *u))
                for hf in range(2):
                    rwkv_half(g, i, d, hf)

            def rwkv_half(g, i, d, hf):
                u = (g, i, d, hf)
                claim(0, "TA", *u)
                claim(1, "TB", *u)
                for j in range(2):
                    f = (2 * hf + j) * 128
                    tp(PB[:, 0, 256 * j:256 * j + 128], tokm[:, 0, f:f + 128])
                    ins = tp(PB[:, 0, 256 * j + 128:256 * j + 256], tokm[:, 1, f:f + 128])
                ins.then_inc(*tick("pe", "tA", *u))
                for j in range(2):
                    f = (2 * hf + j) * 128
                    tp(PB[:, 1, 256 * j:256 * j + 128], tokm[:, 2, f:f + 128])
                    ins = tp(PB[:, 1, 256 * j + 128:256 * j + 256], tokm[:, 3, f:f + 128])
                ins.then_inc(*tick("pe", "tB", *u))
                pe.wait_ge(*when("TA", *u))
                pe.wait_ge(*when("TB", *u))
                for h in range(4):
                    j, r = h // 2, 64 * (h % 2)
                    claim(2 + h, "G4", *u)
                    for a in range(2):
                        ins = mm(PB[:, 2 + h, 256 * a:256 * a + 256], TB[r:r + 64, 2 * j + a, :],
                                 TA[r:r + 64, 2 * j:2 * j + 2, :])
                ins.then_inc(*tick("pe", "gram", *u))
                claim(6, "X0", *u)
                claim(7, "X0", *u)
                for h in range(4):
                    j, r = h // 2, 64 * (h % 2)
                    ins = mm(PB[:, 6 + h % 2, 128 * j:128 * j + 128], TA[r:r + 64, 2 * j, :], TB[r:r + 64, 2 * j, :])
                ins.then_inc(*tick("pe", "gramL", *u))
                for v in range(1, 6):
                    if v == 1:
                        pe.wait_ge(*when("XT0", *u))
                    else:
                        pe.wait_ge(*when("X", *u, v - 1))
                        pe.wait_ge(*when("XT", *u, v - 1))
                    pe.wait_ge(*when("LJ", *u, v))
                    claim(6, "T1", *u, v)
                    for h in range(4):
                        ins = mm(PB[:, 6, 128 * h:128 * h + 128], LJ4[:, h, :], X4[:, h, :])
                    ins.then_inc(*tick("pe", "t1", *u, v))
                    pe.wait_ge(*when("T1", *u, v))
                    if v < 5:
                        claim(7, "X", *u, v)
                        for h in range(4):
                            ins = mm(PB[:, 7, 128 * h:128 * h + 128], XT4[:, h, :], T14[:, h, :])
                        ins.then_inc(*tick("pe", "dx", *u, v))
                    claim(0, "XT", *u, v)
                    for h in range(4):
                        ins = mm(PB[:, 0, 128 * h:128 * h + 128], T14[:, h, :], XT4[:, h, :])
                    ins.then_inc(*tick("pe", "dxt", *u, v))
                pe.wait_ge(*when("XT", *u, 5))
                for n, c in enumerate((0, 1) if d == 0 else (1, 0)):
                    r = CH * c
                    if n:
                        pe.wait_ge(*when("S", *u, 0))
                    claim(1, "RH", *u, n)
                    for h in range(4):
                        V = E[:, i, EVB + (4 * hf + h) * 64:EVB + (4 * hf + h + 1) * 64]
                        mm(PB[r:r + CH, 1, 64 * h:64 * h + 64], G4[:, h, 256 + r:256 + r + CH], V, h == 0, False,
                           skip_group_check=True)
                    for j in range(2):
                        ins = mm(PB[r:r + CH, 1, 128 * j:128 * j + 128], TA[:, 2 * j, r:r + CH], SR[:, d, 2 * hf + j, :],
                                 False, j == 1, skip_group_check=True)
                    ins.then_inc(*tick("pe", "rh", *u, n))
                    claim(4, "Y", *u, n)
                    for h in range(4):
                        V = E[:, i, EVB + (4 * hf + h) * 64:EVB + (4 * hf + h + 1) * 64]
                        mm(PB[r:r + CH, 4, 64 * h:64 * h + 64], G4[:, h, 384 + r:384 + r + CH], V, h == 0, False,
                           skip_group_check=True)
                    for j in range(2):
                        mm(PB[r:r + CH, 4, 128 * j:128 * j + 128], TA[:, 2 * j + 1, r:r + CH], SR[:, d, 2 * hf + j, :],
                           False, False, skip_group_check=True)
                    pe.wait_ge(*when("RH", *u, n))
                    claim(2, "U", *u, n)
                    for h in range(4):
                        ins = mm(PB[r:r + CH, 2, 64 * h:64 * h + 64], XT4[:, h, r:r + CH], RH[:, 64 * h:64 * h + 64],
                                 skip_group_check=True)
                    ins.then_inc(*tick("pe", "uu", *u, n))
                    pe.wait_ge(*when("U", *u, n))
                    claim(6 + c, "S", *u, n)
                    for j in range(2):
                        f = (2 * hf + j) * 128
                        mm(PB[:, 6 + c, 128 * j:128 * j + 128], tokm[r:r + CH, 2, f:f + 128],
                           UU[r:r + CH, 128 * j:128 * j + 128], True, False, skip_group_check=True)
                        ins = mm(PB[:, 6 + c, 128 * j:128 * j + 128], tokm[r:r + CH, 3, f:f + 128],
                                 E[r:r + CH, i, EVB + f:EVB + f + 128], False, True, skip_group_check=True)
                    ins.then_inc(*tick("pe", "su", *u, n))
                    for h in range(4):
                        ins = mm(PB[r:r + CH, 4, 64 * h:64 * h + 64], G4[:, h, 128 + r:128 + r + CH],
                                 UU[:, 64 * h:64 * h + 64], False, h == 3, skip_group_check=True)
                    ins.then_inc(*tick("pe", "yy", *u, n))

            def states_T(name, src, wait):
                pe.wait_ge(*when(*wait)) if isinstance(wait, tuple) else pe.wait_ge(sem(wait), 16 * 16)
                for d in range(2):
                    claim(d, name, d)
                    for j in range(4):
                        ins = tp(PB[:, d, 128 * j:128 * j + 128], src(d, j))
                    ins.then_inc(*tick("pe", name + "_p", d))

            def even_out(g, i, t):
                pe.wait_ge(sem("ld_late"), 32 * (g + 1))
                claim(5, "omix", g, i)
                mm(PB[:, 5, :], loT[:, i, 2, :], g2w).then_inc(*tick("pe", "gm", g, i))
                mixed_T(("omix", g, i), lambda k: (oG if k < 4 else yR)[:, i, 128 * (k % 4):128 * (k % 4) + 128], t, 0)

            def mixed_T(name, src, t, l):
                pe.wait_ge(*when(*name))
                for b in range(2):
                    claim(6 + b, "mT", l, t, b)
                    for k in range(4):
                        ins = tp(PB[:, 6 + b, 128 * k:128 * k + 128], src(4 * b + k))
                    ins.then_inc(*tick("pe", "mixT", l, t, b))

            def router(l):
                pe.wait_ge(sem("ld_router"), 32)
                for t in range(TILES):
                    for b in range(2):
                        pe.wait_ge(*when("hT", l, 1, t, b))
                claim(0, "scores", l)
                for t in range(TILES):
                    for k in range(KD):
                        ins = mm(PB[:, 0, 16 * t:16 * t + 16], hTv[:, k, t * P:(t + 1) * P],
                                 wrout[:, 16 * k:16 * k + 16], k == 0, k == KD - 1)
                ins.then_inc(*tick("pe", "rt", l))
                for t in range(TILES):
                    for b in range(2):
                        claim(2 + (2 * t + b) % 4, "htok_c", l, t, b)
                        for k in range(4):
                            ins = tp(PB[:, 2 + (2 * t + b) % 4, 128 * k:128 * k + 128],
                                     hTv[:, 4 * b + k, t * P:(t + 1) * P])
                        ins.then_inc(*tick("pe", "htok_p", l, t, b))
                pe.wait_ge(*when("mask", l))
                claim(1, "place", l)
                pe.wait_ge(sem("ld_cmoe"), 16 * (l + 1))
                for t in range(TILES + 1):
                    for q in range(t):
                        ins = mm(PB[:, 1, 16 * t:16 * t + 16], M("ones"), mask[:, 16 * q:16 * q + 16], q == 0,
                                 t == TILES and q == t - 1)
                    if t < TILES:
                        mm(PB[:, 1, 16 * t:16 * t + 16], M("earlier"), mask[:, 16 * t:16 * t + 16], t == 0, True)
                ins.then_inc(*tick("pe", "places", l))

            def rows_T(L, i, c, b):
                pe.wait_ge(*loads_of(L, L["rows"][0][b], L["rows"][1], i, c))
                pe.wait_ge(*steps_of(L, "xT_v", i, c - 1))
                pe.wait_ge(*steps_of(L, "xT_a", i, c - 1))
                pe.wait_ge(*steps_of(L, "hT_v", i, c - L["k"]))
                for k in range(KD):
                    ins = tp(PB[:, k // 4, 128 * (k % 4):128 * (k % 4) + 128], xb[:, b, 128 * k:128 * k + 128])
                ins.then_inc(L["S"]["xT_p"], 1)

            def gate_up(L, i, c, b):
                pe.wait_ge(*steps_of(L, "xT_a", i, c))
                pe.wait_ge(*steps_of(L, "xT_v", i, c))
                pe.wait_ge(*steps_of(L, "silu", i, c - L["k"]))
                pe.wait_ge(*steps_of(L, "hid", i, c - L["k"]))
                for m in range(2):
                    pe.wait_ge(*loads_of(L, L["land"][b][m], L["land_base"][b][m], i, c))
                    w = wslot[b][m].rearrange("p (k n) -> p k n", k=KD)
                    for k in range(KD):
                        ins = mm(PB[:, 2 + 2 * m + b, :], xT[:, b, 128 * k:128 * k + 128], w[:, k, :], k == 0, k == KD - 1)
                ins.then_inc(L["S"]["gu"], 1)

            def hidden_T(L, i, c, b, ahead):
                pe.wait_ge(*steps_of(L, "hid", i, c))
                pe.wait_ge(*steps_of(L, "xT_a", i, c + ahead))
                for k in range(KF):
                    ins = tp(PB[:, 0, 128 * k:128 * k + 128], hid[:, b, 128 * k:128 * k + 128])
                ins.then_inc(L["S"]["hT_p"], 1)

            def down(L, i, c, b):
                pe.wait_ge(*steps_of(L, "hT_v", i, c))
                pe.wait_ge(*steps_of(L, "y_a", i, c - 1))
                pe.wait_ge(*steps_of(L, "y_v", i, c - 1))
                pe.wait_ge(*loads_of(L, L["land"][b][2], L["land_base"][b][2], i, c))
                w = wslot[b][2].rearrange("p (k n) -> p k n", k=KF)
                for h in range(2):
                    for k in range(KF):
                        ins = mm(PB[:, 6 + h, :], hidT[:, b, 128 * k:128 * k + 128], w[:, k, 512 * h:512 * h + 512],
                                 k == 0, k == KF - 1)
                ins.then_inc(L["S"]["dn"], 1)

            def experts(l):
                for b in range(8):
                    if reader[b] is not None:
                        pe.wait_ge(*when(*reader[b]))
                    reader[b] = None
                L = base_loop[l]
                rows_T(L, None, 0, 0)
                gate_up(L, None, 0, 0)
                rows_T(L, None, 1, 1)
                hidden_T(L, None, 0, 0, 1)
                gate_up(L, None, 1, 1)
                with pe.Fori(0, half - 1) as i:
                    for n in (1, 2):
                        rows_T(L, i, n + 1, (n + 1) % 2)
                        down(L, i, n - 1, (n - 1) % 2)
                        hidden_T(L, i, n, n % 2, 1)
                        gate_up(L, i, n + 1, (n + 1) % 2)
                down(L, None, NE - 2, 0)
                hidden_T(L, None, NE - 1, 1, 0)
                down(L, None, NE - 1, 1)
                n_extra = nc.tensor.value_load(xtab[0:1, 7:8], min_val=0, max_val=NX)
                with pe.If(n_extra > 0):
                    X = extra_loop[l]
                    for step in ("hT_v", "y_a", "y_v"):
                        pe.wait_ge(*steps_of(L, step, None, NE - 1))
                    with pe.Fori(0, NX) as i:
                        rows_T(X, i, 0, 0)
                        gate_up(X, i, 0, 0)
                        hidden_T(X, i, 0, 0, 0)
                        down(X, i, 0, 0)
                pe.wait_ge(*when("y_all", l))

            def odd_keys_queries():
                for t in range(TILES):
                    pe.wait_ge(*when("ocn", t))
                    claim(0, "cqT", t)
                    for k in range(2):
                        tp(PB[:, 0, 128 * k:128 * k + 128], O[:, t, OCQ + 128 * k:OCQ + 128 * k + 128])
                    ins = tp(PB[:, 0, 256:384], O[:, t, OCKV:OCKV + 128])
                    ins.then_inc(*tick("pe", "cT", t))
                pe.wait_ge(sem("ld_odd"), 17 * 16)
                claim(1, "cqT", 3)
                tp(PB[:, 1, 0:128], cckv).then_inc(*tick("pe", "cT", 3))
                for t in range(TILES):
                    pe.wait_ge(*when("cqT", t))
                    for b in range(2):
                        claim(2 + b, "q_raw", t)
                        for k in range(2):
                            ins = mm(PB[:, 2 + b, 0:384], cqT[:, k, t * P:(t + 1) * P], qup[:, k, 384 * b:384 * b + 384],
                                     k == 0, k == 1)
                    ins.then_inc(*tick("pe", "q_up", t))
                    heads_T(("q_n", t), hd, "qT", t)
                for kt in range(4):
                    pe.wait_ge(*when("cqT", [0, 3, 1, 2][kt]))
                    for b in range(2):
                        claim(2 + b, "k_raw", kt)
                        ins = mm(PB[:, 2 + b, :], ckT[:, kt, :], kvup[:, 512 * b:512 * b + 512])
                    ins.then_inc(*tick("pe", "kv_up", kt))
                    heads_T(("k_n", kt), hd, "kT", kt)
                for t in range(TILES):
                    pe.wait_ge(*when("dqk", t))
                    pairs_T("dqT", t, lambda h: O[:, t, OQD + 128 * h:OQD + 128 * h + 128])
                    pairs_T("dkT", [0, 2, 3][t], lambda h: O[:, t, OKD + 128 * h:OKD + 128 * h + 128])
                pairs_T("dkT", 1, lambda h: cdk[:, 2 * h:2 * h + 2, :].rearrange("p m n -> p (m n)"))

            def heads_T(name, src, out, t):
                pe.wait_ge(*when(*name))
                for b in range(2):
                    claim(4 + b, out, t, b)
                    for h in range(4):
                        ins = tp(PB[0:96, 4 + b, 128 * h:128 * h + 128], src[:, 96 * (4 * b + h):96 * (4 * b + h) + 96])
                    ins.then_inc(*tick("pe", out + "_p", t, b))

            def pairs_T(out, t, src):
                b = 6 if out == "dqT" else 7
                claim(b, out, t)
                for h in range(4):
                    ins = tp(PB[:, b, 128 * h:128 * h + 128], src(h))
                ins.then_inc(*tick("pe", out + "_p", t))

            def attend():
                units = [(t, m) for t in range(TILES) for m in range(16)]

                def operands(u):
                    t, m = units[u]
                    ks = [0] if t == 0 else [1, 2, 3]
                    if m < 8:
                        q, kk = hTv[0:96, m, t * P:(t + 1) * P], kT[0:96, m, 128 * ks[0]:128 * ks[0] + 128 * len(ks)]
                        vs = [vC[:, k, m, :] for k in ks]
                    else:
                        h, r = (m - 8) // 2, 64 * (m % 2)
                        q = dqT[r:r + 64, h, t * P:(t + 1) * P]
                        kk = dkT[r:r + 64, h, 128 * ks[0]:128 * ks[0] + 128 * len(ks)]
                        vt = [O[:, 0, OVD:ODD], cdv.rearrange("p h n -> p (h n)"), O[:, 1, OVD:ODD], O[:, 2, OVD:ODD]]
                        vs = [vt[k][:, 128 * h:128 * h + 128] for k in ks]
                    return q, kk, vs, len(ks)

                def scores(u):
                    q, kk, vs, n = operands(u)
                    claim(u % 2, "prob", u)
                    mm(PB[:, u % 2, 0:128 * n], q, kk).then_inc(*tick("pe", "sc", u))

                def turn(u):
                    n = operands(u)[3]
                    pe.wait_ge(*when("prob", u))
                    claim(2 + u % 2, "probT", u)
                    for k in range(n):
                        ins = tp(PB[:, 2 + u % 2, 128 * k:128 * k + 128], prob[:, u % 2, 128 * k:128 * k + 128])
                    ins.then_inc(*tick("pe", "pT", u))

                def values(u):
                    vs = operands(u)[2]
                    pe.wait_ge(*when("probT", u))
                    claim(4 + u % 2, "ov", u)
                    w = 64 if units[u][1] < 8 else 128
                    for k, v in enumerate(vs):
                        ins = mm(PB[:, 4 + u % 2, 0:w], probT[:, u % 2, k, :], v, k == 0, k == len(vs) - 1)
                    ins.then_inc(*tick("pe", "pv", u))

                for s in ("act", "dve"):
                    pe.wait_ge(*when("end", s, "odd_prep"))
                scores(0)
                for u in range(48):
                    if u + 1 < 48:
                        scores(u + 1)
                    turn(u)
                    if u % 16:
                        values(u - 1)
                    if u % 16 == 15:
                        values(u)
                        t = u // 16
                        mixed_T(("omix1", t), lambda k: mix[:, 128 * k:128 * k + 128], t, 1)

            pe.wait_ge(sem("ld_const"), 32)
            pe.wait_ge(*when("scT"))
            mods(0)
            norm(0, 0)
            for g, tiles in enumerate(((0,), (1, 2))):
                for t in tiles:
                    for b in range(2):
                        pe.wait_ge(*when("hT", 0, 0, t, b))
                project(("ein", g), tiles, 7, EVEN)
                if g == 0:
                    pe.wait_ge(sem("ld_even"), 16 * 5)
                    pe.wait_ge(*when("SG0"))
                    pe.wait_ge(*when("SR0"))
                else:
                    pe.wait_ge(sem("ld_sg"), 8 * 16)
                    pe.wait_ge(*when("SG1"))
                    states_T("state_in", lambda d, j: stg[:, d, 128 * j:128 * j + 128], "ld_sr")
                    pe.wait_ge(*when("state_in", 1))
                for i in range(len(tiles)):
                    lora_T(g, i)
                for i, d in (((0, 0), (0, 1)), ((0, 0), (1, 0), (1, 1), (0, 1)))[g]:
                    gla(g, i, d)
                    rwkv(g, i, d)
                end("pe", f"units{g}")
                if g == 0:
                    states_T("state_out", lambda d, j: SR[:, d, j, :], ("S", 0, 0, 1, 1, 1))
                for i, t in enumerate(tiles):
                    even_out(g, i, t)
                end("pe", f"out_g{g}")
            for l in range(2):
                if l == 1:
                    mods(1)
                    norm(1, 0)
                    for t in range(TILES):
                        for b in range(2):
                            pe.wait_ge(*when("hT", 1, 0, t, b))
                    project(("oin",), (0, 1, 2), 4, ODD)
                    odd_keys_queries()
                    end("pe", "odd_prep")
                    attend()
                for t in range(TILES):
                    for b in range(2):
                        pe.wait_ge(*when("mT", l, t, b))
                project(("outp", l), (0, 1, 2), 2, D)
                end("pe", f"mixer{l}")
                norm(l, 1)
                router(l)
                experts(l)
                end("pe", f"moe{l}")

        @block.scalar
        def _(act):
            def step(ins, *name):
                ins.then_inc(*tick("act", *name))
                act.wait_ge(sem("act"), count["act"])

            def fn(out, in_, f, *name, **k):
                step(nc.scalar.activation(out, in_, f, **k), *name)

            def mods(l):
                for n in range(12):
                    act.wait_ge(*when("modp", l, n))
                    if n >= 2:
                        act.wait_ge(*(when("gb", l, n - 2, 1) if (n - 2) // 2 in (2, 5) else when("mt", l, n - 2)))
                    fn(rowb[0:2, 512 * (n % 2):512 * (n % 2) + 512], PB[0:2, n % 2, :], ACT.Copy, "modrow", l, n)
                end("act", f"mods{l}")

            def root(*name):
                act.wait_ge(*when("var", *name))
                n = known_n[name[0]]
                fn(small[:, 0:n], small[:, 0:n], ACT.Sqrt, "root", *name)

            def copies(name, tiles, chunks, width, dst):
                bank = 0
                for n in range(chunks):
                    ncol = min(512, width - 512 * n)
                    for i in range(len(tiles)):
                        if bank % 2 == 0:
                            act.wait_ge(*when(*name, "p", n, i))
                            fn(dst[:, i, 512 * n:512 * n + ncol], PB[:, bank % 4, 0:ncol], ACT.Copy, *name, "evac", n, i)
                        bank += 1

            def norm(l, s):
                for t in range(TILES):
                    if t:
                        act.wait_ge(*when("xnT", l, s, t - 1, 1))
                    act.wait_ge(*when("norm_in", l, s, t))
                    fn(xn, xv[:, t, :], ACT.Square, "sq", l, s, t, accum_out=small[:, 0:1])
                    root("norm", l, s, t)

            def gla(g, i, d):
                u = (g, i, d)
                la, t1 = tmpE[0][:, 0:256], tmpE[1][:, 0:256]
                act.wait_ge(*when("ga_z", *u))
                fn(t1, la, ACT.Abs)
                fn(t1, t1, ACT.Exp, scale=-1.0)
                fn(t1, t1, ACT.Ln, "ln", *u, bias=1.0)
                act.wait_ge(*when("gcum", *u))
                s = 1.0 / 16
                fn(tmpE[1][:, 0:256], PB[:, 1, 0:256], ACT.Exp, scale=s)
                fn(tmpE[1][:, 256:512], PB[:, 1, 0:256], ACT.Exp, scale=-s)
                fn(tmpE[2][:, 0:256], PB[:, 1, 256:512], ACT.Exp, "g_exp", *u, scale=s)
                fn(small[:, 16:20], PB[:, 2, 0:4], ACT.Exp, "g_dec", *u, scale=s)
                act.wait_ge(*when("gT", *u))
                fn(TA.rearrange("p a n -> p (a n)"), PB[:, 3, :], ACT.Copy, "gqkT", *u)

            def rwkv(g, i, d):
                u = (g, i, d)
                act.wait_ge(*when("r_zw", *u))
                fn(tmpE[0], tmpE[0], ACT.Sigmoid, "lw", *u)
                act.wait_ge(*when("r_za", *u))
                fn(tmpE[1], tmpE[1], ACT.Sigmoid, "aa", *u)
                act.wait_ge(*when("rcum", *u))
                fn(tokm[:, 0, :], PB[:, 5, :], ACT.Exp, "e_exc", *u, scale=-RW)
                fn(tokm[:, 1, :], PB[:, 4, :], ACT.Exp, scale=-RW)
                fn(tmpE[2], PB[:, 4, :], ACT.Exp, "e_inc", *u, scale=RW)
                fn(small[:, 32:40], PB[:, 6, 0:8], ACT.Exp, "e_wc", *u, scale=-RW)
                for hf in range(2):
                    w = (g, i, d, hf)
                    act.wait_ge(*when("tA", *w))
                    if hf:
                        act.wait_ge(*when("yy", g, i, d, 0, 1))
                    fn(TA.rearrange("p a n -> p (a n)"), PB[:, 0, :], ACT.Copy, "TA", *w)
                    for v in range(1, 6):
                        act.wait_ge(*when("t1", *w, v))
                        fn(T14.rearrange("p h n -> p (h n)"), PB[:, 6, :], ACT.Copy, "T1", *w, v)
                    for n in range(2):
                        act.wait_ge(*when("uu", *w, n))
                        r = CH * ((n, 1 - n)[d])
                        fn(UU[r:r + CH, :], PB[r:r + CH, 2, 0:256], ACT.Copy, "U", *w, n)

            known_n = {"norm": 1, "kk": 8, "og": 4, "oy": 8, "cq": 1, "ckv": 1, "qh": 8, "kh": 8, "dq": 8, "dk": 8, "dd": 4}

            def even_out(g, i):
                act.wait_ge(*when("end", "dve", f"units{g}"))
                fn(E[:, i, EG:EG + 512], E[:, i, EG:EG + 512], ACT.Silu, "siluG", g, i)
                root("og", g, i)
                root("oy", g, i)

            def rows_copy(L, i, c, b):
                act.wait_ge(*steps_of(L, "xT_p", i, c))
                act.wait_ge(*steps_of(L, "gu", i, c - L["k"]))
                nc.scalar.activation(xT[:, b, 0:512], PB[:, 0, :], ACT.Copy).then_inc(L["S"]["xT_a"], 1)

            def silu(L, i, c, b):
                act.wait_ge(*steps_of(L, "gu", i, c))
                act.wait_ge(*steps_of(L, "hid", i, c - L["k"]))
                nc.scalar.activation(sil[:, b, :], PB[:, 2 + b, :], ACT.Silu).then_inc(L["S"]["silu"], 1)

            def store(L, i, c, b, row):
                act.wait_ge(*steps_of(L, "dn", i, c))
                act.wait_ge(*loads_of(L, L["stores"][0][b], L["stores"][1], i, c - L["k"]))
                nc.scalar.activation(yb[:, b, 0:512], PB[:, 6, :], ACT.Copy).then_inc(L["S"]["y_a"], 1)
                act.wait_ge(*steps_of(L, "y_a", i, c))
                act.wait_ge(*steps_of(L, "y_v", i, c))
                act.dma_start(Yd[row, :], yb[:, b, :]).then_inc(L["stores"][0][b], 16)

            def experts(l):
                L = base_loop[l]
                rows_copy(L, None, 0, 0)
                silu(L, None, 0, 0)
                rows_copy(L, None, 1, 1)
                silu(L, None, 1, 1)
                with act.Fori(0, half - 1) as i:
                    for n in (1, 2):
                        rows_copy(L, i, n + 1, (n + 1) % 2)
                        store(L, i, n - 1, (n - 1) % 2, bass.ds(i * 2 * P + (n - 1) * P, P))
                        silu(L, i, n + 1, (n + 1) % 2)
                for n in (NE - 2, NE - 1):
                    store(L, None, n, n % 2, slice(n * P, (n + 1) * P))
                n_extra = nc.scalar.value_load(xtab[0:1, 7:8], min_val=0, max_val=NX)
                with act.If(n_extra > 0):
                    X = extra_loop[l]
                    for b in range(2):
                        act.wait_ge(*loads_of(L, y_st[b], L["stores"][1], None, NE - 2 + b))
                    with act.Fori(0, NX) as i:
                        rows_copy(X, i, 0, 0)
                        silu(X, i, 0, 0)
                        store(X, i, 0, 0, bass.ds(i * P + NE * P, P))
                    act.wait_ge(*loads_of(X, X["stores"][0][0], X["stores"][1], None, NX - 1))
                for b in range(2):
                    act.wait_ge(*loads_of(L, y_st[b], L["stores"][1], None, NE - 2 + b))
                fn(small[:, 254:255], small[:, 75:76], ACT.Copy, "y_all", l)

            act.wait_ge(sem("ld_const"), 32)
            act.wait_ge(*when("zeros"))
            act.dma_start(Xd.rearrange("(b p) d -> p b d", p=P), bc(zeros, 1, NE + NX)).then_inc(sem("xd_zero"), 16)
            act.dma_start(Yd[NE * P:ROWS, :].rearrange("(b p) d -> p b d", p=P), bc(zeros, 1, NX)).then_inc(sem("xd_zero"), 16)
            fn(scT[:, :], cols[:, COL_C:COL_C + 16], ACT.Silu, "scT")
            mods(0)
            norm(0, 0)
            for g, tiles in enumerate(((0,), (1, 2))):
                if g:
                    meet(act, "act", "out_g0")
                copies(("ein", g), tiles, 7, EVEN, E)
                for i in range(len(tiles)):
                    act.wait_ge(*when("e_ready", g, i))
                    fn(E[:, i, EWL:EWL + 128], E[:, i, EWL:EWL + 128], ACT.Tanh)
                    fn(E[:, i, EGL:EGL + 128], E[:, i, EGL:EGL + 128], ACT.Sigmoid, "lora", g, i)
                    root("kk", g, i)
                for i, d in (((0, 0), (0, 1)), ((0, 0), (1, 0), (1, 1), (0, 1)))[g]:
                    gla(g, i, d)
                    rwkv(g, i, d)
                end("act", f"units{g}")
                for i in range(len(tiles)):
                    even_out(g, i)
                end("act", f"out_g{g}")
            for l in range(2):
                if l == 1:
                    mods(1)
                    norm(1, 0)
                    copies(("oin",), (0, 1, 2), 4, ODD, O)
                    act.wait_ge(*when("lamsum"))
                    fn(small[:, 60:62], small[:, 60:62], ACT.Exp, "lamexp")
                    for t in range(TILES):
                        root("cq", t)
                        root("ckv", t)
                    for t in range(TILES):
                        root("qh", t)
                    for kt in range(4):
                        root("kh", kt)
                    for t in range(TILES):
                        root("dq", t)
                        root("dk", t)
                    end("act", "odd_prep")
                    for u in range(48):
                        m = u % 16
                        n = 128 if u < 16 else 384
                        act.wait_ge(*when("nmax", u))
                        if u >= 2:
                            act.wait_ge(*when("pT", u - 2))
                            act.wait_ge(*when("ov", u - 2))
                        scale = (96 if m < 8 else 64) ** -0.5
                        fn(prob[:, u % 2, 0:n], PB[:, u % 2, 0:n], ACT.Exp, "prob", u,
                           bias=small[:, 64 + u % 2:65 + u % 2], scale=scale, accum_out=small[:, 66 + u % 2:67 + u % 2])
                        if m == 15:
                            root("dd", u // 16)
                end("act", f"mixer{l}")
                norm(l, 1)
                act.wait_ge(*when("rt", l))
                fn(small[:, 128:176], PB[:, 0, 0:48], ACT.Sigmoid, "scores", l)
                for t in range(TILES):
                    for b in range(2):
                        act.wait_ge(*when("htok_p", l, t, b))
                        fn(htok[:, t, 512 * b:512 * b + 512], PB[:, 2 + (2 * t + b) % 4, :], ACT.Copy,
                           "htok_c", l, t, b)
                    seen[("htok", l, t)] = ("act", count["act"])
                act.wait_ge(*when("rows", l))
                experts(l)
                end("act", f"moe{l}")

        @block.vector
        def _(dve):
            V = nc.vector

            def step(ins, *name):
                ins.then_inc(*tick("dve", *name))
                dve.wait_ge(sem("dve"), count["dve"])

            def tt(out, a, b, op, *name):
                step(V.tensor_tensor(out, a, b, op), *name)

            def ts(out, a, s1, s2, op0, op1, *name):
                step(V.tensor_scalar(out, a, s1, s2, op0, op1) if op1 is not None else
                     V.tensor_scalar(out, a, s1, None, op0), *name)

            def stt(out, a, s, b, op0, op1, *name):
                step(V.scalar_tensor_tensor(out=out, in0=a, scalar=s, in1=b, op0=op0, op1=op1), *name)

            def cp(out, a, *name):
                step(V.tensor_copy(out, a), *name)

            def red(out, a, *name, op=ALU.add):
                step(V.tensor_reduce(out, a, AX.X, op), *name)

            def rstd(n, scale, eps, *name):
                ts(small[:, 0:n], small[:, 0:n], scale, eps, ALU.mult, ALU.add, "var", *name)
                dve.wait_ge(*when("root", *name))
                step(V.reciprocal(small[:, 0:n], small[:, 0:n]))
                return small[:, 0:n]

            def mods(l):
                dve.wait_ge(sem("ld_bgate"), 16 * 4 * (l + 1))
                for n in range(12):
                    kind, half = n // 2, n % 2
                    if kind in (2, 5):
                        for c in range(2):
                            dve.wait_ge(*when("gb", l, n, c))
                            gv = gatev[:, c, kind // 3, 512 * half:512 * half + 512]
                            tt(gv, gv, PB[:, 2 + c, :], ALU.add, "gadd", l, n, c)
                    else:
                        dve.wait_ge(*when("mt", l, n))
                        tt(modTv[:, 4 * n:4 * n + 4, :], PB[:, 4 + n % 2, 0:8].rearrange("p (j c) -> p j c", c=2),
                           bc(cols[:, COL_BM + 48 * l + 4 * n:COL_BM + 48 * l + 4 * n + 4], 2, 2), ALU.add, "modT", l, n)
                for s in range(2):
                    sc = modTv[:, 24 * s + 8:24 * s + 16, :]
                    ng = bc(cols[:, COL_NG + 8 * (2 * l + s):COL_NG + 8 * (2 * l + s) + 8], 2, 2)
                    stt(mulAv[:, s, :, :], sc, 1.0, ng, ALU.add, ALU.mult)
                end("dve", f"mods{l}")

            def norm(l, s):
                for t in range(TILES):
                    ts(small[:, 1:2], cols[:, 0:1], 0.0, None, ALU.mult, None, "norm_in", l, s, t)
                    dve.wait_ge(*when("sq", l, s, t))
                    r = rstd(1, 1.0 / D, EPS, "norm", l, s, t)
                    ts(xn, xv[:, t, :], r, None, ALU.mult, None, "xn", l, s, t)
                    cond = 0 if t == 0 else 1
                    for b in range(2):
                        dve.wait_ge(*when("xnT", l, s, t, b))
                        for k in range(4):
                            kk = 4 * b + k
                            ts(hTv[:, kk, t * P:(t + 1) * P], PB[:, 6 + b, 128 * k:128 * k + 128],
                               mulAv[:, s, kk, cond:cond + 1], modTv[:, 24 * s + kk, cond:cond + 1],
                               ALU.mult, ALU.add, *(("hT", l, s, t, b) if k == 3 else ()))

            def copies(name, tiles, chunks, width, dst):
                bank = 0
                for n in range(chunks):
                    ncol = min(512, width - 512 * n)
                    for i in range(len(tiles)):
                        if bank % 2:
                            dve.wait_ge(*when(*name, "p", n, i))
                            cp(dst[:, i, 512 * n:512 * n + ncol], PB[:, bank % 4, 0:ncol], *name, "evac", n, i)
                        bank += 1

            def h8(ap, h=8):
                return ap.rearrange("p (h n) -> p h n", h=h)

            def prepare(g, i):
                tmp = tmpE[0]
                dve.wait_ge(*when("lora_T", g, i))
                for j, n in ((0, 128), (1, 128), (2, 128), (3, 32)):
                    cp(loT[0:n, i, j, :], PB[0:n, 0, 128 * j:128 * j + 128], *(("loT", g, i) if j == 3 else ()))
                kk = kkn[:, i, :]
                kb, rr = E[:, i, EKB:EKB + 512], E[:, i, ER:ER + 512]
                tt(kk, kb, R(rowsE, "rw_kk"), ALU.mult)
                tt(tmp, kk, kk, ALU.mult)
                red(small[:, 0:8], h8(tmp))
                r = rstd(8, 1.0, EPS, "kk", g, i)
                tt(h8(kk), h8(kk), bc(r, 2, 64), ALU.mult)
                tt(tmp, rr, kb, ALU.mult)
                tt(tmp, tmp, R(rowsE, "rw_rk"), ALU.mult)
                red(bon[:, i, :], h8(tmp))

            def gla(g, i, d, first):
                u = (g, i, d)
                la, t1 = tmpE[0][:, 0:256], tmpE[1][:, 0:256]
                q, k = E[:, i, EQ:EQ + 256], E[:, i, EK_:EK_ + 256]
                dve.wait_ge(*when("za", *u))
                tt(la, PB[:, 0, 0:256], R(rowsE, "gla_a_b", 256 * d, 256), ALU.add, "ga_z", *u)
                dve.wait_ge(*when("ln", *u))
                stt(la, la, 0.0, t1, ALU.min, ALU.subtract, "la", *u)
                dve.wait_ge(*when("g_exp", *u))
                stt(tokm[:, 0, 0:256], q, 64 ** -0.5, tmpE[1][:, 0:256], ALU.mult, ALU.mult)
                tt(tokm[:, 1, 0:256], k, tmpE[1][:, 256:512], ALU.mult)
                tt(tokm[:, 2, 0:256], k, tmpE[2][:, 0:256], ALU.mult, "gk", *u)
                dve.wait_ge(*when("g_dec", *u))
                dve.wait_ge(*when("gA", *u))
                m = C("le") if d == 0 else C("ge")
                for b in range(2):
                    tt(G4[:, b:4:2, 0:128], PB[:, 4 + b, 0:256].rearrange("p (j n) -> p j n", j=2), bc(m, 1, 2),
                       ALU.mult, *(("gatt", *u) if b else ()))
                for n, c in enumerate((0, 1) if d == 0 else (1, 0)):
                    dve.wait_ge(*when("gu", *u, n))
                    tt(tmpE[1].rearrange("p (j n) -> p j n", j=2), PB[:, 7, :].rearrange("p (j n) -> p j n", j=2),
                       bc(C("bdg"), 1, 2), ALU.mult)
                    for j in range(2):
                        stt(SG[:, d, j, :], SG[:, d, j, :], small[:, 16 + 2 * j + c:17 + 2 * j + c],
                            tmpE[1][:, 256 * j:256 * j + 256], ALU.mult, ALU.add, *(("gS", *u, n) if j else ()))
                if first:
                    cp(oG[:, i, :], PB[:, 6, :], "gout", *u)
                else:
                    tt(oG[:, i, :], oG[:, i, :], PB[:, 6, :], ALU.add, "gout", *u)

            def rwkv(g, i, d, first):
                u = (g, i, d)
                kb, rr = E[:, i, EKB:EKB + 512], E[:, i, ER:ER + 512]
                dve.wait_ge(*when("zw", *u))
                tt(tmpE[0], PB[:, d, :], R(rowsE, "rw_w0", 512 * d, 512), ALU.add, "r_zw", *u)
                dve.wait_ge(*when("zr", *u))
                tt(tmpE[1], PB[:, 2 + d, :], R(rowsE, "rw_a0", 512 * d, 512), ALU.add, "r_za", *u)
                dve.wait_ge(*when("e_wc", *u))
                tt(tokm[:, 0, :], tokm[:, 0, :], kkn[:, i, :], ALU.mult)
                tt(tokm[:, 1, :], tokm[:, 1, :], rr, ALU.mult)
                tt(tokm[:, 2, :], tmpE[1], kkn[:, i, :], ALU.mult)
                tt(tokm[:, 2, :], tokm[:, 2, :], tmpE[2], ALU.mult)
                stt(tokm[:, 3, :], tmpE[1], -1.0, R(rowsE, "rw_ka"), ALU.add, ALU.mult)
                stt(tokm[:, 3, :], tokm[:, 3, :], 1.0, kb, ALU.add, ALU.mult)
                tt(tokm[:, 3, :], tokm[:, 3, :], tmpE[2], ALU.mult, "tokm", *u)
                strict = cst[:, _C["lt" if d == 0 else "gt"][0]:_C["lt" if d == 0 else "gt"][0] + 256]
                lvl, lvl_t = (C("lvl0"), C("lvl1")) if d == 0 else (C("lvl1"), C("lvl0"))
                I4 = bc(ident, 1, 4)
                for hf in range(2):
                    w = (g, i, d, hf)
                    dve.wait_ge(*when("tB", *w))
                    cp(TB.rearrange("p a n -> p (a n)"), PB[:, 1, :], "TB", *w)
                    dve.wait_ge(*when("gramL", *w))
                    tt(G4.rearrange("p h (a n) -> p (h a) n", a=2), PB[:, 2:6, :].rearrange("p h (a n) -> p (h a) n", a=2),
                       bc(strict, 1, 8), ALU.mult, "G4", *w)
                    for b in range(2):
                        tt(T14[:, b:4:2, :], PB[:, 6 + b, 0:256].rearrange("p (j n) -> p j n", j=2),
                           bc(lvl_t[:, 0:128], 1, 2), ALU.mult, *(("X0", *w) if b else ()))
                    tt(X4, I4, T14, ALU.subtract)
                    tt(T14, G4[:, :, 0:128], bc(lvl[:, 0:128], 1, 4), ALU.mult)
                    tt(XT4, I4, T14, ALU.subtract, "XT0", *w)
                    for v in range(1, 6):
                        if v == 1:
                            tt(LJ4, G4[:, :, 0:128], bc(lvl[:, 128:256], 1, 4), ALU.mult, "LJ", *w, 1)
                        if v < 5:
                            dve.wait_ge(*when("t1", *w, v))
                            tt(LJ4, G4[:, :, 0:128], bc(lvl[:, 128 * v + 128:128 * v + 256], 1, 4),
                               ALU.mult, "LJ", *w, v + 1)
                            dve.wait_ge(*when("dx", *w, v))
                            tt(X4, X4, PB[:, 7, :].rearrange("p (h n) -> p h n", h=4), ALU.subtract, "X", *w, v)
                        dve.wait_ge(*when("dxt", *w, v))
                        tt(XT4, XT4, PB[:, 0, :].rearrange("p (h n) -> p h n", h=4), ALU.subtract, "XT", *w, v)
                    for n in range(2):
                        c = (n, 1 - n)[d]
                        r = CH * c
                        dve.wait_ge(*when("rh", *w, n))
                        ts(RH[r:r + CH, :], PB[r:r + CH, 1, 0:256], -1.0, None, ALU.mult, None, "RH", *w, n)
                        dve.wait_ge(*when("su", *w, n))
                        s2 = SR[:, d, 2 * hf:2 * hf + 2, :]
                        dve.wait_ge(*when("yy", *w, n))
                        tt(s2, s2, PB[:, 6 + c, 0:256].rearrange("p (j n) -> p j n", j=2), ALU.add)
                        tt(s2, s2, bc(small[:, 32 + 4 * hf + c:32 + 4 * hf + c + 3:2], 2, 128), ALU.mult)
                        tt(s2, s2, bc(C("bdr"), 1, 2), ALU.mult, "S", *w, n)
                        yo = yR[r:r + CH, i, 256 * hf:256 * hf + 256]
                        if first:
                            cp(yo, PB[r:r + CH, 4, 0:256], "Y", *w, n)
                        else:
                            tt(yo, yo, PB[r:r + CH, 4, 0:256], ALU.add, "Y", *w, n)

            def even_out(g, i):
                dve.wait_ge(sem("ld_late"), 32 * (g + 1))
                o, y, tmp = oG[:, i, :], yR[:, i, :], tmpE[0]
                tt(tmp, o, o, ALU.mult)
                red(small[:, 0:4], h8(tmp, 4))
                r = rstd(4, 1.0 / 128, EPS, "og", g, i)
                tt(h8(o, 4), h8(o, 4), bc(r, 2, 128), ALU.mult)
                tt(h8(o, 4), h8(o, 4), bc(R(rowsG, "gla_o_g"), 1, 4), ALU.mult)
                dve.wait_ge(*when("siluG", g, i))
                tt(o, o, E[:, i, EG:EG + 512], ALU.mult)
                red(small[:, 8:16], h8(y))
                ts(small[:, 8:16], small[:, 8:16], 1.0 / 64, None, ALU.mult, None)
                tt(h8(y), h8(y), bc(small[:, 8:16], 2, 64), ALU.subtract)
                tt(tmp, y, y, ALU.mult)
                red(small[:, 0:8], h8(tmp))
                r = rstd(8, 1.0 / 64, GN_EPS, "oy", g, i)
                tt(h8(y), h8(y), bc(r, 2, 64), ALU.mult)
                tt(y, y, R(rowsG, "rw_gn_g"), ALU.mult)
                tt(y, y, R(rowsG, "rw_gn_b"), ALU.add)
                tt(h8(tmp), h8(E[:, i, EVB:EVB + 512]), bc(bon[:, i, :], 2, 64), ALU.mult)
                tt(y, y, tmp, ALU.add)
                dve.wait_ge(*when("gm", g, i))
                tt(y, y, PB[:, 5, :], ALU.mult, "omix", g, i)

            def mixed(l, t):
                for b in range(2):
                    dve.wait_ge(*when("mixT", l, t, b))
                    cp(hTv[:, 4 * b:4 * b + 4, t * P:(t + 1) * P], PB[:, 6 + b, :].rearrange("p (k n) -> p k n", k=4),
                       "mT", l, t, b)

            def residual(l):
                bank = 0
                for n in range(2):
                    for t in range(TILES):
                        dve.wait_ge(*when("outp", l, "p", n, t))
                        gv = gatev[:, 0 if t == 0 else 1, 0, 512 * n:512 * n + 512]
                        tmp = xn[:, 0:512]
                        tt(tmp, PB[:, bank % 4, :], gv, ALU.mult, "outp", l, "evac", n, t)
                        xs = xv[:, t, 512 * n:512 * n + 512]
                        tt(xs, xs, tmp, ALU.add)
                        bank += 1

            def route(l):
                at = [0]

                def w(n):
                    at[0] += n
                    return route_w[:, at[0] - n:at[0]]

                sel, c2, gsc, grank, big = w(48), w(192), w(12), w(48), w(768)
                rank, f0, f1, gw, row, ge = w(48), w(48), w(48), w(48), w(48), w(48)
                cum, xbk, off, ov, rec = w(16), w(16), w(16), w(16), w(4)
                c1 = big[:, 0:192]
                v4 = lambda a: a.rearrange("p (g e) -> p g e", e=4)
                v44 = lambda a: a.rearrange("p (g e j) -> p g e j", e=4, j=4)
                v16 = lambda a: a.rearrange("p (t e) -> p t e", e=16)
                s = small[:, 128:176]
                tie = bc(C("tie").rearrange("p (e j) -> p e j", e=4), 1, 12)
                dve.wait_ge(sem("ld_router"), 32)
                dve.wait_ge(*when("scores", l))
                tt(v16(sel), v16(s), bc(brout[:, :], 1, TILES), ALU.add)
                tt(v44(c1), bc(v4(sel), 2, 4), bc(v4(sel), 3, 4), ALU.is_gt)
                tt(v44(c2), bc(v4(sel), 2, 4), bc(v4(sel), 3, 4), ALU.is_equal)
                tt(v44(c2), v44(c2), tie, ALU.mult)
                tt(c1, c1, c2, ALU.add)
                red(rank, c1.rearrange("p (g j) -> p g j", j=4))
                ts(mask, rank, 1.5, None, ALU.is_lt, None)
                tt(sel, sel, mask, ALU.mult)
                red(gsc, v4(sel))
                tt(v44(c1[:, 0:48]), bc(v4(gsc), 2, 4), bc(v4(gsc), 3, 4), ALU.is_gt)
                tt(v44(c2[:, 0:48]), bc(v4(gsc), 2, 4), bc(v4(gsc), 3, 4), ALU.is_equal)
                tt(v44(c2[:, 0:48]), v44(c2[:, 0:48]), tie[:, 0:TILES], ALU.mult)
                tt(c1[:, 0:48], c1[:, 0:48], c2[:, 0:48], ALU.add)
                red(grank[:, 0:12], c1[:, 0:48].rearrange("p (g j) -> p g j", j=4))
                ts(grank[:, 0:12], grank[:, 0:12], 0.5, None, ALU.is_lt, None)
                tt(v4(mask), v4(mask), bc(grank[:, 0:12], 2, 4), ALU.mult, "mask", l)
                tt(gw, mask, s, ALU.mult)
                red(rec[:, 0:TILES], v16(gw))
                step(V.reciprocal(rec[:, 0:TILES], rec[:, 0:TILES]))
                tt(v16(gw), v16(gw), bc(rec[:, 0:TILES], 2, 16), ALU.mult)
                dve.wait_ge(sem("ld_cmoe"), 16 * (l + 1))
                tri = M("tri16").rearrange("p (e j) -> p e j", e=16)
                tt(big.rearrange("p (t e j) -> p t e j", t=TILES, e=16), bc(v16(mask), 2, 16), bc(tri, 1, TILES), ALU.mult)
                red(rank, big.rearrange("p (g j) -> p g j", j=16))
                ts(f0, rank, 0.5, None, ALU.is_lt, None)
                tt(f0, f0, mask, ALU.mult)
                tt(f1, mask, f0, ALU.subtract)
                dve.wait_ge(*when("places", l))
                cp(cum, PB[:, 1, 48:64])
                ts(xbk, cum, CAP + 0.5, None, ALU.is_ge, None)
                ts(ov, cum, 2 * CAP + 0.5, None, ALU.is_ge, None)
                tt(xbk, xbk, ov, ALU.add)
                tt(big[:, 0:256].rearrange("p (e j) -> p e j", e=16), bc(xbk, 1, 16), tri, ALU.mult)
                red(off, big[:, 0:256].rearrange("p (e j) -> p e j", e=16))
                tt(cum, off, xbk, ALU.add)
                ts(ov, off, float(CAP), float((NE - 1) * P), ALU.mult, ALU.add)
                tt(ov, ov, M("row0"), ALU.subtract)
                ts(ge, PB[:, 1, 0:48], CAP - 0.5, None, ALU.is_ge, None)
                tt(v16(row), PB[:, 1, 0:48].rearrange("p (t e) -> p t e", e=16), bc(M("row0"), 1, TILES), ALU.add,
                   "place", l)
                tt(v16(ge), v16(ge), bc(ov, 1, TILES), ALU.mult)
                tt(row, row, ge, ALU.add)
                for ch, f in enumerate((f0, f1)):
                    tt(c2[:, 0:48], f, gw, ALU.mult)
                    red(gatek[:, 3 * ch:3 * ch + 3], v16(c2[:, 0:48]))
                    tt(f, f, row, ALU.mult)
                    red(rec[:, 0:3], v16(f))
                    cp(rows_i[:, 3 * ch:3 * ch + 3], rec[:, 0:3])
                tt(big[:, 0:80].rearrange("p (b e) -> p b e", e=16), bc(cum, 1, NX),
                   M("extra").rearrange("p (b e) -> p b e", e=16), ALU.is_le)
                red(off[:, 0:NX], big[:, 0:80].rearrange("p (b e) -> p b e", e=16))
                ts(off[:, 0:NX], off[:, 0:NX], float(NE - 1), None, ALU.min, None)
                cp(off[:, 7:8], cum[:, 15:16])
                step(V.memset(off[:, NX:7], 0.0))
                cp(xtab[:, :], off[:, 0:8], "rows", l)

            def rows_copy(L, i, c, b):
                dve.wait_ge(*steps_of(L, "xT_p", i, c))
                dve.wait_ge(*steps_of(L, "gu", i, c - L["k"]))
                V.tensor_copy(xT[:, b, 512:1024], PB[:, 1, :]).then_inc(L["S"]["xT_v"], 1)

            def hidden(L, i, c, b):
                dve.wait_ge(*steps_of(L, "silu", i, c))
                dve.wait_ge(*steps_of(L, "hT_p", i, c - L["k"]))
                V.tensor_tensor(hid[:, b, :], sil[:, b, :], PB[:, 4 + b, :], ALU.mult).then_inc(L["S"]["hid"], 1)

            def hidden_copy(L, i, c, b):
                dve.wait_ge(*steps_of(L, "hT_p", i, c))
                dve.wait_ge(*steps_of(L, "dn", i, c - L["k"]))
                V.tensor_copy(hidT[:, b, :], PB[:, 0, :]).then_inc(L["S"]["hT_v"], 1)

            def out_copy(L, i, c, b):
                dve.wait_ge(*steps_of(L, "dn", i, c))
                dve.wait_ge(*loads_of(L, L["stores"][0][b], L["stores"][1], i, c - L["k"]))
                V.tensor_copy(yb[:, b, 512:1024], PB[:, 7, :]).then_inc(L["S"]["y_v"], 1)

            def experts(l):
                L = base_loop[l]
                rows_copy(L, None, 0, 0)
                hidden(L, None, 0, 0)
                rows_copy(L, None, 1, 1)
                hidden_copy(L, None, 0, 0)
                hidden(L, None, 1, 1)
                with dve.Fori(0, half - 1) as i:
                    for n in (1, 2):
                        rows_copy(L, i, n + 1, (n + 1) % 2)
                        out_copy(L, i, n - 1, (n - 1) % 2)
                        hidden_copy(L, i, n, n % 2)
                        hidden(L, i, n + 1, (n + 1) % 2)
                out_copy(L, None, NE - 2, 0)
                hidden_copy(L, None, NE - 1, 1)
                out_copy(L, None, NE - 1, 1)
                n_extra = nc.vector.value_load(xtab[0:1, 7:8], min_val=0, max_val=NX)
                with dve.If(n_extra > 0):
                    X = extra_loop[l]
                    for b in range(2):
                        dve.wait_ge(*loads_of(L, y_st[b], L["stores"][1], None, NE - 2 + b))
                    with dve.Fori(0, NX) as i:
                        rows_copy(X, i, 0, 0)
                        hidden(X, i, 0, 0)
                        hidden_copy(X, i, 0, 0)
                        out_copy(X, i, 0, 0)
                for t in range(TILES):
                    dve.wait_ge(sem(f"combined{t}"), 32 * (l + 1))
                    y0, y1 = yg[:, t, :], yg[:, 3 + t, :]
                    ts(y0, y0, gatek[:, t:t + 1], None, ALU.mult, None)
                    stt(y0, y1, gatek[:, 3 + t:4 + t], y0, ALU.mult, ALU.add)
                    tt(y0, y0, gatev[:, 0 if t == 0 else 1, 1, :], ALU.mult)
                    tt(xv[:, t, :], xv[:, t, :], y0, ALU.add, "x_moe", l, t)

            def rope(v, t, kind, nh, tmp):
                w = 32 if kind == "c" else 64
                q = w // 4
                cos = bc(C("cos" + kind, w * (t - 1), w), 1, nh)
                sin = C("sin" + kind, w * (t - 1), w).rearrange("p (a b q) -> p a b q", a=2, b=2)
                for a in range(2):
                    for b in range(2):
                        o = a * 2 * q + b * q
                        src = a * 2 * q + (1 - b) * q
                        tt(tmp[:, :, o:o + q], v[:, :, src:src + q], bc(sin[:, a, b, :], 1, nh), ALU.mult)
                tt(v, v, cos, ALU.mult)
                tt(v, v, tmp, ALU.add)

            def head_norm(v, tmp, nh, width, gain, *name):
                tt(tmp, v, v, ALU.mult)
                red(small[:, 0:nh], tmp)
                r = rstd(nh, 1.0 / width, EPS, *name)
                tt(v, v, bc(r, 2, width), ALU.mult)
                tt(v, v, bc(gain, 1, nh), ALU.mult)

            def odd_prepare():
                dve.wait_ge(sem("ld_odd"), 17 * 16)
                lam = R(rowsO, "diff_lam").rearrange("p (a b n) -> p a b n", a=2, b=2)
                lt_ = hd[:, 0:128].rearrange("p (a n) -> p a n", a=2)
                tt(lt_, lam[:, :, 0, :], lam[:, :, 1, :], ALU.mult)
                red(small[:, 60:62], lt_, "lamsum")
                dve.wait_ge(*when("lamexp"))
                tt(small[:, 62:63], small[:, 61:62], small[:, 60:61], ALU.subtract)
                ts(small[:, 62:63], small[:, 62:63], -LAM_INIT, None, ALU.add, None)
                for t in range(TILES):
                    for c0, w, gn, nm in ((OCQ, 256, "mla_qa_g", "cq"), (OCKV, 128, "mla_kva_g", "ckv")):
                        v = O[:, t, c0:c0 + w]
                        tt(hd[:, 0:w], v, v, ALU.mult)
                        red(small[:, 0:1], hd[:, 0:w])
                        r = rstd(1, 1.0 / w, EPS, nm, t)
                        stt(v, v, r, R(rowsO, gn), ALU.mult, ALU.mult, *(("ocn", t) if nm == "ckv" else ()))
                for t in range(4):
                    dve.wait_ge(*when("cT", t))
                    if t < 3:
                        cp(cqT[:, :, t * P:(t + 1) * P], PB[:, 0, 0:256].rearrange("p (k n) -> p k n", k=2))
                        cp(ckT[:, [0, 2, 3][t], :], PB[:, 0, 256:384], "cqT", t)
                    else:
                        cp(ckT[:, 1, :], PB[:, 1, 0:128], "cqT", 3)
                hv, hv2 = h8(hd), h8(hd2)
                for t in range(TILES):
                    dve.wait_ge(*when("q_up", t))
                    if t:
                        dve.wait_ge(*when("qT_p", t - 1, 1))
                    for b in range(2):
                        cp(hd[:, 384 * b:384 * b + 384], PB[:, 2 + b, 0:384], *(("q_raw", t) if b else ()))
                    head_norm(hv, hv2, 8, 96, R(rowsO, "mla_qn_g"), "qh", t)
                    if t:
                        rope(hv[:, :, 64:96], t, "c", 8, hv2[:, :, 0:32])
                    step(V.tensor_copy(hd2[:, 0:8], hd[:, 0:8]), "q_n", t)
                    for b in range(2):
                        dve.wait_ge(*when("qT_p", t, b))
                        cp(hTv[0:96, 4 * b:4 * b + 4, t * P:(t + 1) * P],
                           PB[0:96, 4 + b, :].rearrange("p (k n) -> p k n", k=4), "qT", t, b)
                for kt in range(4):
                    dve.wait_ge(*when("kv_up", kt))
                    t = [0, None, 1, 2][kt]
                    kr = ckr if kt == 1 else O[:, t, OKR:OKR + 32]
                    for b in range(2):
                        src = PB[:, 2 + b, :].rearrange("p (h n) -> p h n", h=4)
                        cp(hv[:, 4 * b:4 * b + 4, 0:64], src[:, :, 0:64])
                        cp(vC[:, kt, 4 * b:4 * b + 4, :], src[:, :, 64:128], *(("k_raw", kt) if b else ()))
                    cp(hv[:, :, 64:96], bc(kr, 1, 8))
                    head_norm(hv, hv2, 8, 96, R(rowsO, "mla_kn_g"), "kh", kt)
                    if kt >= 2:
                        rope(hv[:, :, 64:96], t, "c", 8, hv2[:, :, 0:32])
                    step(V.tensor_copy(hd2[:, 0:8], hd[:, 0:8]), "k_n", kt)
                    for b in range(2):
                        dve.wait_ge(*when("kT_p", kt, b))
                        cp(kT[0:96, 4 * b:4 * b + 4, 128 * kt:128 * kt + 128],
                           PB[0:96, 4 + b, :].rearrange("p (k n) -> p k n", k=4), "kT", kt, b)
                tmp = h8(hd[:, 0:512])
                for t in range(TILES):
                    qd, kd = h8(O[:, t, OQD:OQD + 512]), h8(O[:, t, OKD:OKD + 512])
                    head_norm(qd, tmp, 8, 64, R(rowsO, "diff_qn_g"), "dq", t)
                    head_norm(kd, tmp, 8, 64, R(rowsO, "diff_kn_g"), "dk", t)
                    if t:
                        rope(qd, t, "d", 8, tmp)
                        rope(kd, t, "d", 8, tmp)
                    else:
                        cp(hd2[:, 0:8], hd[:, 0:8], "caches")
                    cp(hd2[:, 8:16], hd[:, 0:8], "dqk", t)
                for t in (0, 1, 2, 3):
                    if t < 3:
                        dve.wait_ge(*when("dqT_p", t))
                        cp(dqT[:, :, t * P:(t + 1) * P], PB[:, 6, :].rearrange("p (k n) -> p k n", k=4), "dqT", t)
                    kt = [0, 2, 3, 1][t]
                    dve.wait_ge(*when("dkT_p", kt))
                    cp(dkT[:, :, 128 * kt:128 * kt + 128], PB[:, 7, :].rearrange("p (k n) -> p k n", k=4), "dkT", kt)
                end("dve", "odd_prep")

            def attend():
                def top(u):
                    n = 128 if u < 16 else 384
                    dve.wait_ge(*when("sc", u))
                    if u >= 2:
                        dve.wait_ge(*when("prob", u - 2))
                    m = small[:, 64 + u % 2:65 + u % 2]
                    red(m, PB[:, u % 2, 0:n], op=ALU.max)
                    ts(m, m, -((96 if u % 16 < 8 else 64) ** -0.5), None, ALU.mult, None, "nmax", u)

                def turned(u):
                    n = 128 if u < 16 else 384
                    dve.wait_ge(*when("pT", u))
                    cp(probT[:, u % 2, :, :].rearrange("p k n -> p (k n)")[:, 0:n], PB[:, 2 + u % 2, 0:n], "probT", u)

                def out(u):
                    t, m = u // 16, u % 16
                    dve.wait_ge(*when("pv", u))
                    rec = small[:, 68:69]
                    step(V.reciprocal(rec, small[:, 66 + u % 2:67 + u % 2]))
                    if m < 8:
                        ts(mix[:, 64 * m:64 * m + 64], PB[:, 4 + u % 2, 0:64], rec, None, ALU.mult, None, "ov", u)
                        return
                    o = mix[:, 512 + 128 * ((m - 8) // 2):640 + 128 * ((m - 8) // 2)]
                    if m % 2 == 0:
                        ts(o, PB[:, 4 + u % 2, 0:128], rec, None, ALU.mult, None, "ov", u)
                    else:
                        tt(rec, rec, small[:, 62:63], ALU.mult)
                        stt(o, PB[:, 4 + u % 2, 0:128], rec, o, ALU.mult, ALU.add, "ov", u)

                top(0)
                for u in range(48):
                    if u + 1 < 48:
                        top(u + 1)
                    turned(u)
                    if u % 16:
                        out(u - 1)
                    if u % 16 == 15:
                        out(u)
                        t = u // 16
                        od = h8(mix[:, 512:1024], 4)
                        head_norm(od, h8(hd[:, 0:512], 4), 4, 128, R(rowsO, "diff_subln_g"), "dd", t)
                        ts(od, od, 1.0 - LAM_INIT, None, ALU.mult, None, "omix1", t)
                        mixed(1, t)

            dve.wait_ge(sem("ld_const"), 32)
            dve.wait_ge(sem("ld_x"), 16 * TILES)
            step(V.memset(zeros, 0.0), "zeros")
            step(V.memset(small[:, 70:80], 0.0))
            ahead = [(S[name], EARLY) for S in [blk] + [X["S"] for X in extra_loop] for name in S]
            ahead += [(n, 16) for n in y_st + [X["stores"][0][0] for X in extra_loop]]
            for n, (which, value) in enumerate(ahead):
                V.memset(small[:, 80 + n:81 + n], 0.0).then_inc(which, value)
            mods(0)
            norm(0, 0)
            for g, tiles in enumerate(((0,), (1, 2))):
                if g == 1:
                    pass
                copies(("ein", g), tiles, 7, EVEN, E)
                if g == 0:
                    dve.wait_ge(sem("xd_zero"), 32)
                    dve.wait_ge(sem("ld_even"), 16 * 5)
                    dve.wait_ge(*when("SG0"))
                    dve.wait_ge(*when("SR0"))
                    step(V.memset(RH, 0.0))
                    step(V.memset(UU, 0.0))
                else:
                    dve.wait_ge(sem("ld_sg"), 8 * 16)
                    for d in range(2):
                        dve.wait_ge(*when("state_in_p", d))
                        cp(SR[:, d, :, :], PB[:, d, :].rearrange("p (j n) -> p j n", j=4), "state_in", d)
                for i in range(len(tiles)):
                    cp(small[:, 72:73], small[:, 70:71], "e_ready", g, i)
                    bank = 0
                    for n in range(7):
                        for ii in range(len(tiles)):
                            if bank % 2 == 0 and n == 6:
                                dve.wait_ge(*when("ein", g, "evac", n, ii))
                            bank += 1
                    dve.wait_ge(*when("lora", g, i))
                    prepare(g, i)
                units = (((0, 0), (0, 1)), ((0, 0), (1, 0), (1, 1), (0, 1)))[g]
                done = set()
                for i, d in units:
                    gla(g, i, d, i not in done)
                    rwkv(g, i, d, i not in done)
                    done.add(i)
                end("dve", f"units{g}")
                if g == 0:
                    for d in range(2):
                        dve.wait_ge(*when("state_out_p", d))
                        cp(stg[:, d, :], PB[:, d, :], "state_out", d)
                    cp(small[:, 72:73], small[:, 70:71], "state_out_T")
                for i, t in enumerate(tiles):
                    even_out(g, i)
                    mixed(0, t)
                end("dve", f"out_g{g}")
            for l in range(2):
                if l == 1:
                    mods(1)
                    norm(1, 0)
                    copies(("oin",), (0, 1, 2), 4, ODD, O)
                    dve.wait_ge(*when("oin", "evac", 3, 2)) if False else None
                    dve.wait_ge(*when("oin", "evac", 3, 1))
                    odd_prepare()
                    attend()
                residual(l)
                end("dve", f"mixer{l}")
                norm(l, 1)
                if l == 1:
                    dve.wait_ge(*when("caches_stored"))
                route(l)
                experts(l)
                end("dve", f"moe{l}")
    return seen


def constants():
    import numpy as np
    a, b = np.arange(P)[:, None], np.arange(P)[None, :]
    same = (a // CH) == (b // CH)
    c = np.zeros((P, NCONST), np.float32)

    def put(name, v):
        s, w = _C[name]
        c[:, s:s + w] = v

    put("ident", a == b)
    put("lt", same & (a < b))
    put("le", same & (a <= b))
    put("gt", same & (a > b))
    put("ge", same & (a >= b))
    put("half", np.arange(P)[:, None] // CH == np.arange(2)[None, :])
    lv = np.concatenate([(a >> (v + 1) == b >> (v + 1)) & ((a >> v) % 2 == 0) & ((b >> v) % 2 == 1) for v in range(6)], 1)
    lv_t = np.concatenate([(a >> (v + 1) == b >> (v + 1)) & ((a >> v) % 2 == 1) & ((b >> v) % 2 == 0) for v in range(6)], 1)
    put("lvl0", lv)
    put("lvl1", lv_t)
    sel = np.zeros((P, 256))
    sel[0, 0:128] = 1
    sel[1, 128:256] = 1
    put("sel", sel)
    put("bdg", (a // 64) == (np.arange(256)[None, :] // 128))
    put("bdr", (a // 64) == (b // 64))
    put("tie", np.tile((np.arange(4)[None, :] < np.arange(4)[:, None]).reshape(1, 16), (P, 1)))
    put("one", 1.0)
    m = np.zeros((P, NMOE), np.float32)
    for name, v in (("earlier", a < b), ("ones", 1.0), ("row0", np.arange(NE) * P), ("extra", np.arange(80) // 16),
                    ("tri16", (np.arange(16)[None, :] < np.arange(16)[:, None]).reshape(1, 256))):
        s, w = _M[name]
        m[:, s:s + w] = v
    for kind, dim in (("c", 32), ("d", 64)):
        half = dim // 2
        inv = (1.0 / (np.float32(10000.0) ** (np.arange(0, half, 2, dtype=np.float32) / np.float32(half)))).astype(np.float32)
        tok = np.arange(256)
        ang_r = (tok // 64).astype(np.float32)[:, None] * inv
        ang_c = (tok % 64).astype(np.float32)[:, None] * inv
        ang = np.concatenate([ang_r, ang_r, ang_c, ang_c], -1).astype(np.float32)
        q = dim // 4
        sign = np.concatenate([-np.ones(q), np.ones(q), -np.ones(q), np.ones(q)])
        put("cos" + kind, np.cos(ang).reshape(2, P, dim).transpose(1, 0, 2).reshape(P, 2 * dim))
        put("sin" + kind, (np.sin(ang) * sign).reshape(2, P, dim).transpose(1, 0, 2).reshape(P, 2 * dim))
    return c, m


def layout(i):
    import numpy as np

    def blocks(w):
        n = -(-w.shape[1] // 512) * 512
        w = np.concatenate([w, np.zeros((w.shape[0], n - w.shape[1]), w.dtype)], 1) if n != w.shape[1] else w
        return w.reshape(KD, P, n // 512, 512).transpose(2, 1, 0, 3).reshape(n // 512, P, CHUNK)

    def column(v):
        return v.reshape(-1, P).T

    a = {}
    a["consts"], a["consts_moe"] = constants()
    a["x"] = np.concatenate([i["x_prompt"].reshape(1, P, D), i["x_sample"].reshape(2, P, D)], 0)
    cc = np.stack([column(i["c_ctx"]), column(i["c"][0])], 2).reshape(P, 16)
    a["cols"] = np.concatenate([cc, column(i["norm_g"].reshape(-1)), column(i["b_mod"].reshape(-1))], 1)
    a["b_gate"] = np.stack([i["b_mod"][:, 2 * D:3 * D], i["b_mod"][:, 5 * D:6 * D]], 1)
    a["w_mod"] = np.stack([blocks(i["w_mod"][l]) for l in range(2)])
    a["w_mix"] = np.concatenate([blocks(i[n][0]) for n in ("ev_w_in", "ev_w_out", "od_w_in", "od_w_out")])
    for l in range(2):
        for m, n in enumerate(("moe_w_gate", "moe_w_up")):
            a[f"w_moe{l}{m}"] = i[n][l].reshape(NE, KD, P, FF).transpose(0, 2, 1, 3).reshape(NE, P, CHUNK)
        a[f"w_moe{l}2"] = i["moe_w_down"][l].reshape(NE, KF, P, D).transpose(0, 2, 1, 3).reshape(NE, P, CHUNK)
    a["rows_even"] = np.concatenate([i[n].reshape(-1) for n in (
        "gla_a_b", "rw_w0", "rw_a0", "rw_kk", "rw_ka", "rw_rk")])
    a["rows_gain"] = np.concatenate([i[n].reshape(-1) for n in ("rw_gn_g", "rw_gn_b", "gla_o_g")])
    a["rows_odd"] = np.concatenate([i[n].reshape(-1) for n in (
        "mla_qa_g", "mla_kva_g", "mla_qn_g", "mla_kn_g", "diff_qn_g", "diff_kn_g", "diff_lam", "diff_subln_g")])
    a["b_router"] = i["moe_b_router"]
    a["w_router"] = i["moe_w_router"].reshape(KD, P, NE).transpose(1, 0, 2).reshape(P, KD * NE)
    a["gla_a_up"] = i["gla_a_up"][0]
    a["rw_w2"] = i["rw_w2"].reshape(P, 512)
    a["rw_a2"] = i["rw_a2"].reshape(P, 512)
    a["rw_g2"] = i["rw_g2"][0]
    a["state_gla"] = i["state_gla"][0, 0]
    a["state_rwkv"] = i["state_rwkv"][0, 0]
    a["mla_q_up"] = i["mla_q_up"][0]
    a["mla_kv_up"] = i["mla_kv_up"][0]
    for n in ("cache_mla_ckv", "cache_mla_krope", "cache_diff_k", "cache_diff_v"):
        a[n] = i[n][0, 0]
    return {n: np.ascontiguousarray(v) for n, v in a.items()}


_OUTS = {"y": (TILES, P, D), "new_state_gla": (2, 4, 64, 128), "new_state_rwkv": (2, 8, 64, 64), "new_ckv": (P, 128),
         "new_krope": (P, 32), "new_dk": (4, 2, P, 64), "new_dv": (4, P, 128)}


def program(nc, shapes, known):
    io = {n: nc.dram_tensor(f"in_{n}", s, F32, kind="ExternalInput").ap() for n, s in shapes.items()}
    for n, s in _OUTS.items():
        io[n] = nc.dram_tensor(f"out_{n}", s, F32, kind="ExternalOutput").ap()
    io["w_moe"] = [[io[f"w_moe{l}{m}"] for m in range(3)] for l in range(2)]
    return build(nc, io, known)


def kernel(**inputs):
    import numpy as _np
    import concourse.bacc as _bacc
    from concourse.bass_utils import run_bass_kernel_spmd as _run

    arrays = layout({n: _np.asarray(v) for n, v in inputs.items()})
    shapes = {n: v.shape for n, v in arrays.items()}
    stages = program(_bacc.Bacc("TRN2", target_bir_lowering=False, num_devices=1), shapes, None)
    nc = _bacc.Bacc("TRN2", target_bir_lowering=False, num_devices=1)
    program(nc, shapes, stages)
    r = _run(nc, [{f"in_{n}": v for n, v in arrays.items()}], core_ids=[0]).results[0]
    y = r["out_y"]
    return (y[0:1], y[1:3].reshape(1, 2 * P, D), r["out_new_state_gla"][None, None], r["out_new_state_rwkv"][None, None],
            r["out_new_ckv"][None, None], r["out_new_krope"][None, None], r["out_new_dk"][None, None],
            r["out_new_dv"][None, None])
```

```python
import math
from contextlib import ExitStack

import concourse.bass as bass
from concourse import mybir

F32 = mybir.dt.float32
I32 = mybir.dt.int32
ALU = mybir.AluOpType
ACT = mybir.ActivationFunctionType
AX = mybir.AxisListType

P = 128
D = 1024
KD = D // P
TILES = 3
NTOK = TILES * P
CH = 64
EPS = 1e-6
GN_EPS = 64e-5
NE = 16
FF = 512
KF = FF // P
SLOTS = 3
CHUNK = KD * 512
EQ, EK_, EV, EG, EAL, ER, EKB, EVB, EWL, EAA, EGL, EVEN = 0, 256, 512, 1024, 1536, 1568, 2080, 2592, 3104, 3232, 3360, 3488
OCQ, OCKV, OKR, OQD, OKD, OVD, ODD = 0, 256, 384, 416, 928, 1440, 1952
RW = math.exp(-0.5)
LAM_INIT = 0.8 - 0.6 * math.exp(-0.3 * 1)
MIX_EIN, MIX_EOUT, MIX_OIN, MIX_OOUT = 0, 7, 9, 13

_C = {}
_at = 0
for _n, _w in [("ident", 128), ("lt", 128), ("le", 128), ("gt", 128), ("ge", 128), ("half", 2),
               ("lvl0", 768), ("lvl1", 768), ("ones", 128), ("bdg", 256), ("bdr", 128), ("tie", 16),
               ("cosc", 64), ("sinc", 64), ("cosd", 128), ("sind", 128), ("one", 1)]:
    _C[_n] = (_at, _w)
    _at += _w
NCONST = _at
_M = {}
_at = 0
for _n, _w in [("earlier", 128), ("ones", 128), ("tri16", 256), ("row0", 16), ("extra", 80)]:
    _M[_n] = (_at, _w)
    _at += _w
NMOE = _at
CAP = P
NX = (2 * NTOK - NE) // P
ROWS = (NE + NX) * P
COL_C, COL_NG, COL_BM, NCOL = 0, 16, 48, 144
_R = {}
_at = 0
for _n, _w in [("gla_a_b", 512), ("rw_w0", 1024), ("rw_a0", 1024), ("rw_kk", 512), ("rw_ka", 512), ("rw_rk", 512)]:
    _R[_n] = (_at, _w)
    _at += _w
NROW_E = _at
_at = 0
for _n, _w in [("rw_gn_g", 512), ("rw_gn_b", 512), ("gla_o_g", 128)]:
    _R[_n] = (_at, _w)
    _at += _w
NROW_G = _at
_at = 0
for _n, _w in [("mla_qa_g", 256), ("mla_kva_g", 128), ("mla_qn_g", 96), ("mla_kn_g", 96), ("diff_qn_g", 64),
               ("diff_kn_g", 64), ("diff_lam", 256), ("diff_subln_g", 128)]:
    _R[_n] = (_at, _w)
    _at += _w
NROW_O = _at


def bc(ap, axis, n):
    a = ap.unsqueeze(axis)
    shape = list(a.shape)
    shape[axis] = n
    return a.broadcast_to(shape)


def build(nc, io, known):
    seen = {}
    count = {"pe": 0, "act": 0, "dve": 0, "pool": 0}
    with ExitStack() as ctx:
        def sb(name, cols, rows=P):
            return ctx.enter_context(nc.sbuf_tensor(name, [rows, cols], F32))

        sems = {}

        def sem(name):
            if name not in sems:
                sems[name] = ctx.enter_context(nc.semaphore(name))
            return sems[name]

        for e in count:
            sem(e)

        def tick(engine, *name):
            count[engine] += 1
            if name:
                seen[name] = (engine, count[engine])
            return sem(engine), 1

        def when(*name):
            engine, value = known.get(name, ("pe", 1)) if known is not None else ("pe", 1)
            if known and name not in known:
                raise KeyError(name)
            return sem(engine), value

        def end(engine, stage):
            seen[("end", engine, stage)] = (engine, count[engine])

        def meet(eng, me, stage, others=("pe", "act", "dve")):
            for e in others:
                if e != me:
                    s, value = when("end", e, stage)
                    if value > 0:
                        eng.wait_ge(s, value)

        PB = ctx.enter_context(nc.psum_tensor("PB", [P, 8, 512], F32))
        cst = sb("cst", NCONST)
        cols = sb("cols", NCOL)
        x = sb("x", TILES * D)
        hT = sb("hT", KD * NTOK)
        ring = sb("ring", SLOTS * CHUNK)
        gate = sb("gate", 2 * 2 * D)
        modT = sb("modT", 2 * 96)
        mulA = sb("mulA", 4 * KD * 2)
        scT = sb("scT", 16)
        small = sb("small", 256)
        brout = sb("brout", 16)
        wrout = sb("wrout", KD * NE)
        gatek = sb("gatek", 2 * TILES)
        rows_i = ctx.enter_context(nc.sbuf_tensor("rows_i", [P, 2 * TILES], I32))
        xtab = ctx.enter_context(nc.sbuf_tensor("xtab", [P, 8], I32))
        Xd = nc.dram_tensor("dispatched", (ROWS, D), F32, kind="Internal").ap()
        Yd = nc.dram_tensor("expert_out", (ROWS, D), F32, kind="Internal").ap()
        arena_words = 26704
        arena = sb("arena", arena_words)

        def C(name, lo=0, n=None):
            s, w = _C[name]
            return cst[:, s + lo:s + (w if n is None else lo + n)]

        xv = x[:, :].rearrange("p (t d) -> p t d", t=TILES)
        hTv = hT[:, :].rearrange("p (k n) -> p k n", k=KD)
        slot = [ring[:, s * CHUNK:(s + 1) * CHUNK].rearrange("p (k n) -> p k n", k=KD) for s in range(SLOTS)]
        slot_dn = [ring[:, s * CHUNK:(s + 1) * CHUNK].rearrange("p (k n) -> p k n", k=KF) for s in range(SLOTS)]
        gatev = gate[:, :].rearrange("p (c s d) -> p c s d", c=2, s=2)
        mrow = gate[0:2, 0:D].rearrange("p (b n) -> p b n", b=2)
        zeros = gate[:, D:2 * D]
        modTv = modT[:, :].rearrange("p (l j c) -> p l j c", l=2, c=2)
        mulAv = mulA[:, :].rearrange("p (l s k c) -> p l s k c", l=2, s=2, c=2)
        ident = C("ident")

        def carve(at):
            pos = [at]

            def take(words):
                a = pos[0]
                pos[0] += words
                assert pos[0] <= arena_words, pos[0]
                return arena[:, a:a + words]
            return take

        take = carve(0)
        E = take(2 * EVEN).rearrange("p (t n) -> p t n", t=2)
        rowsE = take(NROW_E)
        oG = take(2 * 512).rearrange("p (t n) -> p t n", t=2)
        yR = take(2 * 512).rearrange("p (t n) -> p t n", t=2)
        kkn = take(2 * 512).rearrange("p (t n) -> p t n", t=2)
        loT = take(2 * 512).rearrange("p (t j n) -> p t j n", t=2, j=4)
        bon = take(16).rearrange("p (t h) -> p t h", t=2)
        SG = take(2 * 512).rearrange("p (d j n) -> p d j n", d=2, j=2)
        SR = take(2 * 512).rearrange("p (d j n) -> p d j n", d=2, j=4)
        tokm = take(4 * 512).rearrange("p (a n) -> p a n", a=4)
        G4 = take(4 * 512).rearrange("p (h n) -> p h n", h=4)
        TA = take(512).rearrange("p (a n) -> p a n", a=4)
        TB = take(512).rearrange("p (a n) -> p a n", a=4)
        X4 = take(512).rearrange("p (h n) -> p h n", h=4)
        XT4 = take(512).rearrange("p (h n) -> p h n", h=4)
        T14 = take(512).rearrange("p (h n) -> p h n", h=4)
        LJ4 = take(512).rearrange("p (h n) -> p h n", h=4)
        RH = take(256)
        UU = take(256)
        SG_tmp = take(256)
        aup = take(512)
        w2 = take(512)
        a2 = take(512)
        rowsG = tokm.rearrange("p a n -> p (a n)")[:, 0:NROW_G]
        g2w = tokm[:, 3, :]
        TT = (TA, TB)
        tmpE = X4.rearrange("p h n -> p (h n)"), XT4.rearrange("p h n -> p (h n)"), T14.rearrange("p h n -> p (h n)")
        stg = G4

        xn = tokm.rearrange("p (b c) n -> p b (c n)", b=2)
        gated = G4[:, 0, :]

        take = carve(0)
        O = take(3 * ODD).rearrange("p (t n) -> p t n", t=3)
        rowsO = take(NROW_O)
        cdk = take(512).rearrange("p (m n) -> p m n", m=8)
        cdv = take(512).rearrange("p (h n) -> p h n", h=4)
        cckv = take(128)
        ckr = take(32)
        kvup = take(1024)
        u0 = take(1536)
        cqT = take(2 * NTOK).rearrange("p (k n) -> p k n", k=2)
        ckT = take(4 * P).rearrange("p (k n) -> p k n", k=4)
        kT = take(8 * 512).rearrange("p (h n) -> p h n", h=8)
        vC = take(4 * 512).rearrange("p (k h n) -> p k h n", k=4, h=8)
        dqT = take(4 * NTOK).rearrange("p (h n) -> p h n", h=4)
        dkT = take(4 * 512).rearrange("p (h n) -> p h n", h=4)
        hd = take(768)
        hd2 = take(768)
        qup = u0.rearrange("p (k n) -> p k n", k=2)
        prob = take(2 * 384).rearrange("p (b n) -> p b n", b=2)
        probT = take(2 * 384).rearrange("p (b k n) -> p b k n", b=2, k=3)
        mix = u0[:, 0:1024]
        hds = [hd, prob.rearrange("p b n -> p (b n)")]
        hqs = [hd2, probT.rearrange("p b k n -> p (b k n)")]
        sqd = kT.rearrange("p h n -> p (h n)")
        head_items = [("q", t) for t in range(TILES)] + [("k", kt) for kt in range(4)]

        take = carve(0)
        slots_x = take(3 * CHUNK)
        xb = take(2 * D).rearrange("p (b d) -> p b d", b=2)
        xT = take(2 * D).rearrange("p (b n) -> p b n", b=2)
        sil = take(2 * FF).rearrange("p (b n) -> p b n", b=2)
        hid = take(2 * FF).rearrange("p (b n) -> p b n", b=2)
        hidT = take(2 * FF).rearrange("p (b n) -> p b n", b=2)
        yb = take(2 * D).rearrange("p (b d) -> p b d", b=2)
        cmoe = take(NMOE)
        route_w = take(1920)
        mask = small[:, 176:224]
        yg = slots_x[:, 0:6 * D].rearrange("p (c d) -> p c d", c=6)
        assert 2 * D + 2 * FF == TILES * D
        htok = arena[:, 3 * CHUNK + 2 * D:3 * CHUNK + 2 * D + TILES * D].rearrange("p (t d) -> p t d", t=TILES)
        wslot = [[ring[:, m * CHUNK:(m + 1) * CHUNK] for m in range(3)],
                 [slots_x[:, m * CHUNK:(m + 1) * CHUNK] for m in range(3)]]

        def M(name):
            a, w = _M[name]
            return cmoe[:, a:a + w]

        def R(rows, name, lo=0, n=None):
            s, w = _R[name]
            return rows[:, s + lo:s + (w if n is None else lo + n)]

        EARLY_MODS = 4
        mods_in = [[(0, n) for n in range(EARLY_MODS, 12)], [(1, n) for n in range(12)]]
        stream = [("mod", (0, n), ("modr", 0, n)) for n in range(EARLY_MODS)]
        for g in range(2):
            stream += [("mix", MIX_EIN + n, ("ein", g, n)) for n in range(7)]
            stream += [("mod", ln, ("modr", *ln)) for ln in mods_in[g]]
        stream += [("mix", MIX_EOUT + n, ("outp", 0, n)) for n in range(2)]
        first = len(stream)
        stream += [("mix", MIX_OIN + n, ("oin", n)) for n in range(4)]
        stream += [("mix", MIX_OOUT + n, ("outp", 1, n)) for n in range(2)]
        where, landed = {}, {}
        cnt = [0] * SLOTS
        for i, (kind, src, name) in enumerate(stream):
            s = (i if i < first else i - first) % SLOTS
            cnt[s] += 1
            where[name], landed[name] = s, 16 * cnt[s]
        w_land = [sem(f"w_landed{s}") for s in range(SLOTS)]
        EARLY = 2

        def steps(tag):
            return {n: sem(f"{tag}_{n}") for n in (
                "xT_p", "xT_a", "xT_v", "gu", "silu", "hid", "hT_p", "hT_v", "dn", "y_a", "y_v")}

        def loop(S, base, stride, land, land_base, rows, stores):
            return dict(S=S, base=base, k=stride, land=land, land_base=land_base, rows=rows, stores=stores)

        def steps_of(L, step, i, c):
            v = L["base"] + c + 1 + EARLY
            return L["S"][step], (v if i is None else i * L["k"] + v)

        def loads_of(L, sems, base, i, c):
            v = base + 16 * (c // L["k"] + 1)
            return sems, (v if i is None else i * 16 + v)

        half = NE // 2
        per = [sum(1 for n in stream[:first] if where[n[2]] == m) for m in range(SLOTS)]
        per1 = [sum(1 for n in stream[first:] if where[n[2]] == m) for m in range(SLOTS)]
        for n in stream[first:]:
            landed[n[2]] += 16 * half
        w_land1 = [sem(f"w_landed{m + 3}") for m in range(3)]
        blk = steps("blk")
        x_land = [sem(f"x_landed{b}") for b in range(2)]
        y_st = [sem(f"y_stored{b}") for b in range(2)]
        base_loop, extra_loop = [], []
        for l in range(2):
            ring_base = [16 * (per[m] + l * (half + per1[m])) for m in range(SLOTS)]
            base_loop.append(loop(blk, l * NE, 2, [w_land, w_land1], [ring_base, [16 * half * l] * 3],
                                  (x_land, 16 * half * l), (y_st, 16 * half * l + 16)))
            ext = [sem(f"ext{l}_w_landed{m}") for m in range(3)]
            extra_loop.append(loop(steps(f"ext{l}"), 0, 1, [ext], [[0] * 3],
                                   ([sem(f"ext{l}_x_landed")], 0), ([sem(f"ext{l}_y_stored")], 16)))

        COMBOS = [[((0, 0), (0, 1))], [((0, 0), (1, 1)), ((1, 0), (0, 1))]]

        def beside(g, i, d, hf):
            n = 2 * [u for combo in COMBOS[g] for u in combo].index((i, d)) + hf
            if g == 0:
                return mods_in[0][2 * n:2 * n + 2]
            return mods_in[1][n + (n + 1) // 2:n + 1 + (n + 2) // 2]

        block = ctx.enter_context(nc.Block())

        @block.sync
        def _(sp):
            owner = [None] * SLOTS

            def load(kind, src, name):
                s = where[name]
                if owner[s] is not None:
                    sp.wait_ge(*when(*owner[s]))
                owner[s] = name
                dram = io["w_mod"][src[0], src[1]] if kind == "mod" else io["w_mix"][src]
                sp.dma_start(ring[:, s * CHUNK:(s + 1) * CHUNK], dram).then_inc(w_land[s], 16)

            def weights(L, l, i, c, b, e):
                for m in range(3):
                    sp.wait_ge(*steps_of(L, "gu" if m < 2 else "dn", i, c - L["k"]))
                    sp.dma_start(wslot[b][m], io["w_moe"][l][m][bass.ds(e, 1)].rearrange("e p n -> (e p) n"))\
                        .then_inc(L["land"][b][m], 16)

            def experts(l):
                L = base_loop[l]
                for m in range(SLOTS):
                    if owner[m] is not None:
                        sp.wait_ge(*when(*owner[m]))
                    owner[m] = None
                weights(L, l, None, 0, 0, 0)
                meet(sp, "sp", f"mixer{l}")
                if l:
                    sp.wait_ge(sem("st_cache"), 14 * 16)
                weights(L, l, None, 1, 1, 1)
                with sp.Fori(1, half) as i:
                    for b in range(2):
                        weights(L, l, i, b, b, i * 2 + b)
                sp.wait_ge(*when("rows", l))
                n_extra = nc.sync.value_load(xtab[0:1, 7:8], min_val=0, max_val=NX)
                with sp.If(n_extra > 0):
                    X = extra_loop[l]
                    sp.wait_ge(*steps_of(L, "gu", None, NE - 1))
                    sp.wait_ge(*steps_of(L, "dn", None, NE - 1))
                    with sp.Fori(0, NX) as i:
                        e = nc.sync.value_load(xtab[0:1, bass.ds(i, 1)], min_val=0, max_val=NE - 1)
                        weights(X, l, i, 0, 0, e)
                        sp.wait_ge(*steps_of(X, "xT_p", i, -1))
                        sp.dma_start(xb[:, 0, :], Xd[bass.ds(i * P + NE * P, P), :]).then_inc(X["rows"][0][0], 16)
                sp.wait_ge(*when("y_all", l))

            for item in stream[:first]:
                load(*item)
            experts(0)
            sp.wait_ge(sem(f"combined{TILES - 1}"), 32)
            for item in stream[first:]:
                load(*item)
            experts(1)

        @block.gpsimd
        def _(pool):
            def dma(dst, src, name):
                pool.dma_start(dst, src).then_inc(sem(name), 16)

            dma(cols[:, :], io["cols"], "ld_cols")
            dma(cst[:, :], io["consts"], "ld_const")
            for t in range(TILES):
                dma(xv[:, t, :], io["x"][t], "ld_x")
            dma(brout[:, :], io["b_router"].partition_broadcast(P), "ld_router")
            dma(wrout[:, :], io["w_router"], "ld_router")
            dma(rowsE, io["rows_even"].partition_broadcast(P), "ld_even")
            nc.gpsimd.memset(aup[0:32, :], 0.0).then_inc(*tick("pool", "aup0"))
            pool.wait_ge(*when("aup0"))
            for d in range(2):
                dma(aup[16 * d:16 * d + 16, 256 * d:256 * d + 256], io["gla_a_up"][d], "ld_even")
            dma(w2, io["rw_w2"], "ld_even")
            dma(a2, io["rw_a2"], "ld_even")

            def late_rows(g):
                meet(pool, "pool", f"units{g}")
                dma(rowsG, io["rows_gain"].partition_broadcast(P), "ld_late")
                dma(g2w, io["rw_g2"], "ld_late")

            nc.gpsimd.memset(SG, 0.0).then_inc(*tick("pool", "SG0"))
            nc.gpsimd.memset(SR, 0.0).then_inc(*tick("pool", "SR0"))
            def level_blocks(g, i, d, hf):
                lvl = C("lvl0") if d == 0 else C("lvl1")
                for v in range(1, 6):
                    for p in range(2):
                        w = (g, i, d, hf, p)
                        pool.wait_ge(*when("G", *w))
                        if v > 1:
                            pool.wait_ge(*when("t1", *w, v - 1))
                        nc.gpsimd.tensor_tensor(LJ4[:, 2 * p:2 * p + 2, :], G4[:, 2 * p:2 * p + 2, 0:128],
                                                bc(lvl[:, 128 * v:128 * v + 128], 1, 2), ALU.mult)\
                            .then_inc(*tick("pool", "LJ", *w, v))
                        if v == 1:
                            XT = XT4[:, 2 * p:2 * p + 2, :]
                            nc.gpsimd.tensor_tensor(XT, G4[:, 2 * p:2 * p + 2, 0:128], bc(lvl[:, 0:128], 1, 2), ALU.mult)\
                                .then_inc(*tick("pool"))
                            pool.wait_ge(sem("pool"), count["pool"])
                            nc.gpsimd.tensor_tensor(XT, bc(ident, 1, 2), XT, ALU.subtract)\
                                .then_inc(*tick("pool", "XT", *w, 0))

            def units(g):
                for combo in COMBOS[g]:
                    for i, d in combo:
                        for hf in range(2):
                            level_blocks(g, i, d, hf)

            units(0)
            late_rows(0)
            for d in range(2):
                for h in range(4):
                    r = 64 * (h % 2)
                    dma(io["new_state_gla"][d, h], SG[r:r + 64, d, h // 2, 128 * (h % 2):128 * (h % 2) + 128], "st_gla")
            pool.wait_ge(*when("state_out_T"))
            for d in range(2):
                for h in range(8):
                    r = 64 * (h % 2)
                    dma(io["new_state_rwkv"][d, h], stg[r:r + 64, d, (h // 2) * 128 + r:(h // 2) * 128 + r + 64], "st_rwkv")
            pool.wait_ge(sem("st_gla"), 8 * 16)
            pool.wait_ge(sem("st_rwkv"), 16 * 16)
            nc.gpsimd.memset(SG, 0.0).then_inc(*tick("pool", "SG1"))
            nc.gpsimd.memset(stg[:, 0:2, :], 0.0).then_inc(*tick("pool", "stg0"))
            pool.wait_ge(*when("stg0"))
            for d in range(2):
                for h in range(4):
                    r = 64 * (h % 2)
                    dma(SG[r:r + 64, d, h // 2, 128 * (h % 2):128 * (h % 2) + 128], io["state_gla"][d, h], "ld_sg")
                for h in range(8):
                    r = 64 * (h % 2)
                    dma(stg[r:r + 64, d, (h // 2) * 128 + r:(h // 2) * 128 + r + 64], io["state_rwkv"][d, h], "ld_sr")
            units(1)
            late_rows(1)

            def experts(l):
                meet(pool, "pool", f"mixer{l}")
                dma(cmoe, io["consts_moe"], "ld_cmoe")
                pool.wait_ge(sem("xd_zero"), 32)
                pool.wait_ge(*when("rows", l))
                for t in range(TILES):
                    pool.wait_ge(*when("htok", l, t))
                    for ch in range(2):
                        pool.indirect_dma_start(
                            Xd, bass.IndirectOffsetOnAxis(ap=rows_i[:, 3 * ch + t:3 * ch + t + 1], axis=0),
                            htok[:, t, :], None).then_inc(sem("dispatched"), 16)
                pool.wait_ge(sem("dispatched"), 96 * (l + 1))
                L = base_loop[l]
                with pool.Fori(0, half) as i:
                    for b in range(2):
                        pool.wait_ge(*steps_of(L, "xT_p", i, b - 2))
                        pool.dma_start(xb[:, b, :], Xd[bass.ds(i * 2 * P + b * P, P), :]).then_inc(x_land[b], 16)
                pool.wait_ge(*when("y_all", l))
                for t in range(TILES):
                    for ch in range(2):
                        pool.indirect_dma_start(
                            yg[:, 3 * ch + t, :], None, Yd,
                            bass.IndirectOffsetOnAxis(ap=rows_i[:, 3 * ch + t:3 * ch + t + 1], axis=0))\
                            .then_inc(sem(f"combined{t}"), 16)

            experts(0)
            meet(pool, "pool", "moe0")
            dma(rowsO, io["rows_odd"].partition_broadcast(P), "ld_odd")
            dma(qup, io["mla_q_up"].rearrange("(k p) n -> p k n", p=P), "ld_odd")
            dma(kvup, io["mla_kv_up"], "ld_odd")
            dma(cckv, io["cache_mla_ckv"], "ld_odd")
            dma(ckr, io["cache_mla_krope"], "ld_odd")
            for m in range(8):
                dma(cdk[:, m, :], io["cache_diff_k"][m // 2, m % 2], "ld_odd")
            for h in range(4):
                dma(cdv[:, h, :], io["cache_diff_v"][h], "ld_odd")
            pool.wait_ge(*when("caches"))
            dma(io["new_ckv"], O[:, 0, OCKV:OCKV + 128], "st_cache")
            dma(io["new_krope"], O[:, 0, OKR:OKR + 32], "st_cache")
            for m in range(8):
                dma(io["new_dk"][m // 2, m % 2], O[:, 0, OKD + 64 * m:OKD + 64 * m + 64], "st_cache")
            for h in range(4):
                dma(io["new_dv"][h], O[:, 0, OVD + 128 * h:OVD + 128 * h + 128], "st_cache")
            pool.wait_ge(sem("st_cache"), 14 * 16)
            nc.gpsimd.memset(small[:, 255:256], 0.0).then_inc(*tick("pool", "caches_stored"))
            experts(1)
            for t in range(TILES):
                pool.wait_ge(*when("x_moe", 1, t))
                dma(io["y"][t], xv[:, t, :], "st_y")
            pool.wait_ge(sem("st_y"), TILES * 16)

        @block.tensor
        def _(pe):
            reader = [None] * 8

            def claim(b, *name):
                if reader[b] is not None:
                    pe.wait_ge(*when(*reader[b]))
                reader[b] = name

            def mm(out, lhsT, rhs, start=True, stop=True, **k):
                return nc.tensor.matmul(out, lhsT, rhs, start=start, stop=stop, **k)

            def tp(out, in_, n=P):
                return nc.tensor.transpose(out, in_, ident[0:n, 0:n])

            def chunk_landed(*name):
                pe.wait_ge(w_land[where[name]], landed[name])
                return slot[where[name]]

            def mod_rows(l, n, k, bank):
                w = slot[where[("modr", l, n)]]
                if k == 0:
                    chunk_landed("modr", l, n)
                    claim(bank, "mrow", l, n)
                ins = mm(PB[0:2, bank, :], scT[:, 2 * k:2 * k + 2], w[:, k, :], k == 0, k == KD - 1)
                if k == KD - 1:
                    ins.then_inc(*tick("pe", "modr", l, n))

            def mod_columns(l, n, bank, b):
                pe.wait_ge(*when("mrow", l, n))
                claim(bank, "modT", l, n)
                for j in range(4):
                    ins = tp(PB[:, bank, 2 * j:2 * j + 2], mrow[:, b, 128 * j:128 * j + 128], 2)
                ins.then_inc(*tick("pe", "modp", l, n))

            def spread_gates(l, s):
                for n in range(4):
                    pe.wait_ge(*when("diag", l, s, n))
                    claim(4 + n % 2, "gate", l, s, n)
                    mm(PB[:, 4 + n % 2, :], C("ones"), tokm[:, n, :]).then_inc(*tick("pe", "spread", l, s, n))

            def norm(l, s):
                for t in range(TILES):
                    pe.wait_ge(*when("xn", l, s, t))
                    for b in range(2):
                        claim(6 + b, "hT", l, s, t, b)
                        for k in range(4):
                            ins = tp(PB[:, 6 + b, 128 * k:128 * k + 128],
                                     xn[:, t % 2, (4 * b + k) * 128:(4 * b + k + 1) * 128])
                        ins.then_inc(*tick("pe", "xnT", l, s, t, b))

            def project(name, tiles, chunks, width, after=None):
                bank = 0
                for n in range(chunks):
                    w = chunk_landed(*name, n)
                    ncol = min(512, width - 512 * n)
                    for i, t in enumerate(tiles):
                        claim(bank % 4, *name, "evac", n, i)
                        for k in range(KD):
                            ins = mm(PB[:, bank % 4, 0:ncol], hTv[:, k, t * P:(t + 1) * P], w[:, k, 0:ncol],
                                     k == 0, k == KD - 1)
                        bank += 1
                        ins.then_inc(*tick("pe", *name, "p", n, i))
                    seen[(*name, n)] = ("pe", count["pe"])
                    if after:
                        after(n)

            def lora_T(g, i):
                pe.wait_ge(*when("lora", g, i))
                claim(0, "loT", g, i)
                for j, (c0, n) in enumerate([(EWL, 128), (EAA, 128), (EGL, 128), (EAL, 32)]):
                    ins = tp(PB[0:n, 0, 128 * j:128 * j + 128], E[:, i, c0:c0 + n])
                ins.then_inc(*tick("pe", "lora_T", g, i))

            def gla(g, w, combo):
                u = (g, w)
                for i, d in combo:
                    pe.wait_ge(*when("loT", g, i))
                claim(0, "ga_z", *u)
                for i, d in combo:
                    ins = mm(PB[:, 0, 256 * d:256 * d + 256], loT[0:32, i, 3, :], aup[0:32, 256 * d:256 * d + 256])
                ins.then_inc(*tick("pe", "za", *u))
                pe.wait_ge(*when("la", *u))
                claim(1, "g_exp", *u)
                claim(2, "g_exp", *u)
                claim(3, "g_dec", *u)
                for i, d in combo:
                    inc, rest = (C("le"), C("gt")) if d == 0 else (C("ge"), C("lt"))
                    la = tmpE[0][:, 256 * d:256 * d + 256]
                    mm(PB[:, 1, 256 * d:256 * d + 256], inc, la)
                    ins = mm(PB[:, 2, 256 * d:256 * d + 256], rest, la)
                ins.then_inc(*tick("pe", "gcum", *u))
                for i, d in combo:
                    la = tmpE[0][:, 256 * d:256 * d + 256]
                    for j in range(2):
                        ins = mm(PB[:, 3, 4 * d + 2 * j:4 * d + 2 * j + 2], la[:, 128 * j:128 * j + 128], C("half"))
                ins.then_inc(*tick("pe", "gsum", *u))
                pe.wait_ge(*when("gk", *u))
                for d in range(2):
                    claim(4 + d, "gqkT", *u, d)
                    for j in range(4):
                        ins = tp(PB[:, 4 + d, 128 * j:128 * j + 128],
                                 tokm[:, j // 2, 256 * d + 128 * (j % 2):256 * d + 128 * (j % 2) + 128])
                    ins.then_inc(*tick("pe", "gT", *u, d))
                claim(6, "gatt", *u)
                claim(7, "gatt", *u)
                for d in range(2):
                    pe.wait_ge(*when("gqkT", *u, d))
                    for h in range(4):
                        r, j = 64 * (h % 2), h // 2
                        ins = mm(PB[:, 6 + h % 2, 256 * d + 128 * j:256 * d + 128 * j + 128],
                                 TT[d][r:r + 64, 2 + j, :], TT[d][r:r + 64, j, :])
                ins.then_inc(*tick("pe", "gA", *u))
                pe.wait_ge(*when("gatt", *u))
                for i, d in combo:
                    claim(d, "gout", *u, d)
                    for h in range(4):
                        mm(PB[:, d, 128 * h:128 * h + 128], G4[:, h, 128 * d:128 * d + 128],
                           E[:, i, EV + 128 * h:EV + 128 * h + 128], h == 0, False, skip_group_check=True)
                for n in range(2):
                    for i, d in combo:
                        r = CH * (n if d == 0 else 1 - n)
                        if n:
                            pe.wait_ge(*when("gS", *u, d, 0))
                        for j in range(2):
                            mm(PB[r:r + CH, d, 256 * j:256 * j + 256], TT[d][:, j, r:r + CH], SG[:, d, j, :],
                               False, n == 1, skip_group_check=True)
                        claim(2 + d, "gS", *u, d, n)
                        for j in range(2):
                            ins = mm(PB[:, 2 + d, 256 * j:256 * j + 256],
                                     tokm[r:r + CH, 2, 256 * d + 128 * j:256 * d + 128 * j + 128],
                                     E[r:r + CH, i, EV + 256 * j:EV + 256 * j + 256], skip_group_check=True)
                        ins.then_inc(*tick("pe", "gu", *u, d, n))

            def rwkv(g, i, d):
                u = (g, i, d)
                inc, exc = (C("le"), C("lt")) if d == 0 else (C("ge"), C("gt"))
                r = 64 * d
                claim(d, "r_zw", *u)
                mm(PB[:, d, :], loT[r:r + 64, i, 0, :], w2[r:r + 64, :]).then_inc(*tick("pe", "zw", *u))
                claim(2 + d, "r_za", *u)
                mm(PB[:, 2 + d, :], loT[r:r + 64, i, 1, :], a2[r:r + 64, :]).then_inc(*tick("pe", "zr", *u))
                pe.wait_ge(*when("lw", *u))
                lw = tmpE[0]
                claim(5, "e_exc", *u)
                mm(PB[:, 5, :], exc, lw).then_inc(*tick("pe", "sum_exc", *u))
                claim(4, "e_inc", *u)
                mm(PB[:, 4, :], inc, lw).then_inc(*tick("pe", "sum_inc", *u))
                claim(6, "e_wc", *u)
                for j in range(4):
                    ins = mm(PB[:, 6, 2 * j:2 * j + 2], lw[:, 128 * j:128 * j + 128], C("half"))
                ins.then_inc(*tick("pe", "rcum", *u))
                pe.wait_ge(*when("tokm", *u))
                for hf in range(2):
                    rwkv_half(g, i, d, hf)

            def rwkv_half(g, i, d, hf):
                u = (g, i, d, hf)
                mods = beside(*u)

                def between(q):
                    if q < KD:
                        mod_rows(*mods[0], q, 5)
                    elif q == KD + 1:
                        mod_columns(*mods[0], 4, 0)
                    if q > KD and len(mods) > 1:
                        mod_rows(*mods[1], q - KD - 1, 5)

                for p in range(2):
                    claim(p, "TT", *u, p)
                    f = (2 * hf + p) * 128
                    for a in range(4):
                        ins = tp(PB[:, p, 128 * a:128 * a + 128], tokm[:, a, f:f + 128])
                    ins.then_inc(*tick("pe", "tT", *u, p))
                for p in range(2):
                    pe.wait_ge(*when("TT", *u, p))
                    T = TT[p]
                    for b in range(2):
                        r = 64 * b
                        claim(2 + 2 * p + b, "G", *u, p)
                        for a in range(2):
                            ins = mm(PB[:, 2 + 2 * p + b, 256 * a:256 * a + 256], T[r:r + 64, 2 + a, :], T[r:r + 64, 0:2, :])
                    ins.then_inc(*tick("pe", "gram", *u, p))
                    for b in range(2):
                        r, bank = 64 * b, (6 if p == 0 else 0) + b
                        claim(bank, "L0", *u, p)
                        ins = mm(PB[:, bank, 0:128], T[r:r + 64, 0, :], T[r:r + 64, 2, :])
                    ins.then_inc(*tick("pe", "gramL", *u, p))
                for v in range(1, 6):
                    for p in range(2):
                        pe.wait_ge(*when("X", *u, p, v - 1))
                        pe.wait_ge(*when("LJ", *u, p, v))
                        claim(6 + p, "T1", *u, p, v)
                        for b in range(2):
                            h = 2 * p + b
                            ins = mm(PB[:, 6 + p, 128 * b:128 * b + 128], LJ4[:, h, :], X4[:, h, :])
                        ins.then_inc(*tick("pe", "t1", *u, p, v))
                    between(2 * v - 2)
                    for p in range(2):
                        pe.wait_ge(*when("T1", *u, p, v))
                        pe.wait_ge(*when("XT", *u, p, v - 1))
                        if v < 5:
                            claim(6 + p, "X", *u, p, v)
                            for b in range(2):
                                h = 2 * p + b
                                ins = mm(PB[:, 6 + p, 256 + 128 * b:384 + 128 * b], XT4[:, h, :], T14[:, h, :])
                            ins.then_inc(*tick("pe", "dx", *u, p, v))
                        claim(p, "XT", *u, p, v)
                        for b in range(2):
                            h = 2 * p + b
                            ins = mm(PB[:, p, 128 * b:128 * b + 128], T14[:, h, :], XT4[:, h, :])
                        ins.then_inc(*tick("pe", "dxt", *u, p, v))
                    between(2 * v - 1)
                for n, c in enumerate((0, 1) if d == 0 else (1, 0)):
                    r = CH * c
                    for p in range(2):
                        if n:
                            pe.wait_ge(*when("S", *u, p, 0))
                        claim(2 + p, "RH", *u, p, n)
                        for b in range(2):
                            h = 2 * p + b
                            V = E[:, i, EVB + (4 * hf + h) * 64:EVB + (4 * hf + h + 1) * 64]
                            mm(PB[r:r + CH, 2 + p, 64 * b:64 * b + 64], G4[:, h, 256 + r:256 + r + CH], V, b == 0, False,
                               skip_group_check=True)
                        mm(PB[r:r + CH, 2 + p, 0:128], TT[p][:, 0, r:r + CH], SR[:, d, 2 * hf + p, :], False, True,
                           skip_group_check=True).then_inc(*tick("pe", "rh", *u, p, n))
                    claim(4, "Y", *u, n)
                    for h in range(4):
                        V = E[:, i, EVB + (4 * hf + h) * 64:EVB + (4 * hf + h + 1) * 64]
                        mm(PB[r:r + CH, 4, 64 * h:64 * h + 64], G4[:, h, 384 + r:384 + r + CH], V, h == 0, False,
                           skip_group_check=True)
                    for p in range(2):
                        mm(PB[r:r + CH, 4, 128 * p:128 * p + 128], TT[p][:, 1, r:r + CH], SR[:, d, 2 * hf + p, :],
                           False, False, skip_group_check=True)
                    between(10 + 3 * n)
                    for p in range(2):
                        if n == 0:
                            pe.wait_ge(*when("XT", *u, p, 5))
                        pe.wait_ge(*when("RH", *u, p, n))
                        claim(p, "U", *u, p, n)
                        for b in range(2):
                            h = 2 * p + b
                            ins = mm(PB[r:r + CH, p, 64 * b:64 * b + 64], XT4[:, h, r:r + CH], RH[:, 64 * h:64 * h + 64],
                                     skip_group_check=True)
                        ins.then_inc(*tick("pe", "uu", *u, p, n))
                    between(11 + 3 * n)
                    for p in range(2):
                        pe.wait_ge(*when("U", *u, p, n))
                        claim(6 + p, "S", *u, p, n)
                        f = (2 * hf + p) * 128
                        mm(PB[:, 6 + p, 0:128], tokm[r:r + CH, 2, f:f + 128], UU[r:r + CH, 128 * p:128 * p + 128],
                           True, False, skip_group_check=True)
                        mm(PB[:, 6 + p, 0:128], tokm[r:r + CH, 3, f:f + 128], E[r:r + CH, i, EVB + f:EVB + f + 128],
                           False, True, skip_group_check=True).then_inc(*tick("pe", "su", *u, p, n))
                    for h in range(4):
                        ins = mm(PB[r:r + CH, 4, 64 * h:64 * h + 64], G4[:, h, 128 + r:128 + r + CH],
                                 UU[:, 64 * h:64 * h + 64], False, h == 3, skip_group_check=True)
                    ins.then_inc(*tick("pe", "yy", *u, n))
                    between(12 + 3 * n)
                if len(mods) > 1:
                    between(16)
                    mod_columns(*mods[1], 5, 1)

            def states_T(name, src, wait):
                pe.wait_ge(*when(*wait)) if isinstance(wait, tuple) else pe.wait_ge(sem(wait), 16 * 16)
                for d in range(2):
                    claim(d, name, d)
                    for j in range(4):
                        ins = tp(PB[:, d, 128 * j:128 * j + 128], src(d, j))
                    ins.then_inc(*tick("pe", name + "_p", d))

            def even_out(g, i, t):
                pe.wait_ge(sem("ld_late"), 32 * (g + 1))
                claim(5, "omix", g, i)
                mm(PB[:, 5, :], loT[:, i, 2, :], g2w).then_inc(*tick("pe", "gm", g, i))
                mixed_T(("omix", g, i), lambda k: (oG if k < 4 else yR)[:, i, 128 * (k % 4):128 * (k % 4) + 128], t, 0)

            def mixed_T(name, src, t, l):
                pe.wait_ge(*when(*name))
                for b in range(2):
                    claim(6 + b, "mT", l, t, b)
                    for k in range(4):
                        ins = tp(PB[:, 6 + b, 128 * k:128 * k + 128], src(4 * b + k))
                    ins.then_inc(*tick("pe", "mixT", l, t, b))

            def router(l):
                pe.wait_ge(sem("ld_router"), 32)
                for t in range(TILES):
                    for b in range(2):
                        pe.wait_ge(*when("hT", l, 1, t, b))
                claim(0, "scores", l)
                for t in range(TILES):
                    for k in range(KD):
                        ins = mm(PB[:, 0, 16 * t:16 * t + 16], hTv[:, k, t * P:(t + 1) * P],
                                 wrout[:, 16 * k:16 * k + 16], k == 0, k == KD - 1)
                ins.then_inc(*tick("pe", "rt", l))
                for t in range(TILES):
                    for b in range(2):
                        claim(2 + (2 * t + b) % 4, "htok_c", l, t, b)
                        for k in range(4):
                            ins = tp(PB[:, 2 + (2 * t + b) % 4, 128 * k:128 * k + 128],
                                     hTv[:, 4 * b + k, t * P:(t + 1) * P])
                        ins.then_inc(*tick("pe", "htok_p", l, t, b))
                pe.wait_ge(*when("mask", l))
                claim(1, "place", l)
                pe.wait_ge(sem("ld_cmoe"), 16 * (l + 1))
                for t in range(TILES + 1):
                    for q in range(t):
                        ins = mm(PB[:, 1, 16 * t:16 * t + 16], M("ones"), mask[:, 16 * q:16 * q + 16], q == 0,
                                 t == TILES and q == t - 1)
                    if t < TILES:
                        mm(PB[:, 1, 16 * t:16 * t + 16], M("earlier"), mask[:, 16 * t:16 * t + 16], t == 0, True)
                ins.then_inc(*tick("pe", "places", l))

            def rows_T(L, i, c, b):
                pe.wait_ge(*loads_of(L, L["rows"][0][b], L["rows"][1], i, c))
                pe.wait_ge(*steps_of(L, "xT_v", i, c - 1))
                pe.wait_ge(*steps_of(L, "xT_a", i, c - 1))
                pe.wait_ge(*steps_of(L, "hT_v", i, c - L["k"]))
                for k in range(KD):
                    ins = tp(PB[:, k // 4, 128 * (k % 4):128 * (k % 4) + 128], xb[:, b, 128 * k:128 * k + 128])
                ins.then_inc(L["S"]["xT_p"], 1)

            def gate_up(L, i, c, b):
                pe.wait_ge(*steps_of(L, "xT_a", i, c))
                pe.wait_ge(*steps_of(L, "xT_v", i, c))
                pe.wait_ge(*steps_of(L, "silu", i, c - L["k"]))
                pe.wait_ge(*steps_of(L, "hid", i, c - L["k"]))
                for m in range(2):
                    pe.wait_ge(*loads_of(L, L["land"][b][m], L["land_base"][b][m], i, c))
                    w = wslot[b][m].rearrange("p (k n) -> p k n", k=KD)
                    for k in range(KD):
                        ins = mm(PB[:, 2 + 2 * m + b, :], xT[:, b, 128 * k:128 * k + 128], w[:, k, :], k == 0, k == KD - 1)
                ins.then_inc(L["S"]["gu"], 1)

            def hidden_T(L, i, c, b, ahead):
                pe.wait_ge(*steps_of(L, "hid", i, c))
                pe.wait_ge(*steps_of(L, "xT_a", i, c + ahead))
                for k in range(KF):
                    ins = tp(PB[:, 0, 128 * k:128 * k + 128], hid[:, b, 128 * k:128 * k + 128])
                ins.then_inc(L["S"]["hT_p"], 1)

            def down(L, i, c, b):
                pe.wait_ge(*steps_of(L, "hT_v", i, c))
                pe.wait_ge(*steps_of(L, "y_a", i, c - 1))
                pe.wait_ge(*steps_of(L, "y_v", i, c - 1))
                pe.wait_ge(*loads_of(L, L["land"][b][2], L["land_base"][b][2], i, c))
                w = wslot[b][2].rearrange("p (k n) -> p k n", k=KF)
                for h in range(2):
                    for k in range(KF):
                        ins = mm(PB[:, 6 + h, :], hidT[:, b, 128 * k:128 * k + 128], w[:, k, 512 * h:512 * h + 512],
                                 k == 0, k == KF - 1)
                ins.then_inc(L["S"]["dn"], 1)

            def experts(l):
                for b in range(8):
                    if reader[b] is not None:
                        pe.wait_ge(*when(*reader[b]))
                    reader[b] = None
                L = base_loop[l]
                rows_T(L, None, 0, 0)
                gate_up(L, None, 0, 0)
                rows_T(L, None, 1, 1)
                hidden_T(L, None, 0, 0, 1)
                gate_up(L, None, 1, 1)
                with pe.Fori(0, half - 1) as i:
                    for n in (1, 2):
                        rows_T(L, i, n + 1, (n + 1) % 2)
                        down(L, i, n - 1, (n - 1) % 2)
                        hidden_T(L, i, n, n % 2, 1)
                        gate_up(L, i, n + 1, (n + 1) % 2)
                down(L, None, NE - 2, 0)
                hidden_T(L, None, NE - 1, 1, 0)
                down(L, None, NE - 1, 1)
                n_extra = nc.tensor.value_load(xtab[0:1, 7:8], min_val=0, max_val=NX)
                with pe.If(n_extra > 0):
                    X = extra_loop[l]
                    for step in ("hT_v", "y_a", "y_v"):
                        pe.wait_ge(*steps_of(L, step, None, NE - 1))
                    with pe.Fori(0, NX) as i:
                        rows_T(X, i, 0, 0)
                        gate_up(X, i, 0, 0)
                        hidden_T(X, i, 0, 0, 0)
                        down(X, i, 0, 0)
                pe.wait_ge(*when("y_all", l))

            def odd_keys_queries():
                for t in range(TILES):
                    pe.wait_ge(*when("ocn", t))
                    claim(0, "cqT", t)
                    for k in range(2):
                        tp(PB[:, 0, 128 * k:128 * k + 128], O[:, t, OCQ + 128 * k:OCQ + 128 * k + 128])
                    ins = tp(PB[:, 0, 256:384], O[:, t, OCKV:OCKV + 128])
                    ins.then_inc(*tick("pe", "cT", t))
                pe.wait_ge(sem("ld_odd"), 17 * 16)
                claim(1, "cqT", 3)
                tp(PB[:, 1, 0:128], cckv).then_inc(*tick("pe", "cT", 3))
                heads_up(0)
                heads_up(1)
                for n in range(len(head_items)):
                    heads_T(n)
                    if n + 2 < len(head_items):
                        heads_up(n + 2)
                    if n < TILES:
                        pe.wait_ge(*when("dqk", n))
                        pairs_T("dqT", n, lambda h: O[:, n, OQD + 128 * h:OQD + 128 * h + 128])
                        pairs_T("dkT", [0, 2, 3][n], lambda h: O[:, n, OKD + 128 * h:OKD + 128 * h + 128])
                    elif n == TILES:
                        pairs_T("dkT", 1, lambda h: cdk[:, 2 * h:2 * h + 2, :].rearrange("p m n -> p (m n)"))

            def heads_up(n):
                kind, j = head_items[n]
                pe.wait_ge(*when("cqT", j if kind == "q" else [0, 3, 1, 2][j]))
                for b in range(2):
                    claim(2 + b, "raw", n)
                    if kind == "q":
                        for k in range(2):
                            ins = mm(PB[:, 2 + b, 0:384], cqT[:, k, j * P:(j + 1) * P], qup[:, k, 384 * b:384 * b + 384],
                                     k == 0, k == 1)
                    else:
                        ins = mm(PB[:, 2 + b, :], ckT[:, j, :], kvup[:, 512 * b:512 * b + 512])
                ins.then_inc(*tick("pe", "up", n))

            def heads_T(n):
                pe.wait_ge(*when("heads", n))
                for b in range(2):
                    claim(4 + b, "headsT", n, b)
                    for h in range(4):
                        ins = tp(PB[0:96, 4 + b, 128 * h:128 * h + 128],
                                 hds[n % 2][:, 96 * (4 * b + h):96 * (4 * b + h) + 96])
                    ins.then_inc(*tick("pe", "heads_p", n, b))

            def pairs_T(out, t, src):
                b = 6 if out == "dqT" else 7
                claim(b, out, t)
                for h in range(4):
                    ins = tp(PB[:, b, 128 * h:128 * h + 128], src(h))
                ins.then_inc(*tick("pe", out + "_p", t))

            def attend():
                units = [(t, m) for t in range(TILES) for m in range(16)]

                def operands(u):
                    t, m = units[u]
                    ks = [0] if t == 0 else [1, 2, 3]
                    if m < 8:
                        q, kk = hTv[0:96, m, t * P:(t + 1) * P], kT[0:96, m, 128 * ks[0]:128 * ks[0] + 128 * len(ks)]
                        vs = [vC[:, k, m, :] for k in ks]
                    else:
                        h, r = (m - 8) // 2, 64 * (m % 2)
                        q = dqT[r:r + 64, h, t * P:(t + 1) * P]
                        kk = dkT[r:r + 64, h, 128 * ks[0]:128 * ks[0] + 128 * len(ks)]
                        vt = [O[:, 0, OVD:ODD], cdv.rearrange("p h n -> p (h n)"), O[:, 1, OVD:ODD], O[:, 2, OVD:ODD]]
                        vs = [vt[k][:, 128 * h:128 * h + 128] for k in ks]
                    return q, kk, vs, len(ks)

                def scores(u):
                    q, kk, vs, n = operands(u)
                    claim(u % 2, "prob", u)
                    mm(PB[:, u % 2, 0:128 * n], q, kk).then_inc(*tick("pe", "sc", u))

                def turn(u):
                    n = operands(u)[3]
                    pe.wait_ge(*when("prob", u))
                    claim(2 + u % 2, "probT", u)
                    for k in range(n):
                        ins = tp(PB[:, 2 + u % 2, 128 * k:128 * k + 128], prob[:, u % 2, 128 * k:128 * k + 128])
                    ins.then_inc(*tick("pe", "pT", u))

                def values(u):
                    vs = operands(u)[2]
                    pe.wait_ge(*when("probT", u))
                    claim(4 + u % 2, "ov", u)
                    w = 64 if units[u][1] < 8 else 128
                    for k, v in enumerate(vs):
                        ins = mm(PB[:, 4 + u % 2, 0:w], probT[:, u % 2, k, :], v, k == 0, k == len(vs) - 1)
                    ins.then_inc(*tick("pe", "pv", u))

                for s in ("act", "dve"):
                    pe.wait_ge(*when("end", s, "odd_prep"))
                scores(0)
                for u in range(48):
                    if u + 1 < 48:
                        scores(u + 1)
                    turn(u)
                    if u % 16:
                        values(u - 1)
                    if u % 16 == 15:
                        values(u)
                        t = u // 16
                        mixed_T(("omix1", t), lambda k: mix[:, 128 * k:128 * k + 128], t, 1)

            pe.wait_ge(*when("scT"))
            for n in range(EARLY_MODS):
                for k in range(KD):
                    mod_rows(0, n, k, n % 2)
                if n == 0:
                    pe.wait_ge(sem("ld_const"), 16)
                if n:
                    mod_columns(0, n - 1, 2 + (n - 1) % 2, (n - 1) % 2)
            mod_columns(0, EARLY_MODS - 1, 2 + (EARLY_MODS - 1) % 2, (EARLY_MODS - 1) % 2)
            norm(0, 0)
            for g, tiles in enumerate(((0,), (1, 2))):
                for t in tiles:
                    for b in range(2):
                        pe.wait_ge(*when("hT", 0, 0, t, b))
                project(("ein", g), tiles, 7, EVEN)
                if g == 0:
                    pe.wait_ge(sem("ld_even"), 16 * 5)
                    pe.wait_ge(*when("SG0"))
                    pe.wait_ge(*when("SR0"))
                else:
                    pe.wait_ge(sem("ld_sg"), 8 * 16)
                    pe.wait_ge(*when("SG1"))
                    states_T("state_in", lambda d, j: stg[:, d, 128 * j:128 * j + 128], "ld_sr")
                    pe.wait_ge(*when("state_in", 1))
                for i in range(len(tiles)):
                    lora_T(g, i)
                for w, combo in enumerate(COMBOS[g]):
                    gla(g, w, combo)
                    for i, d in combo:
                        rwkv(g, i, d)
                end("pe", f"units{g}")
                if g == 0:
                    states_T("state_out", lambda d, j: SR[:, d, j, :], ("S", 0, 0, 1, 1, 1, 1))
                for i, t in enumerate(tiles):
                    even_out(g, i, t)
                end("pe", f"out_g{g}")
            for l in range(2):
                if l == 1:
                    norm(1, 0)
                    for t in range(TILES):
                        for b in range(2):
                            pe.wait_ge(*when("hT", 1, 0, t, b))
                    project(("oin",), (0, 1, 2), 4, ODD)
                    odd_keys_queries()
                    end("pe", "odd_prep")
                    attend()
                for t in range(TILES):
                    for b in range(2):
                        pe.wait_ge(*when("mT", l, t, b))
                project(("outp", l), (0, 1, 2), 2, D, lambda n: spread_gates(l, n))
                end("pe", f"mixer{l}")
                norm(l, 1)
                router(l)
                experts(l)
                end("pe", f"moe{l}")

        @block.scalar
        def _(act):
            def step(ins, *name):
                ins.then_inc(*tick("act", *name))
                act.wait_ge(sem("act"), count["act"])

            def fn(out, in_, f, *name, **k):
                step(nc.scalar.activation(out, in_, f, **k), *name)

            def root(*name):
                act.wait_ge(*when("var", *name))
                n = known_n[name[0]]
                fn(small[:, 0:n], small[:, 0:n], ACT.Sqrt, "root", *name)

            def copies(name, tiles, chunks, width, dst):
                bank = 0
                for n in range(chunks):
                    ncol = min(512, width - 512 * n)
                    for i in range(len(tiles)):
                        if bank % 2 == 0:
                            act.wait_ge(*when(*name, "p", n, i))
                            fn(dst[:, i, 512 * n:512 * n + ncol], PB[:, bank % 4, 0:ncol], ACT.Copy, *name, "evac", n, i)
                        bank += 1

            def norm(l, s):
                act.wait_ge(*when("norm_in", l, s))
                for t in range(TILES):
                    fn(xn[:, 0, :], xv[:, t, :], ACT.Square, "sq", l, s, t, accum_out=small[:, t:t + 1])
                root("norm", l, s)
                for t in range(TILES):
                    act.wait_ge(*when("xnT", l, s, t, 1))
                    cond = 0 if t == 0 else 1
                    for k in range(4, 8):
                        fn(hTv[:, k, t * P:(t + 1) * P], PB[:, 7, 128 * (k - 4):128 * (k - 4) + 128], ACT.Identity,
                           *(("hT", l, s, t, 1) if k == 7 else ()), scale=mulAv[:, l, s, k, cond:cond + 1],
                           bias=modTv[:, l, 24 * s + k, cond:cond + 1])

            def weights_T(u):
                n = 128 if u < 16 else 384
                act.wait_ge(*when("pT", u))
                if u > 1:
                    act.wait_ge(*when("pv", u - 2))
                fn(probT[:, u % 2, :, :].rearrange("p k n -> p (k n)")[:, 0:n], PB[:, 2 + u % 2, 0:n], ACT.Copy, "probT", u)

            def heads_raw(n):
                kind, j = head_items[n]
                act.wait_ge(*when("up", n))
                if n > 1:
                    act.wait_ge(*when("heads_p", n - 2, 1))
                buf = hds[n % 2]
                if kind == "q":
                    for b in range(2):
                        fn(buf[:, 384 * b:384 * b + 384], PB[:, 2 + b, 0:384], ACT.Copy, *(("raw", n) if b else ()))
                else:
                    v = buf.rearrange("p (h n) -> p h n", h=8)
                    for b in range(2):
                        src = PB[:, 2 + b, :].rearrange("p (h n) -> p h n", h=4)
                        fn(v[:, 4 * b:4 * b + 4, 0:64], src[:, :, 0:64], ACT.Copy)
                        fn(vC[:, j, 4 * b:4 * b + 4, :], src[:, :, 64:128], ACT.Copy, *(("raw", n) if b else ()))
                    kr = ckr if j == 1 else O[:, [0, None, 1, 2][j], OKR:OKR + 32]
                    fn(v[:, :, 64:96], bc(kr, 1, 8), ACT.Copy)
                fn(hqs[n % 2], buf, ACT.Square, "hsq", n)

            def mod_row(l, n, bank, b):
                act.wait_ge(*when("modr", l, n))
                fn(mrow[:, b, :], PB[0:2, bank, :], ACT.Copy, "mrow", l, n)

            def gla(g, w):
                u = (g, w)
                la, t1 = tmpE[0], tmpE[1]
                act.wait_ge(*when("ga_z", *u))
                fn(t1, la, ACT.Abs)
                fn(t1, t1, ACT.Exp, scale=-1.0)
                fn(t1, t1, ACT.Ln, "ln", *u, bias=1.0)
                act.wait_ge(*when("gcum", *u))
                s = 1.0 / 16
                fn(tmpE[1], PB[:, 1, :], ACT.Exp, scale=s)
                fn(tmpE[2], PB[:, 1, :], ACT.Exp, scale=-s)
                fn(LJ4.rearrange("p h n -> p (h n)"), PB[:, 2, :], ACT.Exp, "g_exp", *u, scale=s)
                act.wait_ge(*when("gsum", *u))
                fn(small[:, 16:24], PB[:, 3, 0:8], ACT.Exp, "g_dec", *u, scale=s)
                act.wait_ge(*when("gT", *u, 0))
                fn(TA.rearrange("p a n -> p (a n)"), PB[:, 4, :], ACT.Copy, "gqkT", *u, 0)

            def rwkv(g, i, d):
                u = (g, i, d)
                act.wait_ge(*when("r_zw", *u))
                fn(tmpE[0], tmpE[0], ACT.Sigmoid, "lw", *u)
                act.wait_ge(*when("r_za", *u))
                fn(tmpE[1], tmpE[1], ACT.Sigmoid, "aa", *u)
                act.wait_ge(*when("sum_exc", *u))
                fn(tokm[:, 0, :], PB[:, 5, :], ACT.Exp, "e_exc", *u, scale=-RW)
                act.wait_ge(*when("sum_inc", *u))
                fn(tmpE[2], PB[:, 4, :], ACT.Exp, "e_dec", *u, scale=RW)
                fn(tokm[:, 1, :], PB[:, 4, :], ACT.Exp, "e_inc", *u, scale=-RW)
                act.wait_ge(*when("rcum", *u))
                fn(small[:, 32:40], PB[:, 6, 0:8], ACT.Exp, "e_wc", *u, scale=-RW)
                for hf in range(2):
                    w = (g, i, d, hf)
                    act.wait_ge(*when("tT", *w, 0))
                    if hf:
                        act.wait_ge(*when("yy", g, i, d, 0, 1))
                    fn(TA.rearrange("p a n -> p (a n)"), PB[:, 0, :], ACT.Copy, "TT", *w, 0)
                    mods = beside(*w)
                    for v in range(1, 6):
                        for p in range(2):
                            act.wait_ge(*when("t1", *w, p, v))
                            fn(T14[:, 2 * p:2 * p + 2, :].rearrange("p h n -> p (h n)"), PB[:, 6 + p, 0:256], ACT.Copy,
                               "T1", *w, p, v)
                        if v == 5:
                            mod_row(*mods[0], 5, 0)
                    for n in range(2):
                        r = CH * ((n, 1 - n)[d])
                        for p in range(2):
                            act.wait_ge(*when("uu", *w, p, n))
                            if n:
                                act.wait_ge(*when("yy", *w, 0))
                            fn(UU[r:r + CH, 128 * p:128 * p + 128], PB[r:r + CH, p, 0:128], ACT.Copy, "U", *w, p, n)
                    if len(mods) > 1:
                        mod_row(*mods[1], 5, 1)

            known_n = {"norm": TILES, "kk": 8, "og": 4, "oy": 8, "dd": 4}

            def even_out(g, i):
                root("og", g, i)
                root("oy", g, i)

            def rows_copy(L, i, c, b):
                act.wait_ge(*steps_of(L, "xT_p", i, c))
                act.wait_ge(*steps_of(L, "gu", i, c - L["k"]))
                nc.scalar.activation(xT[:, b, 0:512], PB[:, 0, :], ACT.Copy).then_inc(L["S"]["xT_a"], 1)

            def silu(L, i, c, b):
                act.wait_ge(*steps_of(L, "gu", i, c))
                act.wait_ge(*steps_of(L, "hid", i, c - L["k"]))
                nc.scalar.activation(sil[:, b, :], PB[:, 2 + b, :], ACT.Silu).then_inc(L["S"]["silu"], 1)

            def store(L, i, c, b, row):
                act.wait_ge(*steps_of(L, "dn", i, c))
                act.wait_ge(*loads_of(L, L["stores"][0][b], L["stores"][1], i, c - L["k"]))
                nc.scalar.activation(yb[:, b, 0:512], PB[:, 6, :], ACT.Copy).then_inc(L["S"]["y_a"], 1)
                act.wait_ge(*steps_of(L, "y_a", i, c))
                act.wait_ge(*steps_of(L, "y_v", i, c))
                act.dma_start(Yd[row, :], yb[:, b, :]).then_inc(L["stores"][0][b], 16)

            def experts(l):
                L = base_loop[l]
                rows_copy(L, None, 0, 0)
                silu(L, None, 0, 0)
                rows_copy(L, None, 1, 1)
                silu(L, None, 1, 1)
                with act.Fori(0, half - 1) as i:
                    for n in (1, 2):
                        rows_copy(L, i, n + 1, (n + 1) % 2)
                        store(L, i, n - 1, (n - 1) % 2, bass.ds(i * 2 * P + (n - 1) * P, P))
                        silu(L, i, n + 1, (n + 1) % 2)
                for n in (NE - 2, NE - 1):
                    store(L, None, n, n % 2, slice(n * P, (n + 1) * P))
                n_extra = nc.scalar.value_load(xtab[0:1, 7:8], min_val=0, max_val=NX)
                with act.If(n_extra > 0):
                    X = extra_loop[l]
                    for b in range(2):
                        act.wait_ge(*loads_of(L, y_st[b], L["stores"][1], None, NE - 2 + b))
                    with act.Fori(0, NX) as i:
                        rows_copy(X, i, 0, 0)
                        silu(X, i, 0, 0)
                        store(X, i, 0, 0, bass.ds(i * P + NE * P, P))
                    act.wait_ge(*loads_of(X, X["stores"][0][0], X["stores"][1], None, NX - 1))
                for b in range(2):
                    act.wait_ge(*loads_of(L, y_st[b], L["stores"][1], None, NE - 2 + b))
                fn(small[:, 254:255], small[:, 75:76], ACT.Copy, "y_all", l)
                for t in range(TILES):
                    act.wait_ge(sem(f"combined{t}"), 32 * (l + 1))
                    fn(yg[:, t, :], yg[:, t, :], ACT.Copy, "chosen0", l, t, scale=gatek[:, t:t + 1])

            act.wait_ge(sem("ld_cols"), 16)
            fn(scT[:, :], cols[:, COL_C:COL_C + 16], ACT.Silu, "scT")
            for n in range(EARLY_MODS):
                mod_row(0, n, n % 2, n % 2)
            norm(0, 0)
            for g, tiles in enumerate(((0,), (1, 2))):
                if g:
                    meet(act, "act", "out_g0")
                copies(("ein", g), tiles, 7, EVEN, E)
                if g == 0:
                    act.wait_ge(*when("zeros"))
                    act.dma_start(Xd.rearrange("(b p) d -> p b d", p=P), bc(zeros, 1, NE + NX)).then_inc(sem("xd_zero"), 16)
                    act.dma_start(Yd[NE * P:ROWS, :].rearrange("(b p) d -> p b d", p=P), bc(zeros, 1, NX)).then_inc(sem("xd_zero"), 16)
                act.wait_ge(*when("e_ready", g))
                for i in range(len(tiles)):
                    fn(E[:, i, EWL:EWL + 128], E[:, i, EWL:EWL + 128], ACT.Tanh)
                for i in range(len(tiles)):
                    fn(E[:, i, EGL:EGL + 128], E[:, i, EGL:EGL + 128], ACT.Sigmoid, "lora", g, i)
                for i in range(len(tiles)):
                    root("kk", g, i)
                for w, combo in enumerate(COMBOS[g]):
                    gla(g, w)
                    for i, d in combo:
                        rwkv(g, i, d)
                end("act", f"units{g}")
                for i in range(len(tiles)):
                    fn(E[:, i, EG:EG + 512], E[:, i, EG:EG + 512], ACT.Silu, "siluG", g, i)
                for i in range(len(tiles)):
                    even_out(g, i)
                end("act", f"out_g{g}")
            for l in range(2):
                if l == 1:
                    norm(1, 0)
                    copies(("oin",), (0, 1, 2), 4, ODD, O)
                    act.wait_ge(*when("oin", "evac", 3, 2))
                    for t in range(TILES):
                        fn(sqd[:, 3072:3328], O[:, t, OCQ:OCQ + 256], ACT.Square, accum_out=small[:, t:t + 1])
                        fn(sqd[:, 3072:3200], O[:, t, OCKV:OCKV + 128], ACT.Square,
                           *(("csq",) if t == 2 else ()), accum_out=small[:, 3 + t:4 + t])
                    act.wait_ge(*when("var", "c"))
                    fn(small[:, 0:6], small[:, 0:6], ACT.Sqrt, "root", "c")
                    for t in range(TILES):
                        fn(sqd[:, 1024 * t:1024 * t + 1024], O[:, t, OQD:OVD], ACT.Square, "dsq", t)
                    act.wait_ge(*when("var", "d"))
                    fn(small[:, 80:128], small[:, 80:128], ACT.Sqrt, "root", "d")
                    act.wait_ge(*when("lamsum"))
                    fn(small[:, 60:62], small[:, 60:62], ACT.Exp, "lamexp")
                    heads_raw(0)
                    heads_raw(1)
                    for n in range(len(head_items)):
                        act.wait_ge(*when("var", "h", n))
                        v = small[:, 16 + 8 * (n % 2):24 + 8 * (n % 2)]
                        fn(v, v, ACT.Sqrt, "root", "h", n)
                        if n + 2 < len(head_items):
                            heads_raw(n + 2)
                    end("act", "odd_prep")
                    for u in range(48):
                        m = u % 16
                        n = 128 if u < 16 else 384
                        act.wait_ge(*when("nmax", u))
                        if u >= 2:
                            act.wait_ge(*when("pT", u - 2))
                        if u >= 4:
                            act.wait_ge(*when("ov", u - 4))
                        scale = (96 if m < 8 else 64) ** -0.5
                        fn(prob[:, u % 2, 0:n], PB[:, u % 2, 0:n], ACT.Exp, "prob", u,
                           bias=small[:, 64 + u % 2:65 + u % 2], scale=scale, accum_out=small[:, 240 + u % 4:241 + u % 4])
                        if m:
                            weights_T(u - 1)
                        if m == 15:
                            weights_T(u)
                        if m == 15:
                            root("dd", u // 16)
                end("act", f"mixer{l}")
                norm(l, 1)
                act.wait_ge(*when("rt", l))
                fn(small[:, 128:176], PB[:, 0, 0:48], ACT.Sigmoid, "scores", l)
                for t in range(TILES):
                    for b in range(2):
                        act.wait_ge(*when("htok_p", l, t, b))
                        fn(htok[:, t, 512 * b:512 * b + 512], PB[:, 2 + (2 * t + b) % 4, :], ACT.Copy,
                           "htok_c", l, t, b)
                    seen[("htok", l, t)] = ("act", count["act"])
                act.wait_ge(*when("rows", l))
                experts(l)
                end("act", f"moe{l}")

        @block.vector
        def _(dve):
            V = nc.vector

            def step(ins, *name):
                ins.then_inc(*tick("dve", *name))
                dve.wait_ge(sem("dve"), count["dve"])

            def tt(out, a, b, op, *name):
                step(V.tensor_tensor(out, a, b, op), *name)

            def ts(out, a, s1, s2, op0, op1, *name):
                step(V.tensor_scalar(out, a, s1, s2, op0, op1) if op1 is not None else
                     V.tensor_scalar(out, a, s1, None, op0), *name)

            def stt(out, a, s, b, op0, op1, *name):
                step(V.scalar_tensor_tensor(out=out, in0=a, scalar=s, in1=b, op0=op0, op1=op1), *name)

            def cp(out, a, *name):
                step(V.tensor_copy(out, a), *name)

            def red(out, a, *name, op=ALU.add):
                step(V.tensor_reduce(out, a, AX.X, op), *name)

            def rstd(n, scale, eps, *name):
                ts(small[:, 0:n], small[:, 0:n], scale, eps, ALU.mult, ALU.add, "var", *name)
                dve.wait_ge(*when("root", *name))
                step(V.reciprocal(small[:, 0:n], small[:, 0:n]))
                return small[:, 0:n]

            def mod_chunk(l, n, bank):
                dve.wait_ge(*when("modp", l, n))
                tt(modTv[:, l, 4 * n:4 * n + 4, :], PB[:, bank, 0:8].rearrange("p (j c) -> p j c", c=2),
                   bc(cols[:, COL_BM + 48 * l + 4 * n:COL_BM + 48 * l + 4 * n + 4], 2, 2), ALU.add, "modT", l, n)
                for s in range(2):
                    if n == 6 * s + 3:
                        ng = bc(cols[:, COL_NG + 8 * (2 * l + s):COL_NG + 8 * (2 * l + s) + 8], 2, 2)
                        stt(mulAv[:, l, s, :, :], modTv[:, l, 24 * s + 8:24 * s + 16, :], 1.0, ng, ALU.add, ALU.mult,
                            "mulA", l, s)

            def diagonals(l, s):
                for n in range(4):
                    if s:
                        dve.wait_ge(*when("spread", l, 0, n))
                    col = modTv[:, l, 24 * s + 16 + 4 * (n % 2):24 * s + 20 + 4 * (n % 2), n // 2]
                    tt(tokm[:, n, :].rearrange("p (j n) -> p j n", j=4), bc(ident, 1, 4), bc(col, 2, P), ALU.mult,
                       "diag", l, s, n)

            def gate_rows(l, s):
                if l == 0 and s == 0:
                    dve.wait_ge(sem("xd_zero"), 32)
                for n in range(4):
                    dve.wait_ge(*when("spread", l, s, n))
                    cp(gatev[:, n // 2, s, 512 * (n % 2):512 * (n % 2) + 512], PB[:, 4 + n % 2, :], "gate", l, s, n)

            def norm(l, s):
                cp(small[:, 72:73], small[:, 70:71], "norm_in", l, s)
                dve.wait_ge(*when("sq", l, s, TILES - 1))
                r = rstd(TILES, 1.0 / D, EPS, "norm", l, s)
                for t in range(TILES):
                    if t == 2:
                        dve.wait_ge(*when("xnT", l, s, 0, 1))
                    ts(xn[:, t % 2, :], xv[:, t, :], r[:, t:t + 1], None, ALU.mult, None, "xn", l, s, t)
                for t in range(TILES):
                    cond = 0 if t == 0 else 1
                    dve.wait_ge(*when("xnT", l, s, t, 0))
                    for k in range(4):
                        ts(hTv[:, k, t * P:(t + 1) * P], PB[:, 6, 128 * k:128 * k + 128],
                           mulAv[:, l, s, k, cond:cond + 1], modTv[:, l, 24 * s + k, cond:cond + 1],
                           ALU.mult, ALU.add, *(("hT", l, s, t, 0) if k == 3 else ()))

            def copies(name, tiles, chunks, width, dst):
                bank = 0
                for n in range(chunks):
                    ncol = min(512, width - 512 * n)
                    for i in range(len(tiles)):
                        if bank % 2:
                            dve.wait_ge(*when(*name, "p", n, i))
                            cp(dst[:, i, 512 * n:512 * n + ncol], PB[:, bank % 4, 0:ncol], *name, "evac", n, i)
                        bank += 1

            def h8(ap, h=8):
                return ap.rearrange("p (h n) -> p h n", h=h)

            def prepare(g, i):
                tmp = tmpE[0]
                dve.wait_ge(*when("lora_T", g, i))
                for j, n in ((0, 128), (1, 128), (2, 128), (3, 32)):
                    cp(loT[0:n, i, j, :], PB[0:n, 0, 128 * j:128 * j + 128], *(("loT", g, i) if j == 3 else ()))
                kk = kkn[:, i, :]
                kb, rr = E[:, i, EKB:EKB + 512], E[:, i, ER:ER + 512]
                tt(kk, kb, R(rowsE, "rw_kk"), ALU.mult)
                tt(tmp, kk, kk, ALU.mult)
                red(small[:, 0:8], h8(tmp))
                r = rstd(8, 1.0, EPS, "kk", g, i)
                tt(h8(kk), h8(kk), bc(r, 2, 64), ALU.mult)
                tt(tmp, rr, kb, ALU.mult)
                tt(tmp, tmp, R(rowsE, "rw_rk"), ALU.mult)
                red(bon[:, i, :], h8(tmp))

            def gla(g, w, combo, done):
                u = (g, w)
                la, t1 = tmpE[0], tmpE[1]
                dve.wait_ge(*when("za", *u))
                tt(la, PB[:, 0, :], R(rowsE, "gla_a_b"), ALU.add, "ga_z", *u)
                dve.wait_ge(*when("ln", *u))
                stt(la, la, 0.0, t1, ALU.min, ALU.subtract, "la", *u)
                dve.wait_ge(*when("g_exp", *u))
                for i, d in combo:
                    q, k, f = E[:, i, EQ:EQ + 256], E[:, i, EK_:EK_ + 256], slice(256 * d, 256 * d + 256)
                    stt(tokm[:, 0, f], q, 64 ** -0.5, tmpE[1][:, f], ALU.mult, ALU.mult)
                    tt(tokm[:, 1, f], k, tmpE[2][:, f], ALU.mult)
                    tt(tokm[:, 2, f], k, LJ4.rearrange("p h n -> p (h n)")[:, f], ALU.mult, *(("gk", *u) if d else ()))
                dve.wait_ge(*when("gT", *u, 1))
                cp(TB.rearrange("p a n -> p (a n)"), PB[:, 5, :], "gqkT", *u, 1)
                dve.wait_ge(*when("g_dec", *u))
                dve.wait_ge(*when("gA", *u))
                for d in range(2):
                    m = C("le") if d == 0 else C("ge")
                    for b in range(2):
                        tt(G4[:, b:4:2, 128 * d:128 * d + 128],
                           PB[:, 6 + b, 256 * d:256 * d + 256].rearrange("p (j n) -> p j n", j=2), bc(m, 1, 2),
                           ALU.mult, *(("gatt", *u) if b and d else ()))
                for n in range(2):
                    for i, d in combo:
                        c = n if d == 0 else 1 - n
                        dve.wait_ge(*when("gu", *u, d, n))
                        tt(tmpE[1].rearrange("p (j n) -> p j n", j=2), PB[:, 2 + d, :].rearrange("p (j n) -> p j n", j=2),
                           bc(C("bdg"), 1, 2), ALU.mult)
                        for j in range(2):
                            q = 16 + 4 * d + 2 * j + c
                            stt(SG[:, d, j, :], SG[:, d, j, :], small[:, q:q + 1],
                                tmpE[1][:, 256 * j:256 * j + 256], ALU.mult, ALU.add, *(("gS", *u, d, n) if j else ()))
                for i, d in combo:
                    if i not in done:
                        cp(oG[:, i, :], PB[:, d, :], "gout", *u, d)
                        done.add(i)
                    else:
                        tt(oG[:, i, :], oG[:, i, :], PB[:, d, :], ALU.add, "gout", *u, d)

            def rwkv(g, i, d, first):
                u = (g, i, d)
                kb, rr = E[:, i, EKB:EKB + 512], E[:, i, ER:ER + 512]
                dve.wait_ge(*when("zw", *u))
                tt(tmpE[0], PB[:, d, :], R(rowsE, "rw_w0", 512 * d, 512), ALU.add, "r_zw", *u)
                dve.wait_ge(*when("zr", *u))
                tt(tmpE[1], PB[:, 2 + d, :], R(rowsE, "rw_a0", 512 * d, 512), ALU.add, "r_za", *u)
                dve.wait_ge(*when("aa", *u))
                tt(tokm[:, 2, :], tmpE[1], kkn[:, i, :], ALU.mult)
                stt(tokm[:, 3, :], tmpE[1], -1.0, R(rowsE, "rw_ka"), ALU.add, ALU.mult)
                stt(tokm[:, 3, :], tokm[:, 3, :], 1.0, kb, ALU.add, ALU.mult)
                dve.wait_ge(*when("e_exc", *u))
                tt(tokm[:, 0, :], tokm[:, 0, :], kkn[:, i, :], ALU.mult)
                dve.wait_ge(*when("e_dec", *u))
                tt(tokm[:, 2, :], tokm[:, 2, :], tmpE[2], ALU.mult)
                tt(tokm[:, 3, :], tokm[:, 3, :], tmpE[2], ALU.mult)
                dve.wait_ge(*when("e_inc", *u))
                tt(tokm[:, 1, :], tokm[:, 1, :], rr, ALU.mult, "tokm", *u)
                lvl, lvl_t = (C("lvl0"), C("lvl1")) if d == 0 else (C("lvl1"), C("lvl0"))
                strict = cst[:, _C["lt" if d == 0 else "gt"][0]:_C["lt" if d == 0 else "gt"][0] + 256]
                for hf in range(2):
                    w = (g, i, d, hf)
                    dve.wait_ge(*when("tT", *w, 1))
                    cp(TB.rearrange("p a n -> p (a n)"), PB[:, 1, :], "TT", *w, 1)
                    for p in range(2):
                        h = slice(2 * p, 2 * p + 2)
                        dve.wait_ge(*when("gram", *w, p))
                        tt(G4[:, h, :].rearrange("p h (a n) -> p (h a) n", a=2),
                           PB[:, 2 + 2 * p:4 + 2 * p, :].rearrange("p h (a n) -> p (h a) n", a=2),
                           bc(strict, 1, 4), ALU.mult, "G", *w, p)
                        dve.wait_ge(*when("gramL", *w, p))
                        b0 = 6 if p == 0 else 0
                        tt(X4[:, h, :], PB[:, b0:b0 + 2, 0:128], bc(lvl_t[:, 0:128], 1, 2), ALU.mult, "L0", *w, p)
                        tt(X4[:, h, :], bc(ident, 1, 2), X4[:, h, :], ALU.subtract, "X", *w, p, 0)
                    mods = beside(*w)
                    for v in range(1, 6):
                        for p in range(2):
                            h = slice(2 * p, 2 * p + 2)
                            if v < 5:
                                dve.wait_ge(*when("dx", *w, p, v))
                                tt(X4[:, h, :], X4[:, h, :], PB[:, 6 + p, 256:512].rearrange("p (h n) -> p h n", h=2),
                                   ALU.subtract, "X", *w, p, v)
                            dve.wait_ge(*when("dxt", *w, p, v))
                            tt(XT4[:, h, :], XT4[:, h, :], PB[:, p, 0:256].rearrange("p (h n) -> p h n", h=2),
                               ALU.subtract, "XT", *w, p, v)
                    mod_chunk(*mods[0], 4)
                    for n in range(2):
                        c = (n, 1 - n)[d]
                        r = CH * c
                        for p in range(2):
                            dve.wait_ge(*when("rh", *w, p, n))
                            ts(RH[r:r + CH, 128 * p:128 * p + 128], PB[r:r + CH, 2 + p, 0:128], -1.0, None, ALU.mult, None,
                               "RH", *w, p, n)
                        for p in range(2):
                            j = 2 * hf + p
                            dve.wait_ge(*when("su", *w, p, n))
                            tmp = SG_tmp[:, 128 * p:128 * p + 128]
                            tt(tmp, SR[:, d, j, :], PB[:, 6 + p, 0:128], ALU.add)
                            stt(SR[:, d, j, :], tmp, small[:, 32 + 2 * j + c:33 + 2 * j + c], C("bdr"), ALU.mult, ALU.mult,
                                "S", *w, p, n)
                        dve.wait_ge(*when("yy", *w, n))
                        yo = yR[r:r + CH, i, 256 * hf:256 * hf + 256]
                        if first:
                            cp(yo, PB[r:r + CH, 4, 0:256], "Y", *w, n)
                        else:
                            tt(yo, yo, PB[r:r + CH, 4, 0:256], ALU.add, "Y", *w, n)
                    if len(mods) > 1:
                        mod_chunk(*mods[1], 5)

            def even_out(g, i):
                dve.wait_ge(sem("ld_late"), 32 * (g + 1))
                o, y, tmp = oG[:, i, :], yR[:, i, :], tmpE[0]
                tt(tmp, o, o, ALU.mult)
                red(small[:, 0:4], h8(tmp, 4))
                r = rstd(4, 1.0 / 128, EPS, "og", g, i)
                tt(h8(o, 4), h8(o, 4), bc(r, 2, 128), ALU.mult)
                tt(h8(o, 4), h8(o, 4), bc(R(rowsG, "gla_o_g"), 1, 4), ALU.mult)
                dve.wait_ge(*when("siluG", g, i))
                tt(o, o, E[:, i, EG:EG + 512], ALU.mult)
                red(small[:, 8:16], h8(y))
                ts(small[:, 8:16], small[:, 8:16], 1.0 / 64, None, ALU.mult, None)
                tt(h8(y), h8(y), bc(small[:, 8:16], 2, 64), ALU.subtract)
                tt(tmp, y, y, ALU.mult)
                red(small[:, 0:8], h8(tmp))
                r = rstd(8, 1.0 / 64, GN_EPS, "oy", g, i)
                tt(h8(y), h8(y), bc(r, 2, 64), ALU.mult)
                tt(y, y, R(rowsG, "rw_gn_g"), ALU.mult)
                tt(y, y, R(rowsG, "rw_gn_b"), ALU.add)
                tt(h8(tmp), h8(E[:, i, EVB:EVB + 512]), bc(bon[:, i, :], 2, 64), ALU.mult)
                tt(y, y, tmp, ALU.add)
                dve.wait_ge(*when("gm", g, i))
                tt(y, y, PB[:, 5, :], ALU.mult, "omix", g, i)

            def mixed(l, t):
                for b in range(2):
                    dve.wait_ge(*when("mixT", l, t, b))
                    cp(hTv[:, 4 * b:4 * b + 4, t * P:(t + 1) * P], PB[:, 6 + b, :].rearrange("p (k n) -> p k n", k=4),
                       "mT", l, t, b)

            def residual(l):
                bank = 0
                diagonals(l, 0)
                gate_rows(l, 0)
                for n in range(2):
                    for t in range(TILES):
                        dve.wait_ge(*when("outp", l, "p", n, t))
                        gv = gatev[:, 0 if t == 0 else 1, 0, 512 * n:512 * n + 512]
                        tmp = gated
                        tt(tmp, PB[:, bank % 4, :], gv, ALU.mult, "outp", l, "evac", n, t)
                        xs = xv[:, t, 512 * n:512 * n + 512]
                        tt(xs, xs, tmp, ALU.add)
                        bank += 1
                    if n == 0:
                        diagonals(l, 1)
                gate_rows(l, 1)

            def route(l):
                at = [0]

                def w(n):
                    at[0] += n
                    return route_w[:, at[0] - n:at[0]]

                sel, c2, gsc, grank, big = w(48), w(192), w(12), w(48), w(768)
                rank, f0, f1, gw, row, ge = w(48), w(48), w(48), w(48), w(48), w(48)
                cum, xbk, off, ov, rec = w(16), w(16), w(16), w(16), w(4)
                c1 = big[:, 0:192]
                v4 = lambda a: a.rearrange("p (g e) -> p g e", e=4)
                v44 = lambda a: a.rearrange("p (g e j) -> p g e j", e=4, j=4)
                v16 = lambda a: a.rearrange("p (t e) -> p t e", e=16)
                s = small[:, 128:176]
                tie = bc(C("tie").rearrange("p (e j) -> p e j", e=4), 1, 12)
                dve.wait_ge(sem("ld_router"), 32)
                dve.wait_ge(*when("scores", l))
                tt(v16(sel), v16(s), bc(brout[:, :], 1, TILES), ALU.add)
                tt(v44(c1), bc(v4(sel), 2, 4), bc(v4(sel), 3, 4), ALU.is_gt)
                tt(v44(c2), bc(v4(sel), 2, 4), bc(v4(sel), 3, 4), ALU.is_equal)
                tt(v44(c2), v44(c2), tie, ALU.mult)
                tt(c1, c1, c2, ALU.add)
                red(rank, c1.rearrange("p (g j) -> p g j", j=4))
                ts(mask, rank, 1.5, None, ALU.is_lt, None)
                tt(sel, sel, mask, ALU.mult)
                red(gsc, v4(sel))
                tt(v44(c1[:, 0:48]), bc(v4(gsc), 2, 4), bc(v4(gsc), 3, 4), ALU.is_gt)
                tt(v44(c2[:, 0:48]), bc(v4(gsc), 2, 4), bc(v4(gsc), 3, 4), ALU.is_equal)
                tt(v44(c2[:, 0:48]), v44(c2[:, 0:48]), tie[:, 0:TILES], ALU.mult)
                tt(c1[:, 0:48], c1[:, 0:48], c2[:, 0:48], ALU.add)
                red(grank[:, 0:12], c1[:, 0:48].rearrange("p (g j) -> p g j", j=4))
                ts(grank[:, 0:12], grank[:, 0:12], 0.5, None, ALU.is_lt, None)
                tt(v4(mask), v4(mask), bc(grank[:, 0:12], 2, 4), ALU.mult, "mask", l)
                tt(gw, mask, s, ALU.mult)
                red(rec[:, 0:TILES], v16(gw))
                step(V.reciprocal(rec[:, 0:TILES], rec[:, 0:TILES]))
                tt(v16(gw), v16(gw), bc(rec[:, 0:TILES], 2, 16), ALU.mult)
                dve.wait_ge(sem("ld_cmoe"), 16 * (l + 1))
                tri = M("tri16").rearrange("p (e j) -> p e j", e=16)
                tt(big.rearrange("p (t e j) -> p t e j", t=TILES, e=16), bc(v16(mask), 2, 16), bc(tri, 1, TILES), ALU.mult)
                red(rank, big.rearrange("p (g j) -> p g j", j=16))
                ts(f0, rank, 0.5, None, ALU.is_lt, None)
                tt(f0, f0, mask, ALU.mult)
                tt(f1, mask, f0, ALU.subtract)
                dve.wait_ge(*when("places", l))
                cp(cum, PB[:, 1, 48:64])
                ts(xbk, cum, CAP + 0.5, None, ALU.is_ge, None)
                ts(ov, cum, 2 * CAP + 0.5, None, ALU.is_ge, None)
                tt(xbk, xbk, ov, ALU.add)
                tt(big[:, 0:256].rearrange("p (e j) -> p e j", e=16), bc(xbk, 1, 16), tri, ALU.mult)
                red(off, big[:, 0:256].rearrange("p (e j) -> p e j", e=16))
                tt(cum, off, xbk, ALU.add)
                ts(ov, off, float(CAP), float((NE - 1) * P), ALU.mult, ALU.add)
                tt(ov, ov, M("row0"), ALU.subtract)
                ts(ge, PB[:, 1, 0:48], CAP - 0.5, None, ALU.is_ge, None)
                tt(v16(row), PB[:, 1, 0:48].rearrange("p (t e) -> p t e", e=16), bc(M("row0"), 1, TILES), ALU.add,
                   "place", l)
                tt(v16(ge), v16(ge), bc(ov, 1, TILES), ALU.mult)
                tt(row, row, ge, ALU.add)
                for ch, f in enumerate((f0, f1)):
                    tt(c2[:, 0:48], f, gw, ALU.mult)
                    red(gatek[:, 3 * ch:3 * ch + 3], v16(c2[:, 0:48]))
                    tt(f, f, row, ALU.mult)
                    red(rec[:, 0:3], v16(f))
                    cp(rows_i[:, 3 * ch:3 * ch + 3], rec[:, 0:3])
                tt(big[:, 0:80].rearrange("p (b e) -> p b e", e=16), bc(cum, 1, NX),
                   M("extra").rearrange("p (b e) -> p b e", e=16), ALU.is_le)
                red(off[:, 0:NX], big[:, 0:80].rearrange("p (b e) -> p b e", e=16))
                ts(off[:, 0:NX], off[:, 0:NX], float(NE - 1), None, ALU.min, None)
                cp(off[:, 7:8], cum[:, 15:16])
                step(V.memset(off[:, NX:7], 0.0))
                cp(xtab[:, :], off[:, 0:8], "rows", l)

            def rows_copy(L, i, c, b):
                dve.wait_ge(*steps_of(L, "xT_p", i, c))
                dve.wait_ge(*steps_of(L, "gu", i, c - L["k"]))
                V.tensor_copy(xT[:, b, 512:1024], PB[:, 1, :]).then_inc(L["S"]["xT_v"], 1)

            def hidden(L, i, c, b):
                dve.wait_ge(*steps_of(L, "silu", i, c))
                dve.wait_ge(*steps_of(L, "hT_p", i, c - L["k"]))
                V.tensor_tensor(hid[:, b, :], sil[:, b, :], PB[:, 4 + b, :], ALU.mult).then_inc(L["S"]["hid"], 1)

            def hidden_copy(L, i, c, b):
                dve.wait_ge(*steps_of(L, "hT_p", i, c))
                dve.wait_ge(*steps_of(L, "dn", i, c - L["k"]))
                V.tensor_copy(hidT[:, b, :], PB[:, 0, :]).then_inc(L["S"]["hT_v"], 1)

            def out_copy(L, i, c, b):
                dve.wait_ge(*steps_of(L, "dn", i, c))
                dve.wait_ge(*loads_of(L, L["stores"][0][b], L["stores"][1], i, c - L["k"]))
                V.tensor_copy(yb[:, b, 512:1024], PB[:, 7, :]).then_inc(L["S"]["y_v"], 1)

            def experts(l):
                L = base_loop[l]
                rows_copy(L, None, 0, 0)
                hidden(L, None, 0, 0)
                rows_copy(L, None, 1, 1)
                hidden_copy(L, None, 0, 0)
                hidden(L, None, 1, 1)
                with dve.Fori(0, half - 1) as i:
                    for n in (1, 2):
                        rows_copy(L, i, n + 1, (n + 1) % 2)
                        out_copy(L, i, n - 1, (n - 1) % 2)
                        hidden_copy(L, i, n, n % 2)
                        hidden(L, i, n + 1, (n + 1) % 2)
                out_copy(L, None, NE - 2, 0)
                hidden_copy(L, None, NE - 1, 1)
                out_copy(L, None, NE - 1, 1)
                n_extra = nc.vector.value_load(xtab[0:1, 7:8], min_val=0, max_val=NX)
                with dve.If(n_extra > 0):
                    X = extra_loop[l]
                    for b in range(2):
                        dve.wait_ge(*loads_of(L, y_st[b], L["stores"][1], None, NE - 2 + b))
                    with dve.Fori(0, NX) as i:
                        rows_copy(X, i, 0, 0)
                        hidden(X, i, 0, 0)
                        hidden_copy(X, i, 0, 0)
                        out_copy(X, i, 0, 0)
                for t in range(TILES):
                    dve.wait_ge(*when("chosen0", l, t))
                    dve.wait_ge(sem(f"combined{t}"), 32 * (l + 1))
                    y0, y1 = yg[:, t, :], yg[:, 3 + t, :]
                    stt(y0, y1, gatek[:, 3 + t:4 + t], y0, ALU.mult, ALU.add)
                    tt(y0, y0, gatev[:, 0 if t == 0 else 1, 1, :], ALU.mult)
                    tt(xv[:, t, :], xv[:, t, :], y0, ALU.add, "x_moe", l, t)

            def rope(v, t, kind, nh, tmp):
                w = 32 if kind == "c" else 64
                q = w // 4
                cos = bc(C("cos" + kind, w * (t - 1), w), 1, nh)
                sin = C("sin" + kind, w * (t - 1), w).rearrange("p (a b q) -> p a b q", a=2, b=2)
                split = lambda ap, b: ap.rearrange("p h (a b q) -> p h a b q", a=2, b=2)[:, :, :, b, :]
                for b in range(2):
                    tt(split(tmp, b), split(v, 1 - b), bc(sin[:, :, b, :], 1, nh), ALU.mult)
                tt(v, v, cos, ALU.mult)
                tt(v, v, tmp, ALU.add)

            def head_norm(v, tmp, nh, width, gain, *name):
                tt(tmp, v, v, ALU.mult)
                red(small[:, 0:nh], tmp)
                r = rstd(nh, 1.0 / width, EPS, *name)
                tt(v, v, bc(r, 2, width), ALU.mult)
                tt(v, v, bc(gain, 1, nh), ALU.mult)

            def heads_sum(n):
                v = small[:, 16 + 8 * (n % 2):24 + 8 * (n % 2)]
                dve.wait_ge(*when("hsq", n))
                red(v, h8(hqs[n % 2]))
                ts(v, v, 1.0 / 96, EPS, ALU.mult, ALU.add, "var", "h", n)

            def heads_norm(n):
                kind, j = head_items[n]
                t = j if kind == "q" else [0, 0, 1, 2][j]
                hv, r = h8(hds[n % 2]), small[:, 16 + 8 * (n % 2):24 + 8 * (n % 2)]
                dve.wait_ge(*when("root", "h", n))
                step(V.reciprocal(r, r))
                tt(hv, hv, bc(r, 2, 96), ALU.mult)
                tt(hv, hv, bc(R(rowsO, "mla_qn_g" if kind == "q" else "mla_kn_g"), 1, 8), ALU.mult)
                if t:
                    rope(hv[:, :, 64:96], t, "c", 8, h8(hqs[n % 2])[:, :, 0:32])
                seen[("heads", n)] = ("dve", count["dve"])

            def heads_out(n):
                kind, j = head_items[n]
                dst = hTv if kind == "q" else kT
                for b in range(2):
                    dve.wait_ge(*when("heads_p", n, b))
                    cp(dst[0:96, 4 * b:4 * b + 4, 128 * j:128 * j + 128],
                       PB[0:96, 4 + b, :].rearrange("p (k n) -> p k n", k=4), "headsT", n, b)

            def pair_norm(t):
                v = h8(O[:, t, OQD:OVD], 16)
                tt(v, v, bc(small[:, 80 + 16 * t:96 + 16 * t], 2, 64), ALU.mult)
                tt(v[:, 0:8, :], v[:, 0:8, :], bc(R(rowsO, "diff_qn_g"), 1, 8), ALU.mult)
                tt(v[:, 8:16, :], v[:, 8:16, :], bc(R(rowsO, "diff_kn_g"), 1, 8), ALU.mult)
                if t:
                    rope(v, t, "d", 16, h8(sqd[:, 1024 * t:1024 * t + 1024], 16))
                else:
                    seen[("caches",)] = ("dve", count["dve"])
                seen[("dqk", t)] = ("dve", count["dve"])

            def pair_out(out, t):
                dve.wait_ge(*when(out + "_p", t))
                dst, b = (dqT, 6) if out == "dqT" else (dkT, 7)
                cp(dst[:, :, 128 * t:128 * t + 128], PB[:, b, :].rearrange("p (k n) -> p k n", k=4), out, t)

            def odd_prepare():
                dve.wait_ge(sem("ld_odd"), 17 * 16)
                dve.wait_ge(*when("csq"))
                ts(small[:, 0:3], small[:, 0:3], 1.0 / 256, EPS, ALU.mult, ALU.add)
                ts(small[:, 3:6], small[:, 3:6], 1.0 / 128, EPS, ALU.mult, ALU.add, "var", "c")
                lam = R(rowsO, "diff_lam").rearrange("p (a b n) -> p a b n", a=2, b=2)
                lt_ = hd[:, 0:128].rearrange("p (a n) -> p a n", a=2)
                tt(lt_, lam[:, :, 0, :], lam[:, :, 1, :], ALU.mult)
                red(small[:, 60:62], lt_, "lamsum")
                dve.wait_ge(*when("root", "c"))
                step(V.reciprocal(small[:, 0:6], small[:, 0:6]))
                for t in range(TILES):
                    for c0, w, gn, a in ((OCQ, 256, "mla_qa_g", 0), (OCKV, 128, "mla_kva_g", 3)):
                        v = O[:, t, c0:c0 + w]
                        stt(v, v, small[:, a + t:a + t + 1], R(rowsO, gn), ALU.mult, ALU.mult, *(("ocn", t) if a else ()))
                for t in range(TILES):
                    dve.wait_ge(*when("dsq", t))
                    red(small[:, 80 + 16 * t:96 + 16 * t], h8(sqd[:, 1024 * t:1024 * t + 1024], 16))
                ts(small[:, 80:128], small[:, 80:128], 1.0 / 64, EPS, ALU.mult, ALU.add, "var", "d")
                for t in range(4):
                    dve.wait_ge(*when("cT", t))
                    if t < 3:
                        cp(cqT[:, :, t * P:(t + 1) * P], PB[:, 0, 0:256].rearrange("p (k n) -> p k n", k=2))
                        cp(ckT[:, [0, 2, 3][t], :], PB[:, 0, 256:384], "cqT", t)
                    else:
                        cp(ckT[:, 1, :], PB[:, 1, 0:128], "cqT", 3)
                dve.wait_ge(*when("root", "d"))
                step(V.reciprocal(small[:, 80:128], small[:, 80:128]))
                heads_sum(0)
                heads_sum(1)
                for n in range(len(head_items)):
                    heads_norm(n)
                    if n < TILES:
                        pair_norm(n)
                    if 0 < n <= TILES:
                        pair_out("dqT", n - 1)
                        pair_out("dkT", [0, 2, 3][n - 1])
                    elif n == TILES + 1:
                        pair_out("dkT", 1)
                    heads_out(n)
                    if n + 2 < len(head_items):
                        heads_sum(n + 2)
                dve.wait_ge(*when("lamexp"))
                tt(small[:, 62:63], small[:, 61:62], small[:, 60:61], ALU.subtract)
                ts(small[:, 62:63], small[:, 62:63], -LAM_INIT, None, ALU.add, None)
                end("dve", "odd_prep")

            def attend():
                def top(u):
                    n = 128 if u < 16 else 384
                    dve.wait_ge(*when("sc", u))
                    if u >= 2:
                        dve.wait_ge(*when("prob", u - 2))
                    m = small[:, 64 + u % 2:65 + u % 2]
                    red(m, PB[:, u % 2, 0:n], op=ALU.max)
                    ts(m, m, -((96 if u % 16 < 8 else 64) ** -0.5), None, ALU.mult, None, "nmax", u)

                def out(u):
                    t, m = u // 16, u % 16
                    dve.wait_ge(*when("pv", u))
                    rec = small[:, 68:69]
                    step(V.reciprocal(rec, small[:, 240 + u % 4:241 + u % 4]))
                    if m < 8:
                        ts(mix[:, 64 * m:64 * m + 64], PB[:, 4 + u % 2, 0:64], rec, None, ALU.mult, None, "ov", u)
                        return
                    o = mix[:, 512 + 128 * ((m - 8) // 2):640 + 128 * ((m - 8) // 2)]
                    if m % 2 == 0:
                        ts(o, PB[:, 4 + u % 2, 0:128], rec, None, ALU.mult, None, "ov", u)
                    else:
                        tt(rec, rec, small[:, 62:63], ALU.mult)
                        stt(o, PB[:, 4 + u % 2, 0:128], rec, o, ALU.mult, ALU.add, "ov", u)

                top(0)
                for u in range(48):
                    if u + 1 < 48:
                        top(u + 1)
                    if u % 16:
                        out(u - 1)
                    if u % 16 == 15:
                        out(u)
                        t = u // 16
                        od = h8(mix[:, 512:1024], 4)
                        head_norm(od, h8(hd[:, 0:512], 4), 4, 128, R(rowsO, "diff_subln_g"), "dd", t)
                        ts(od, od, 1.0 - LAM_INIT, None, ALU.mult, None, "omix1", t)
                        mixed(1, t)

            dve.wait_ge(sem("ld_cols"), 16)
            dve.wait_ge(sem("ld_const"), 16)
            dve.wait_ge(sem("ld_x"), 16 * TILES)
            step(V.memset(zeros, 0.0), "zeros")
            step(V.memset(small[:, 70:80], 0.0))
            ahead = [(S[name], EARLY) for S in [blk] + [X["S"] for X in extra_loop] for name in S]
            ahead += [(n, 16) for n in y_st + [X["stores"][0][0] for X in extra_loop]]
            for n, (which, value) in enumerate(ahead):
                V.memset(small[:, 80 + n:81 + n], 0.0).then_inc(which, value)
            for n in range(EARLY_MODS):
                mod_chunk(0, n, 2 + n % 2)
            norm(0, 0)
            for g, tiles in enumerate(((0,), (1, 2))):
                copies(("ein", g), tiles, 7, EVEN, E)
                if g == 0:
                    dve.wait_ge(sem("ld_even"), 16 * 5)
                    dve.wait_ge(*when("SG0"))
                    dve.wait_ge(*when("SR0"))
                    step(V.memset(RH, 0.0))
                    step(V.memset(UU, 0.0))
                else:
                    dve.wait_ge(sem("ld_sg"), 8 * 16)
                    for d in range(2):
                        dve.wait_ge(*when("state_in_p", d))
                        cp(SR[:, d, :, :], PB[:, d, :].rearrange("p (j n) -> p j n", j=4), "state_in", d)
                cp(small[:, 72:73], small[:, 70:71], "e_ready", g)
                for i in range(len(tiles)):
                    bank = 0
                    for n in range(7):
                        for ii in range(len(tiles)):
                            if bank % 2 == 0 and n == 6:
                                dve.wait_ge(*when("ein", g, "evac", n, ii))
                            bank += 1
                    dve.wait_ge(*when("lora", g, i))
                    prepare(g, i)
                done, done_y = set(), set()
                for w, combo in enumerate(COMBOS[g]):
                    gla(g, w, combo, done)
                    for i, d in combo:
                        rwkv(g, i, d, i not in done_y)
                        done_y.add(i)
                end("dve", f"units{g}")
                if g == 0:
                    for d in range(2):
                        dve.wait_ge(*when("state_out_p", d))
                        cp(stg[:, d, :], PB[:, d, :], "state_out", d)
                    cp(small[:, 72:73], small[:, 70:71], "state_out_T")
                for i, t in enumerate(tiles):
                    even_out(g, i)
                    mixed(0, t)
                end("dve", f"out_g{g}")
            for l in range(2):
                if l == 1:
                    norm(1, 0)
                    copies(("oin",), (0, 1, 2), 4, ODD, O)
                    dve.wait_ge(*when("oin", "evac", 3, 1))
                    odd_prepare()
                    attend()
                residual(l)
                end("dve", f"mixer{l}")
                norm(l, 1)
                if l == 1:
                    dve.wait_ge(*when("caches_stored"))
                route(l)
                experts(l)
                end("dve", f"moe{l}")
    return seen


def constants():
    import numpy as np
    a, b = np.arange(P)[:, None], np.arange(P)[None, :]
    same = (a // CH) == (b // CH)
    c = np.zeros((P, NCONST), np.float32)

    def put(name, v):
        s, w = _C[name]
        c[:, s:s + w] = v

    put("ident", a == b)
    put("lt", same & (a < b))
    put("le", same & (a <= b))
    put("gt", same & (a > b))
    put("ge", same & (a >= b))
    put("half", np.arange(P)[:, None] // CH == np.arange(2)[None, :])
    lv = np.concatenate([(a >> (v + 1) == b >> (v + 1)) & ((a >> v) % 2 == 0) & ((b >> v) % 2 == 1) for v in range(6)], 1)
    lv_t = np.concatenate([(a >> (v + 1) == b >> (v + 1)) & ((a >> v) % 2 == 1) & ((b >> v) % 2 == 0) for v in range(6)], 1)
    put("lvl0", lv)
    put("lvl1", lv_t)
    put("ones", 1.0)
    put("bdg", (a // 64) == (np.arange(256)[None, :] // 128))
    put("bdr", (a // 64) == (b // 64))
    put("tie", np.tile((np.arange(4)[None, :] < np.arange(4)[:, None]).reshape(1, 16), (P, 1)))
    put("one", 1.0)
    m = np.zeros((P, NMOE), np.float32)
    for name, v in (("earlier", a < b), ("ones", 1.0), ("row0", np.arange(NE) * P), ("extra", np.arange(80) // 16),
                    ("tri16", (np.arange(16)[None, :] < np.arange(16)[:, None]).reshape(1, 256))):
        s, w = _M[name]
        m[:, s:s + w] = v
    for kind, dim in (("c", 32), ("d", 64)):
        half = dim // 2
        inv = (1.0 / (np.float32(10000.0) ** (np.arange(0, half, 2, dtype=np.float32) / np.float32(half)))).astype(np.float32)
        tok = np.arange(256)
        ang_r = (tok // 64).astype(np.float32)[:, None] * inv
        ang_c = (tok % 64).astype(np.float32)[:, None] * inv
        ang = np.concatenate([ang_r, ang_r, ang_c, ang_c], -1).astype(np.float32)
        q = dim // 4
        sign = np.concatenate([-np.ones(q), np.ones(q), -np.ones(q), np.ones(q)])
        put("cos" + kind, np.cos(ang).reshape(2, P, dim).transpose(1, 0, 2).reshape(P, 2 * dim))
        put("sin" + kind, (np.sin(ang) * sign).reshape(2, P, dim).transpose(1, 0, 2).reshape(P, 2 * dim))
    return c, m


def layout(i):
    import numpy as np

    def blocks(w):
        n = -(-w.shape[1] // 512) * 512
        w = np.concatenate([w, np.zeros((w.shape[0], n - w.shape[1]), w.dtype)], 1) if n != w.shape[1] else w
        return w.reshape(KD, P, n // 512, 512).transpose(2, 1, 0, 3).reshape(n // 512, P, CHUNK)

    def column(v):
        return v.reshape(-1, P).T

    a = {}
    a["consts"], a["consts_moe"] = constants()
    a["x"] = np.concatenate([i["x_prompt"].reshape(1, P, D), i["x_sample"].reshape(2, P, D)], 0)
    cc = np.stack([column(i["c_ctx"]), column(i["c"][0])], 2).reshape(P, 16)
    a["cols"] = np.concatenate([cc, column(i["norm_g"].reshape(-1)), column(i["b_mod"].reshape(-1))], 1)
    a["w_mod"] = np.stack([blocks(i["w_mod"][l]) for l in range(2)])
    a["w_mix"] = np.concatenate([blocks(i[n][0]) for n in ("ev_w_in", "ev_w_out", "od_w_in", "od_w_out")])
    for l in range(2):
        for m, n in enumerate(("moe_w_gate", "moe_w_up")):
            a[f"w_moe{l}{m}"] = i[n][l].reshape(NE, KD, P, FF).transpose(0, 2, 1, 3).reshape(NE, P, CHUNK)
        a[f"w_moe{l}2"] = i["moe_w_down"][l].reshape(NE, KF, P, D).transpose(0, 2, 1, 3).reshape(NE, P, CHUNK)
    a["rows_even"] = np.concatenate([i[n].reshape(-1) for n in (
        "gla_a_b", "rw_w0", "rw_a0", "rw_kk", "rw_ka", "rw_rk")])
    a["rows_gain"] = np.concatenate([i[n].reshape(-1) for n in ("rw_gn_g", "rw_gn_b", "gla_o_g")])
    a["rows_odd"] = np.concatenate([i[n].reshape(-1) for n in (
        "mla_qa_g", "mla_kva_g", "mla_qn_g", "mla_kn_g", "diff_qn_g", "diff_kn_g", "diff_lam", "diff_subln_g")])
    a["b_router"] = i["moe_b_router"]
    a["w_router"] = i["moe_w_router"].reshape(KD, P, NE).transpose(1, 0, 2).reshape(P, KD * NE)
    a["gla_a_up"] = i["gla_a_up"][0]
    a["rw_w2"] = i["rw_w2"].reshape(P, 512)
    a["rw_a2"] = i["rw_a2"].reshape(P, 512)
    a["rw_g2"] = i["rw_g2"][0]
    a["state_gla"] = i["state_gla"][0, 0]
    a["state_rwkv"] = i["state_rwkv"][0, 0]
    a["mla_q_up"] = i["mla_q_up"][0]
    a["mla_kv_up"] = i["mla_kv_up"][0]
    for n in ("cache_mla_ckv", "cache_mla_krope", "cache_diff_k", "cache_diff_v"):
        a[n] = i[n][0, 0]
    return {n: np.ascontiguousarray(v) for n, v in a.items()}


_OUTS = {"y": (TILES, P, D), "new_state_gla": (2, 4, 64, 128), "new_state_rwkv": (2, 8, 64, 64), "new_ckv": (P, 128),
         "new_krope": (P, 32), "new_dk": (4, 2, P, 64), "new_dv": (4, P, 128)}


def program(nc, shapes, known):
    io = {n: nc.dram_tensor(f"in_{n}", s, F32, kind="ExternalInput").ap() for n, s in shapes.items()}
    for n, s in _OUTS.items():
        io[n] = nc.dram_tensor(f"out_{n}", s, F32, kind="ExternalOutput").ap()
    io["w_moe"] = [[io[f"w_moe{l}{m}"] for m in range(3)] for l in range(2)]
    return build(nc, io, known)


def kernel(**inputs):
    import numpy as _np
    import concourse.bacc as _bacc
    from concourse.bass_utils import run_bass_kernel_spmd as _run

    arrays = layout({n: _np.asarray(v) for n, v in inputs.items()})
    shapes = {n: v.shape for n, v in arrays.items()}
    stages = program(_bacc.Bacc("TRN2", target_bir_lowering=False, num_devices=1), shapes, None)
    nc = _bacc.Bacc("TRN2", target_bir_lowering=False, num_devices=1)
    program(nc, shapes, stages)
    r = _run(nc, [{f"in_{n}": v for n, v in arrays.items()}], core_ids=[0]).results[0]
    y = r["out_y"]
    return (y[0:1], y[1:3].reshape(1, 2 * P, D), r["out_new_state_gla"][None, None], r["out_new_state_rwkv"][None, None],
            r["out_new_ckv"][None, None], r["out_new_krope"][None, None], r["out_new_dk"][None, None],
            r["out_new_dv"][None, None])
```
